# Optimizing a Trainium2 kernel written in Bass

```python
import math
import jax, jax.numpy as jnp
from jax import lax
import numpy as np

D_MODEL = 1024
BATCH = 1
SEQ = 1024
DEPTH = 1

N_HEADS = 8
HEAD_DIM = 64
ATT_WIDTH = N_HEADS * HEAD_DIM
PATTERNS = ((128, 1), (512, 4), (2048, 16))
SSM_GROUPS = 16
SSM_GROUP_CH = 16
SSM_WIDTH = SSM_GROUPS * SSM_GROUP_CH
SSM_STATE = 64
D_FF = 2048
CONV_W = 3
IN_WIDTH = 3 * ATT_WIDTH + SSM_WIDTH + 2 * D_MODEL
EPS = 1e-6
NEG_INF = -1e30


def _rmsnorm(x, g):
    x32 = x.astype(jnp.float32)
    y = x32 * lax.rsqrt(jnp.mean(x32 * x32, axis=-1, keepdims=True) + EPS)
    return y.astype(x.dtype) * g

def _modulate(x, g, shift, scale):
    return _rmsnorm(x, g) * (1 + scale[:, None, :]) + shift[:, None, :]

def _alibi_slopes():
    return np.array([2.0 ** (-8.0 * (h + 1) / N_HEADS) for h in range(N_HEADS)], dtype=np.float32)

def _dilated_window_attention(q, k, v, slopes, window, dilation):
    b, s, h, hd = q.shape
    w = window // dilation
    L = s // dilation
    nb = -(-L // w)
    Lp = nb * w
    X = b * dilation

    def to_sub(t):
        t = t.reshape(b, L, dilation, h, hd).transpose(0, 2, 3, 1, 4)
        return t.reshape(X, h, L, hd)

    qs, ks, vs = to_sub(q), to_sub(k), to_sub(v)
    qb = jnp.pad(qs, ((0, 0), (0, 0), (0, Lp - L), (0, 0))).reshape(X, h, nb, w, hd)
    kp = jnp.pad(ks, ((0, 0), (0, 0), (w, Lp - L), (0, 0)))
    vp = jnp.pad(vs, ((0, 0), (0, 0), (w, Lp - L), (0, 0)))
    kb = jnp.concatenate([kp[:, :, :Lp].reshape(X, h, nb, w, hd),
                          kp[:, :, w:].reshape(X, h, nb, w, hd)], axis=3)
    vb = jnp.concatenate([vp[:, :, :Lp].reshape(X, h, nb, w, hd),
                          vp[:, :, w:].reshape(X, h, nb, w, hd)], axis=3)

    a_idx = np.arange(w)[:, None]
    j_idx = np.arange(2 * w)[None, :]
    dist = (w + a_idx - j_idx).astype(np.float32)
    kpos = np.arange(nb)[:, None, None] * w - w + j_idx[None]
    valid = (dist[None] >= 0) & (dist[None] <= w) & (kpos >= 0)
    bias = -(slopes[:, None, None] * dilation) * dist[None]

    scale = HEAD_DIM ** -0.5
    sc = jnp.einsum('xhnqd,xhnkd->xhnqk', qb, kb).astype(jnp.float32) * scale
    sc = jnp.where(valid, sc + bias[:, None], NEG_INF)
    m = jnp.max(sc, axis=-1, keepdims=True)
    p = jnp.exp(sc - m)
    den = jnp.sum(p, axis=-1, keepdims=True)
    o = jnp.einsum('xhnqk,xhnkd->xhnqd', p, vb.astype(jnp.float32)) / den
    lse = (m + jnp.log(den))[..., 0]

    o = o.reshape(X, h, Lp, hd)[:, :, :L].reshape(b, dilation, h, L, hd)
    o = o.transpose(0, 3, 1, 2, 4).reshape(b, s, h, hd)
    lse = lse.reshape(X, h, Lp)[:, :, :L].reshape(b, dilation, h, L)
    lse = lse.transpose(0, 3, 1, 2).reshape(b, s, h)
    return o, lse

def _s5_branch(u, a_re, a_im, log_dt, b_re, b_im, c_re, c_im, d_skip, w_glu, b_glu):
    f32 = jnp.float32
    bsz, s, _ = u.shape
    lr, li = a_re.astype(f32), a_im.astype(f32)
    dt = jnp.exp(log_dt.astype(f32))[:, None]
    mag = jnp.exp(lr * dt)
    ang = li * dt
    ab_re, ab_im = mag * jnp.cos(ang), mag * jnp.sin(ang)
    nr, ni = ab_re - 1.0, ab_im
    den = lr * lr + li * li
    f_re = (nr * lr + ni * li) / den
    f_im = (ni * lr - nr * li) / den
    br, bi = b_re.astype(f32), b_im.astype(f32)
    bb_re = f_re[..., None] * br - f_im[..., None] * bi
    bb_im = f_re[..., None] * bi + f_im[..., None] * br

    ug = u.astype(f32).reshape(bsz, s, SSM_GROUPS, SSM_GROUP_CH)
    bu_re = jnp.einsum('bsgc,gnc->bsgn', ug, bb_re)
    bu_im = jnp.einsum('bsgc,gnc->bsgn', ug, bb_im)
    a_re_t = jnp.broadcast_to(ab_re, bu_re.shape)
    a_im_t = jnp.broadcast_to(ab_im, bu_re.shape)

    def combine(left, right):
        ar1, ai1, xr1, xi1 = left
        ar2, ai2, xr2, xi2 = right
        return (ar2 * ar1 - ai2 * ai1,
                ar2 * ai1 + ai2 * ar1,
                ar2 * xr1 - ai2 * xi1 + xr2,
                ar2 * xi1 + ai2 * xr1 + xi2)

    _, _, xr, xi = lax.associative_scan(combine, (a_re_t, a_im_t, bu_re, bu_im), axis=1)
    y = (jnp.einsum('bsgn,gcn->bsgc', xr, c_re.astype(f32))
         - jnp.einsum('bsgn,gcn->bsgc', xi, c_im.astype(f32))
         + d_skip.astype(f32).reshape(SSM_GROUPS, SSM_GROUP_CH) * ug)
    y = y.reshape(bsz, s, SSM_WIDTH).astype(u.dtype)
    y = jax.nn.gelu(y)
    return y * jax.nn.sigmoid(y @ w_glu + b_glu)

def _hybrid_mixer(u, w_in, b_gate, a_re, a_im, log_dt, b_re, b_im, c_re, c_im,
                  d_skip, w_glu, b_glu, w_proj_att, w_proj_ssm, w_out):
    bsz, s, _ = u.shape
    proj = u @ w_in
    q, k, v, us, g_att, g_ssm = jnp.split(
        proj, [ATT_WIDTH, 2 * ATT_WIDTH, 3 * ATT_WIDTH, 3 * ATT_WIDTH + SSM_WIDTH,
               3 * ATT_WIDTH + SSM_WIDTH + D_MODEL], axis=-1)
    q = q.reshape(bsz, s, N_HEADS, HEAD_DIM)
    k = k.reshape(bsz, s, N_HEADS, HEAD_DIM)
    v = v.reshape(bsz, s, N_HEADS, HEAD_DIM)

    slopes = _alibi_slopes()
    outs, lses = [], []
    for window, dilation in PATTERNS:
        o, lse = _dilated_window_attention(q, k, v, slopes, window, dilation)
        outs.append(o)
        lses.append(lse)
    wts = jax.nn.softmax(jnp.stack(lses, axis=0), axis=0)
    o_att = jnp.sum(wts[..., None] * jnp.stack(outs, axis=0), axis=0)
    o_att = o_att.reshape(bsz, s, ATT_WIDTH).astype(u.dtype)
    y_att = o_att @ w_proj_att

    y_ssm = _s5_branch(us, a_re, a_im, log_dt, b_re, b_im, c_re, c_im,
                       d_skip, w_glu, b_glu) @ w_proj_ssm

    gb_att, gb_ssm = jnp.split(b_gate, 2, axis=-1)
    merged = jax.nn.sigmoid(g_att + gb_att) * y_att + jax.nn.sigmoid(g_ssm + gb_ssm) * y_ssm
    return merged @ w_out

def _conv_ffn(u, w_up, w_conv, b_conv, w_down):
    s = u.shape[1]
    a, val = jnp.split(u @ w_up, 2, axis=-1)
    ap = jnp.pad(a, ((0, 0), (CONV_W - 1, 0), (0, 0)))
    conv = b_conv
    for j in range(CONV_W):
        conv = conv + w_conv[j] * ap[:, CONV_W - 1 - j:CONV_W - 1 - j + s]
    return (jax.nn.silu(conv) * val) @ w_down

def first_inputs(seed: int = 0) -> dict:
    key = jax.random.key(seed)
    ks = jax.random.split(key, 32)
    f32 = jnp.float32
    L, D, G, N, C = DEPTH, D_MODEL, SSM_GROUPS, SSM_STATE, SSM_GROUP_CH
    nrm = lambda k, shape, sc: jax.random.normal(k, shape, f32) * sc
    inp = {}
    inp["x"] = nrm(ks[0], (BATCH, SEQ, D), 1.0)
    inp["c"] = nrm(ks[1], (BATCH, D), 1.0)
    inp["w_ada"] = nrm(ks[2], (L, D, 6 * D), 0.5 * D ** -0.5)
    inp["b_ada"] = nrm(ks[3], (L, 6 * D), 0.02)
    inp["g_mix"] = 1.0 + nrm(ks[4], (L, D), 0.02)
    inp["w_in"] = nrm(ks[5], (L, D, IN_WIDTH), D ** -0.5)
    inp["b_gate"] = nrm(ks[6], (L, 2 * D), 0.02)
    inp["a_re"] = -0.5 + nrm(ks[7], (L, G, N), 0.01)
    inp["a_im"] = jnp.pi * jnp.arange(N, dtype=f32)[None, None, :] + nrm(ks[8], (L, G, N), 0.01)
    inp["log_dt"] = jax.random.uniform(ks[9], (L, G), f32, math.log(1e-3), math.log(1e-1))
    inp["b_re"] = nrm(ks[10], (L, G, N, C), (2 * C) ** -0.5)
    inp["b_im"] = nrm(ks[11], (L, G, N, C), (2 * C) ** -0.5)
    inp["c_re"] = nrm(ks[12], (L, G, C, N), (2 * N) ** -0.5)
    inp["c_im"] = nrm(ks[13], (L, G, C, N), (2 * N) ** -0.5)
    inp["d_skip"] = nrm(ks[14], (L, SSM_WIDTH), 1.0)
    inp["w_glu"] = nrm(ks[15], (L, SSM_WIDTH, SSM_WIDTH), SSM_WIDTH ** -0.5)
    inp["b_glu"] = nrm(ks[16], (L, SSM_WIDTH), 0.02)
    inp["w_proj_att"] = nrm(ks[17], (L, ATT_WIDTH, D), ATT_WIDTH ** -0.5)
    inp["w_proj_ssm"] = nrm(ks[18], (L, SSM_WIDTH, D), SSM_WIDTH ** -0.5)
    inp["w_out"] = nrm(ks[19], (L, D, D), D ** -0.5)
    inp["g_ffn"] = 1.0 + nrm(ks[20], (L, D), 0.02)
    inp["w_up"] = nrm(ks[21], (L, D, 2 * D_FF), D ** -0.5)
    inp["w_conv"] = nrm(ks[22], (L, CONV_W, D_FF), CONV_W ** -0.5)
    inp["b_conv"] = nrm(ks[23], (L, D_FF), 0.02)
    inp["w_down"] = nrm(ks[24], (L, D_FF, D), D_FF ** -0.5)
    inp["g_final"] = 1.0 + nrm(ks[25], (D,), 0.02)
    return inp

def first_block(x, c, w_ada, b_ada, g_mix, w_in, b_gate, a_re, a_im, log_dt, b_re, b_im,
              c_re, c_im, d_skip, w_glu, b_glu, w_proj_att, w_proj_ssm, w_out,
              g_ffn, w_up, w_conv, b_conv, w_down, g_final):
    h = x
    c_act = jax.nn.silu(c)
    for l in range(DEPTH):
        mod = c_act @ w_ada[l] + b_ada[l]
        sh1, sc1, gt1, sh2, sc2, gt2 = jnp.split(mod, 6, axis=-1)
        u = _modulate(h, g_mix[l], sh1, sc1)
        h = h + gt1[:, None, :] * _hybrid_mixer(
            u, w_in[l], b_gate[l], a_re[l], a_im[l], log_dt[l], b_re[l], b_im[l],
            c_re[l], c_im[l], d_skip[l], w_glu[l], b_glu[l],
            w_proj_att[l], w_proj_ssm[l], w_out[l])
        u = _modulate(h, g_ffn[l], sh2, sc2)
        h = h + gt2[:, None, :] * _conv_ffn(u, w_up[l], w_conv[l], b_conv[l], w_down[l])
    return _rmsnorm(h, g_final)


CHUNK = 128
A_GROUPS = 8
A_WIDTH = 512
A_HEAD = A_WIDTH // A_GROUPS
B_WIDTH = 512
CONV_WIDTH = 3
C_WIDTH = 512
POOL_WINDOWS = (2, 4, 8, 16)
C_GROUP = C_WIDTH // len(POOL_WINDOWS)
IN_TOTAL = 3 * A_WIDTH + 4 * B_WIDTH + 2 * C_WIDTH + 3 * D_MODEL
RMS_EPS = 1e-6
LN_EPS = 1e-5


def _rmsnorm_2(x, g):
    xf = x.astype(jnp.float32)
    y = xf * lax.rsqrt(jnp.mean(xf * xf, axis=-1, keepdims=True) + RMS_EPS)
    return (y * g.astype(jnp.float32)).astype(x.dtype)

def _layernorm(x, g, b):
    xf = x.astype(jnp.float32)
    mu = jnp.mean(xf, axis=-1, keepdims=True)
    xc = xf - mu
    var = jnp.mean(xc * xc, axis=-1, keepdims=True)
    y = xc * lax.rsqrt(var + LN_EPS)
    return (y * g.astype(jnp.float32) + b.astype(jnp.float32)).astype(x.dtype)

def _split_points():
    widths = [A_WIDTH] * 3 + [B_WIDTH] * 4 + [C_WIDTH] * 2 + [D_MODEL] * 3
    return [int(s) for s in np.cumsum(widths)[:-1]]

def _gmlp_branch(u, v, ln_g, ln_b, w_s, b_s):
    u = jax.nn.gelu(u)
    v = _layernorm(jax.nn.gelu(v), ln_g, ln_b)
    bsz, s, _ = v.shape
    vc = v.reshape(bsz, s // CHUNK, CHUNK, A_GROUPS, A_HEAD)
    causal = jnp.tril(jnp.ones((CHUNK, CHUNK), dtype=bool))
    w_m = jnp.where(causal, w_s, 0.0)
    sg = jnp.einsum('gts,bnsgc->bntgc', w_m, vc) + b_s.T[:, :, None]
    return u * sg.reshape(bsz, s, A_WIDTH)

def _shortconv_branch(xb, bg, cg, conv_w, conv_b):
    y = cg * xb
    y = lax.conv_general_dilated(
        y, conv_w[:, None, :].astype(y.dtype), window_strides=(1,),
        padding=[(CONV_WIDTH - 1, 0)], dimension_numbers=('NWC', 'WIO', 'NWC'),
        feature_group_count=B_WIDTH) + conv_b
    return bg * y

def _pool_branch(xc, w_pool, pool_scale):
    bsz, s, _ = xc.shape
    xf = xc.astype(jnp.float32).reshape(bsz, s, len(POOL_WINDOWS), C_GROUP)
    cs = jnp.cumsum(xf, axis=1)
    t_count = jnp.arange(1, s + 1, dtype=jnp.float32)
    pooled = []
    for gi, w in enumerate(POOL_WINDOWS):
        c = cs[:, :, gi]
        lag = jnp.pad(c[:, :s - w], ((0, 0), (w, 0), (0, 0)))
        cnt = jnp.minimum(t_count, float(w))[None, :, None]
        pooled.append((c - lag) / cnt)
    pooled = (jnp.stack(pooled, axis=2) - xf).astype(xc.dtype)
    y = jnp.einsum('bsgc,gcd->bsgd', pooled, w_pool).reshape(bsz, s, C_WIDTH)
    return y * pool_scale

def _hybrid_layer(x, norm_g, w_in, ln_g, ln_b, w_s, b_s, conv_w, conv_b,
                  w_pool, pool_scale, w_pa, w_pb, w_pc, w_o):
    h = _rmsnorm_2(x, norm_g)
    p = h @ w_in
    (u, v, z_a, x_b, b_g, c_g, z_b, x_c, z_c,
     g_a, g_b, g_c) = jnp.split(p, _split_points(), axis=-1)
    y_a = (_gmlp_branch(u, v, ln_g, ln_b, w_s, b_s) * jax.nn.silu(z_a)) @ w_pa
    y_b = (_shortconv_branch(x_b, b_g, c_g, conv_w, conv_b) * jax.nn.silu(z_b)) @ w_pb
    y_c = (_pool_branch(x_c, w_pool, pool_scale) * jax.nn.silu(z_c)) @ w_pc
    merged = (jax.nn.sigmoid(g_a) * y_a + jax.nn.sigmoid(g_b) * y_b
              + jax.nn.sigmoid(g_c) * y_c)
    return x + merged @ w_o

def second_inputs(seed: int = 0) -> dict:
    key = jax.random.key(seed)
    ks = jax.random.split(key, 20)
    f32 = jnp.float32
    n = lambda k, shape: jax.random.normal(k, shape, dtype=f32)
    return {
        "x": n(ks[0], (BATCH, SEQ, D_MODEL)),
        "norm_g": 1.0 + 0.02 * n(ks[1], (DEPTH, D_MODEL)),
        "w_in": n(ks[2], (DEPTH, D_MODEL, IN_TOTAL)) * D_MODEL ** -0.5,
        "ln_g": 1.0 + 0.02 * n(ks[3], (DEPTH, A_WIDTH)),
        "ln_b": 0.02 * n(ks[4], (DEPTH, A_WIDTH)),
        "w_s": n(ks[5], (DEPTH, A_GROUPS, CHUNK, CHUNK)) * CHUNK ** -0.5,
        "b_s": 1.0 + 0.1 * n(ks[6], (DEPTH, A_GROUPS, CHUNK)),
        "conv_w": n(ks[7], (DEPTH, CONV_WIDTH, B_WIDTH)) * CONV_WIDTH ** -0.5,
        "conv_b": 0.02 * n(ks[8], (DEPTH, B_WIDTH)),
        "w_pool": n(ks[9], (DEPTH, len(POOL_WINDOWS), C_GROUP, C_GROUP)) * C_GROUP ** -0.5,
        "pool_scale": 1.0 + 0.02 * n(ks[10], (DEPTH, C_WIDTH)),
        "w_pa": n(ks[11], (DEPTH, A_WIDTH, D_MODEL)) * A_WIDTH ** -0.5,
        "w_pb": n(ks[12], (DEPTH, B_WIDTH, D_MODEL)) * B_WIDTH ** -0.5,
        "w_pc": n(ks[13], (DEPTH, C_WIDTH, D_MODEL)) * C_WIDTH ** -0.5,
        "w_o": n(ks[14], (DEPTH, D_MODEL, D_MODEL)) * D_MODEL ** -0.5,
        "final_g": 1.0 + 0.02 * n(ks[15], (D_MODEL,)),
    }

def second_block(x, norm_g, w_in, ln_g, ln_b, w_s, b_s, conv_w, conv_b, w_pool,
              pool_scale, w_pa, w_pb, w_pc, w_o, final_g):
    for l in range(DEPTH):
        x = _hybrid_layer(x, norm_g[l], w_in[l], ln_g[l], ln_b[l], w_s[l], b_s[l],
                          conv_w[l], conv_b[l], w_pool[l], pool_scale[l],
                          w_pa[l], w_pb[l], w_pc[l], w_o[l])
    return _rmsnorm_2(x, final_g)


_first_inputs = second_inputs


def second_inputs(seed=0):
    import zlib

    import numpy as np

    out = dict(_first_inputs(seed))
    spreads = {}
    factors = {'norm_g': 3.328,
     'ln_g': 8.0,
     'ln_b': 8.0,
     'b_s': 2.889,
     'conv_b': 8.0,
     'pool_scale': 8.0,
     'final_g': 2.862}
    for name, (base, spread) in spreads.items():
        noise = np.random.default_rng([zlib.crc32(name.encode()), seed]).standard_normal(out[name].shape)
        drawn = base * np.exp(spread * noise) if base else spread * noise
        out[name] = __import__('jax').numpy.asarray(drawn.astype(out[name].dtype))
    for name, factor in factors.items():
        out[name] = (out[name] * factor).astype(out[name].dtype)
    return out


_narrow_inputs = second_inputs


def second_inputs(seed=0):

    out = dict(_narrow_inputs(seed))
    wider = {'ln_g': 11.51,
     'ln_b': 11.61,
     'b_s': 3.97,
     'conv_b': 5.62,
     'pool_scale': 5.78,
     'final_g': 3.22}
    for name, times in wider.items():
        mean = out[name].mean()
        out[name] = (mean + times * (out[name] - mean)).astype(out[name].dtype)
    return out


def setup_inputs(seed=0):
    out = dict(first_inputs(seed))
    for name, value in second_inputs(seed + 1).items():
        if name != "x":
            out[name + "_2"] = value
    return out


def reference(
    x, c, w_ada, b_ada, g_mix, w_in, b_gate, a_re, a_im, log_dt, b_re, b_im, c_re, c_im, d_skip,
    w_glu, b_glu, w_proj_att, w_proj_ssm, w_out, g_ffn, w_up, w_conv, b_conv, w_down, g_final,
    norm_g_2, w_in_2, ln_g_2, ln_b_2, w_s_2, b_s_2, conv_w_2, conv_b_2, w_pool_2, pool_scale_2,
    w_pa_2, w_pb_2, w_pc_2, w_o_2, final_g_2,
):
    x = first_block(
        x, c, w_ada, b_ada, g_mix, w_in, b_gate, a_re, a_im, log_dt, b_re, b_im, c_re, c_im,
        d_skip, w_glu, b_glu, w_proj_att, w_proj_ssm, w_out, g_ffn, w_up, w_conv, b_conv,
        w_down, g_final,
    )
    return second_block(
        x, norm_g_2, w_in_2, ln_g_2, ln_b_2, w_s_2, b_s_2, conv_w_2, conv_b_2, w_pool_2,
        pool_scale_2, w_pa_2, w_pb_2, w_pc_2, w_o_2, final_g_2,
    )


_drawn_inputs = setup_inputs


def setup_inputs(seed=0):
    import zlib

    import numpy as np

    out = dict(_drawn_inputs(seed))
    spreads = {}
    factors = {'g_mix': 8.0,
     'b_gate': 8.0,
     'a_re': 64.0,
     'a_im': 46.8,
     'log_dt': 55.544,
     'b_re': 64.0,
     'b_im': 57.88,
     'c_re': 64.0,
     'c_im': 58.752,
     'b_glu': 8.0,
     'g_ffn': 5.034,
     'b_conv': 7.328}
    for name, (base, spread) in spreads.items():
        noise = np.random.default_rng([zlib.crc32(name.encode()), seed]).standard_normal(out[name].shape)
        drawn = base * np.exp(spread * noise) if base else spread * noise
        out[name] = __import__('jax').numpy.asarray(drawn.astype(out[name].dtype))
    for name, factor in factors.items():
        out[name] = (out[name] * factor).astype(out[name].dtype)
    return out
```

```python
from contextlib import ExitStack, contextmanager

import numpy as np

import concourse.bass as bass
from concourse import mybir

ACT = mybir.ActivationFunctionType
ALU = mybir.AluOpType
F32 = mybir.dt.float32
F32R = mybir.dt.float32r

P = 128
T = 1024
D = 1024
KD = D // P
HALF = 512
NB = 256
HEADS, HD = 8, 64
ATT = HEADS * HD
KA = ATT // P
SSM = 256
GROUPS, GCH, NSTATE = 16, 16, 64
STILES = GROUPS * NSTATE // P
LOGT = 10
FF = 2048
CONV = 3
W2 = 512
K2 = W2 // P
QB = T // P
WINDOWS = (2, 4, 8, 16)
RMS_EPS, LN_EPS = 1e-6, 1e-5
TWO_PI_PARTS = (6.28125, 4058 / 2**21, 2 * np.pi - 6.28125 - 4058 / 2**21)
ROUND = 1.5 * 2**23
MASKED = -1e30

N_US, N_GATE, N_QKV, N_PROJ, N_OUT, N_FFN = 0, 1, 9, 15, 19, 23
N_V2, N_A, N_GA, N_B, N_GB, N_C, N_GC, N_WO, N_END = 55, 57, 61, 69, 77, 85, 89, 97, 101
N_ADA_EARLY, N_ADA = 8, 24


def units_before(n):
    return 2 * n if n <= N_PROJ else 30 + 4 * (n - N_PROJ) if n <= N_OUT else 2 * n + 8


ROWS_A = dict(b_ada=48, g_mix=8, b_gate=16, g_ffn=8, b_conv=16, c=8, a_re=8, a_im=8, d_skip=2, b_glu=2,
              conv_b_2=4)
ROWS_B = dict(w_conv=48, g_final=8, norm_g_2=8, conv_w_2=12, pool_scale_2=4)


def places(rows):
    at, out = 0, {}
    for name, n in rows.items():
        out[name] = at
        at += n
    return out, at


class Steps:

    def __init__(self, eng, sem):
        self.eng, self.sem, self.base, self.n = eng, sem, 0, 0

    def __call__(self, ins):
        ins.then_inc(self.sem, 1)
        self.n += 1
        self.eng.wait_ge(self.sem, self.base + self.n)

    @contextmanager
    def loop(self, trips, per):
        start = self.base + self.n
        with self.eng.Fori(0, trips) as i:
            self.base, self.n = i * per + start, 0
            yield i
            assert self.n == per, (self.n, per)
        self.base, self.n = start + trips * per, 0


def constants():
    p, x = np.arange(P)[:, None], np.arange(T)[None, :]
    delta = p + (T - P) - x
    count = ((delta >= 0) & (delta <= 128)).astype(np.float64)
    count += (delta >= 0) & (delta <= 512) & (delta % 4 == 0)
    count += (delta >= 0) & (delta <= 2048) & (delta % 16 == 0)
    log8 = np.where(count > 0, 8 * np.log(np.maximum(count, 1)), MASKED)
    ch, st = np.arange(P)[None, None, :], np.arange(P)[:, None, None]
    k = np.arange(4)[None, :, None]
    mask_b = (ch // GCH == 2 * k + st // NSTATE)
    mask_c = mask_b.transpose(2, 1, 0)
    inv = np.stack([1.0 / np.minimum(np.arange(1, 17), w) for w in WINDOWS])
    return dict(
        k_ident=np.eye(P, dtype=np.float32),
        k_delta=np.ascontiguousarray(delta, np.float32),
        k_log8=np.ascontiguousarray(log8, np.float32),
        k_mask_b=np.ascontiguousarray(mask_b, np.float32),
        k_mask_c=np.ascontiguousarray(mask_c, np.float32),
        k_inv=np.ascontiguousarray(np.broadcast_to(inv[None], (P, 4, 16)), np.float32),
    )


def build(nc, a, out):
    ctx = ExitStack()
    with ctx:
        base = -(-nc.sbuf_base // 32) * 32
        kib = 1024

        def at(name, shape, offset, dt=F32):
            return nc.alloc_sbuf_tensor_at(name, shape, dt, offset=base + offset)

        fence = ctx.enter_context(nc.sbuf_tensor("fence", [P, (nc.sbuf_top - base) // 4], F32))

        act_h = at("act_h", [P, KD, T], 0, F32R)
        act_l = at("act_l", [P, KD, T], 32 * kib, F32R)
        w_h = at("w_h", [P, 2, KD, NB], 64 * kib, F32R)
        w_l = at("w_l", [P, 2, KD, NB], 80 * kib, F32R)
        in2_h = at("in2_h", [P, 4, T], 96 * kib, F32R)
        in2_l = at("in2_l", [P, 4, T], 112 * kib, F32R)
        raw = at("raw", [P, 2, KD, NB], 128 * kib)

        CONST = 144 * kib
        spot = [CONST]

        def keep(name, shape, dt=F32):
            n = int(np.prod(shape[1:])) * 4
            t = at(name, shape, spot[0], dt)
            spot[0] += -(-n // 32) * 32
            return t

        ident = keep("ident", [P, P])
        ones = keep("ones", [P, P])
        cols_a = keep("cols_a", [P, P])
        cols_b = keep("cols_b", [P, P])
        mod = keep("mod", [P, 48])
        eps_rms = keep("eps_rms", [P, 1])
        gain = keep("gain", [P, 2, KD])
        c_act = keep("c_act", [P, KD])
        late = spot[0]
        mask_b = keep("mask_b", [P, 4, P])
        mask_c = keep("mask_c", [P, 4, P])
        bb = keep("bb", [P, 2, STILES, GCH])
        cc = keep("cc", [P, 2, 2, NSTATE])
        mag = keep("mag", [P, STILES])
        turn = keep("turn", [P, 2, STILES, LOGT])
        cur = keep("cur", [P, 2, 4, LOGT])
        cmag = keep("cmag", [P, 4])
        bct = keep("bct", [P, 2, 4, P])
        w_glu = keep("w_glu", [P, 2, SSM])
        assert spot[0] <= 160 * kib, spot[0] / kib
        spot[0] = late
        wst = keep("wst", [P, 8, P])
        ln_g = keep("ln_g", [P, W2])
        ln_b = keep("ln_b", [P, W2])
        bs_row = keep("bs_row", [P, K2, P])
        w_pool = keep("w_pool", [P, 4, P])
        inv = keep("inv", [P, 4, 16])
        bn = keep("bn", [P, QB, 6])
        bn_mv = keep("bn_mv", [P, QB, 2])
        ln_rstd = keep("ln_rstd", [P, QB])
        assert spot[0] <= 160 * kib, spot[0] / kib

        x_tok = at("x_tok", [P, QB, D], 96 * kib)
        rows = at("rows", [P, 2, P], 200 * kib)
        prep = at("prep", [P, 16, STILES, LOGT], 192 * kib)
        b_in = at("b_in", [P, 2, STILES, GCH], 201 * kib)
        prep2 = at("prep2", [P, STILES, GCH], 198 * kib + 512)
        par = at("par", [P, 13, STILES], 198 * kib)
        h_t = at("h_t", [P, KD, T], 160 * kib)
        sq = at("sq", [P, 2, T], 192 * kib)
        nrm = at("nrm", [P, 2, T], 104 * kib)
        rstd = at("rstd", [P, T], 112 * kib)
        qk = at("qk", [P, 2 * KA, T], 96 * kib)
        s5 = at("s5", [P, 8, T], 96 * kib)
        yg = at("yg", [P, 2, T], 160 * kib)
        v_tok = at("v_tok", [P, QB, ATT], 168 * kib)
        us = at("us", [P, 2, T], 184 * kib)
        gate_st = at("gate_st", [P, 2, T], 192 * kib)
        bc = at("bc", [P, 4, P], 200 * kib)
        o_tok = at("o_tok", [P, QB, ATT], 184 * kib)
        q2 = at("q2", [P, 2, T], 0, F32R)
        k_hh = at("k_hh", [P, 2, T], 8 * kib, F32R)
        k_ll = at("k_ll", [P, 2, T], 16 * kib, F32R)
        v_st = at("v_st", [P, 2, QB, HD], 24 * kib)
        prob = at("prob", [P, 4, T], 28 * kib)
        prob_t = at("prob_t", [P, 2, T], 44 * kib)
        bias = at("bias", [P, 2, T], 52 * kib)
        delta = at("delta", [P, T], 60 * kib)
        log8 = at("log8", [P, T], 64 * kib)
        neg_max = at("neg_max", [P, 4], 204 * kib)
        den = at("den", [P, 4], 204 * kib + 32)
        rden = at("rden", [P, 4], 204 * kib + 64)
        ys_h = at("ys_h", [P, 2, T], 168 * kib, F32R)
        ys_l = at("ys_l", [P, 2, T], 176 * kib, F32R)
        gate_in = at("gate_in", [P, 2, 2, T], 184 * kib)
        mix = at("mix", [P, 2, T], 160 * kib)
        conv = at("conv", [P, 2, T], 192 * kib)
        ffn = at("ffn", [P, T], 200 * kib)
        ws_tok = at("ws_tok", [P, T], 120 * kib)
        vg = at("vg", [P, QB, W2], 160 * kib)
        a_u = at("a_u", [P, 2, T], 176 * kib)
        a_z = at("a_z", [P, 2, T], 184 * kib)
        a_s = at("a_s", [P, T], 192 * kib)
        merged = at("merged", [P, KD, T], 160 * kib)
        br = at("br", [P, 2, T], 192 * kib)
        br2 = at("br2", [P, T], 200 * kib)
        pool_in = [br[:, 1, :], br2[:]]
        y_t = at("y_t", [P, KD, T], 160 * kib)
        o_row = at("o_row", [P, 2, D], 192 * kib)
        g_row = at("g_row", [P, D], 200 * kib)
        o_sq = at("o_sq", [P, D], 64 * kib)
        o_ssq = at("o_ssq", [P, 3, QB], 68 * kib)

        tiles = [(hh, qb) for hh in range(2) for long in range(QB - 1, QB // 2 - 1, -1) for qb in (long, QB - 1 - long)]
        NT = len(tiles)
        STAGED = 7

        ps = ctx.enter_context(nc.psum_tensor("ps", [P, 4, T], F32))

        gates_d = nc.dram_tensor("gates_scratch", [2 * KD, P, T], F32).ap()
        h_d = nc.dram_tensor("h_scratch", [KD, P, T], F32).ap()
        x2_d = nc.dram_tensor("x2_scratch", [KD, P, T], F32).ap()

        names = """vec_in const_in x_in late_in attn_in g_row_in dve act colt colt_read c_ready consts_ready tr
            h_ready h_out ada_done mod_ready mod_read sq_ready sq_used std_ready rstd_ready t_ready hi_ready
            u_ready w_high w_split gemm us_ready gate_read bc_ready bct_done bct_copied bu_ready bu_read
            x_ready y_done y_read yg_ready qkv_read glu_done sig_ready ys_ready staged s_ready sm_ready
            p_ready pt0 pt1 ptc0 ptc1 pv o_ready otr oh_ready ot_ready ysh proj_read mix_ready mh_ready
            merged_ready out_read acc_ready silu_ready a_read v_read fh_ready f_ready down_read x2_ready
            x2_out wst_done wst_ready wst_masked v2_read vn_ready au_read sg_done sg_read az_read ap_ready
            ah_ready a_ready xb_read bc_read bz_read bg_read bp_ready bh_ready b_ready xc_read pooled
            pool_done cz_read cp_ready ch_ready sa_ready pa_read sb_ready pb_read mb_ready sc_ready pc_read
            mc_ready m2_high m2_ready s5_in dt_ready lrdt_ready angle_ready turn_ready mod2_ready passed
            ln_var ln_std ch_done y_gated y_ready otr2 ostd orow""".split()
        s = {n: ctx.enter_context(nc.semaphore(n)) for n in names}

        def pair(name, n=2):
            return [ctx.enter_context(nc.semaphore(f"{name}{i}")) for i in range(n)]

        ada_in, w_in_, ws_in = pair("ada_in"), pair("w_in"), pair("ws_in")
        gate_out, gate_back = pair("gate_out"), pair("gate_back")
        h_back, x2_back, row_out = pair("h_back", KD), pair("x2_back", KD), pair("row_out")

        at_a, n_a = places(ROWS_A)
        at_b, n_b = places(ROWS_B)
        assert n_a == P

        def col_a(name, j=0, n=1):
            return cols_a[:, at_a[name] + j:at_a[name] + j + n]

        def col_b(name, j=0, n=1):
            return cols_b[:, at_b[name] + j:at_b[name] + j + n]

        def weights(name, col, n=NB, row=0, k=KD):
            w = a[name][0]
            return w[row:row + k * P, :].rearrange("(k p) n -> p k n", p=P)[:, :, col]

        def slot(i):
            return ps[:, i, :]

        block = ctx.enter_context(nc.Block())

        @block.sync
        def _(sp):
            for t, rr in enumerate((ROWS_A, ROWS_B)):
                for name, r0 in places(rr)[0].items():
                    v = a[name]
                    v = v.flatten() if len(v.shape) > 1 else v
                    sp.dma_start(rows[r0:r0 + rr[name], t, :],
                                 v.rearrange("(r p) -> r p", p=P)).then_inc(s["vec_in"], 16)
            sp.dma_start(ident[:], a["k_ident"]).then_inc(s["const_in"], 16)
            sp.dma_start(x_tok[:], a["x"][0].rearrange("(t p) d -> p t d", p=P)).then_inc(s["x_in"], 16)

            def ada(b, k):
                sp.dma_start(raw[:, k, :, :], weights("w_ada", bass.ds(b * NB, NB))).then_inc(ada_in[k], 16)

            for b in range(N_ADA_EARLY):
                if b >= 2:
                    sp.wait_ge(s["ada_done"], b - 1)
                ada(b, b % 2)

            def load(n, k, name, col, row=0, kc=KD):
                sp.wait_ge(s["w_split"], n - 1)
                sp.sem_inc(s["passed"], 1)
                sp.dma_start(raw[:, k, 0:kc, :],
                             weights(name, bass.ds(col, NB), row=row, k=kc)).then_inc(w_in_[k], 16)

            sp.wait_ge(s["ada_done"], N_ADA_EARLY - 1)
            sp.dma_start(raw[:, 0, :, :], weights("w_in", bass.ds(3 * ATT, NB))).then_inc(w_in_[0], 16)
            sp.wait_ge(s["ada_done"], N_ADA_EARLY)
            sp.dma_start(raw[:, 1, :, :], weights("w_in", bass.ds(3 * ATT + SSM, NB))).then_inc(w_in_[1], 16)
            load(2, 0, "w_in", 3 * ATT + SSM + NB)
            with sp.Fori(0, 3) as i:
                for k in range(2):
                    load(2 * i + 3 + k, 1 - k, "w_in", i * (2 * NB) + 3 * ATT + SSM + (2 + k) * NB)
            with sp.Fori(0, 3) as i:
                for k in range(2):
                    load(2 * i + N_QKV + k, 1 - k, "w_in", i * (2 * NB) + k * NB)
            sp.wait_ge(s["w_split"], N_PROJ)
            for b in range(N_ADA_EARLY, N_ADA_EARLY + 2):
                ada(b, b % 2)
            sp.wait_ge(s["gemm"], units_before(N_PROJ))
            sp.dma_start(delta[:], a["k_delta"]).then_inc(s["attn_in"], 16)
            sp.dma_start(log8[:], a["k_log8"]).then_inc(s["attn_in"], 16)
            with sp.Fori(0, (N_ADA - N_ADA_EARLY - 2) // 2) as i:
                for k in range(2):
                    sp.wait_ge(s["ada_done"], 2 * i + N_ADA_EARLY + k + 1)
                    sp.sem_inc(s["passed"], 1)
                    ada(2 * i + N_ADA_EARLY + 2 + k, k)

            def proj(j, k):
                sp.dma_start(raw[:, k, 0:KA, :],
                             weights("w_proj_att", bass.ds(j * NB, NB), k=KA)).then_inc(w_in_[k], 16)
                sp.dma_start(raw[:, k, KA:KA + 2, :],
                             weights("w_proj_ssm", bass.ds(j * NB, NB), k=2)).then_inc(ws_in[k], 16)

            def gates(j):
                for cg in range(2):
                    if j:
                        sp.wait_ge(s["proj_read"], 2 * j + cg - 1)
                    for g in range(2):
                        sp.dma_start(gate_in[:, cg, g, :], gates_d[g * KD + 2 * j + cg]).then_inc(gate_back[cg], 16)

            sp.wait_ge(s["ada_done"], N_ADA)
            proj(0, 1)
            proj(1, 0)
            for k in range(2):
                sp.wait_ge(gate_out[k], 16 * KD)
            sp.wait_ge(s["oh_ready"], KA)
            sp.wait_ge(s["ot_ready"], KA)
            gates(0)
            for j in range(2, 4):
                gates(j - 1)
                sp.wait_ge(s["w_split"], N_PROJ + j - 1)
                proj(j, 1 - j % 2)
            gates(3)
            load(N_OUT, 1, "w_out", 0)
            load(N_OUT + 1, 0, "w_out", NB)
            sp.wait_ge(s["h_out"], 16)
            sp.wait_ge(s["gemm"], units_before(N_OUT))
            sp.wait_ge(s["merged_ready"], KD)
            for j in range(KD):
                sp.dma_start(h_t[:, j, :], h_d[j]).then_inc(h_back[j], 16)
            for k in range(2):
                load(N_OUT + 2 + k, 1 - k, "w_out", (2 + k) * NB)

            with sp.Fori(0, 4) as q:
                for p in range(2):
                    for k in range(2):
                        load(8 * q + N_FFN + 2 * p + k, 1 - k, "w_up", q * 512 + (k * FF + p * NB))
                for p in range(2):
                    for k in range(2):
                        n = 8 * q + N_FFN + 4 + 2 * p + k
                        sp.wait_ge(s["w_split"], n - 1)
                        sp.sem_inc(s["passed"], 1)
                        wd = a["w_down"][0].rearrange("(q k p) n -> p (q k) n", p=P, k=4)
                        sp.dma_start(raw[:, 1 - k, 0:4, :],
                                     wd[:, bass.ds(q * 4, 4), (2 * p + k) * NB:(2 * p + k + 1) * NB])\
                          .then_inc(w_in_[1 - k], 16)

            sp.dma_start(ln_g[:], a["ln_g_2"].partition_broadcast(P).rearrange("p a n -> p (a n)")).then_inc(s["late_in"], 16)
            sp.dma_start(ln_b[:], a["ln_b_2"].partition_broadcast(P).rearrange("p a n -> p (a n)")).then_inc(s["late_in"], 16)
            for h in range(2):
                for c in range(K2):
                    sp.dma_start(bs_row[64 * h:64 * h + 64, c, :],
                                 a["b_s_2"][0, 2 * c + h].partition_broadcast(64)).then_inc(s["late_in"], 16)
            sp.dma_start(w_pool[:], a["w_pool_2"][0].rearrange("g c d -> c g d")).then_inc(s["late_in"], 16)
            sp.dma_start(inv[:], a["k_inv"]).then_inc(s["late_in"], 16)
            sp.wait_ge(s["gemm"], units_before(N_V2))
            sp.dma_start(ws_tok[:].rearrange("p (g s) -> p g s", g=8),
                         a["w_s_2"][0].rearrange("g t s -> t g s")).then_inc(s["late_in"], 16)
            IN2 = dict(u=0, v=1, za=2, xb=3, bg=4, cg=5, zb=6, xc=7, zc=8)
            GATE2 = 9 * W2

            def pair2(n, k0, k1):
                load(n, 1, "w_in_2", k0)
                load(n + 1, 0, "w_in_2", k1)

            def gate2(n0, g, name):
                with sp.Fori(0, 4) as j:
                    load(2 * j + n0, 1, "w_in_2", j * NB + (GATE2 + g * D))
                    load(2 * j + n0 + 1, 0, name, j * NB, kc=K2)

            pair2(N_V2, IN2["v"] * W2, IN2["v"] * W2 + NB)
            for p in range(2):
                pair2(N_A + 2 * p, IN2["u"] * W2 + p * NB, IN2["za"] * W2 + p * NB)
            gate2(N_GA, 0, "w_pa_2")
            for p in range(2):
                pair2(N_B + 4 * p, IN2["xb"] * W2 + p * NB, IN2["cg"] * W2 + p * NB)
                pair2(N_B + 4 * p + 2, IN2["bg"] * W2 + p * NB, IN2["zb"] * W2 + p * NB)
            gate2(N_GB, 1, "w_pb_2")
            for p in range(2):
                pair2(N_C + 2 * p, IN2["xc"] * W2 + p * NB, IN2["zc"] * W2 + p * NB)
            gate2(N_GC, 2, "w_pc_2")
            pair_wo = [(N_WO, 1), (N_WO + 1, 0)]
            for n, k in pair_wo:
                load(n, k, "w_o_2", (n - N_WO) * NB)
            sp.wait_ge(s["m2_ready"], KD)
            for j in range(KD):
                sp.dma_start(y_t[:, j, :], x2_d[j]).then_inc(x2_back[j], 16)
            sp.dma_start(g_row[:], a["final_g_2"].partition_broadcast(P)).then_inc(s["g_row_in"], 16)
            for n, k in pair_wo:
                load(n + 2, k, "w_o_2", (n + 2 - N_WO) * NB)
            for t in range(QB):
                sp.wait_ge(s["orow"], t + 1)
                sp.dma_start(out[0, t * P:(t + 1) * P, :], o_row[:, t % 2, :]).then_inc(row_out[t % 2], 16)
            for k in range(2):
                sp.wait_ge(row_out[k], 16 * QB // 2)

        @block.gpsimd
        def _(pool):
            nc.gpsimd.memset(ones[:], 1.0).then_inc(s["consts_ready"], 1)
            nc.gpsimd.memset(eps_rms[:], RMS_EPS).then_inc(s["consts_ready"], 1)

            def split(n, k, landed, before=None, kc=KD, landed_ssm=None):
                pool.wait_ge(w_in_[k], landed)
                if landed_ssm:
                    pool.wait_ge(ws_in[k], landed_ssm)
                if before is not None:
                    pool.wait_ge(s["gemm"], before)
                pool.sem_inc(s["passed"], 1)
                nc.gpsimd.tensor_scalar(w_h[:, k, 0:kc, :], raw[:, k, 0:kc, :], 1.0, None, ALU.mult)\
                  .then_inc(s["w_high"], 1)
                pool.wait_ge(s["w_high"], n + 1)
                nc.gpsimd.tensor_tensor(w_l[:, k, 0:kc, :], raw[:, k, 0:kc, :],
                                        w_h[:, k, 0:kc, :].bitcast(F32), ALU.subtract).then_inc(s["w_split"], 1)

            def single(n, kc=KD, landed_ssm=None):
                split(n, n % 2, 16 * (n // 2 + 1), units_before(n - 1) if n >= 2 else None, kc, landed_ssm)

            def pairs(n0, trips, kcs=(KD, KD)):
                m = len(kcs)
                with pool.Fori(0, trips) as i:
                    for k, kc in enumerate(kcs):
                        n = n0 + k
                        split(i * m + n, n % 2, i * (8 * m) + 16 * (n // 2 + 1),
                              i * (2 * m) + units_before(n - 1), kc)

            for n in range(3):
                single(n)
            pairs(3, 6)

            stage_step = Steps(pool, s["staged"])

            def stage(p, e, done=None):
                own, other = slice(HD * e, HD * e + HD), slice(HD - HD * e, P - HD * e)
                if done is not None:
                    pool.wait_ge(s["pv"], done)
                q, k = qk[own, p, :], qk[own, p + KA, :]
                stage_step(nc.gpsimd.tensor_scalar(q2[own, e, :], q, 1.0, None, ALU.mult))
                stage_step(nc.gpsimd.tensor_scalar(k_hh[own, e, :], k, 1.0, None, ALU.mult))
                stage_step(nc.gpsimd.tensor_scalar(k_hh[other, e, :], k, 1.0, None, ALU.mult))
                stage_step(nc.gpsimd.tensor_tensor(q2[other, e, :], q, q2[own, e, :].bitcast(F32), ALU.subtract))
                for half in (own, other):
                    stage_step(nc.gpsimd.tensor_tensor(k_ll[half, e, :], k, k_hh[own, e, :].bitcast(F32), ALU.subtract))
                stage_step(nc.gpsimd.tensor_copy(v_st[:, e], v_tok[:, :, P * p + HD * e:P * p + HD * (e + 1)]))

            pool.wait_ge(s["qkv_read"], 12)
            for head in range(HEADS):
                stage(head // 2, head % 2, QB * (head - 1) if head >= 2 else None)
            for j in range(4):
                single(N_PROJ + j, KA + 2, 16 * (j // 2 + 1))
            single(N_OUT)
            single(N_OUT + 1)
            pairs(N_OUT + 2, 1)
            pairs(N_FFN, 4, (KD,) * 4 + (4,) * 4)
            pairs(N_V2, 1)
            pool.wait_ge(s["wst_ready"], 1)
            nc.gpsimd.affine_select(out=wst[:], in_=wst[:], compare_op=ALU.is_ge, fill=0.0, base=0,
                                    pattern=[[0, 8], [1, P]], channel_multiplier=-1).then_inc(s["wst_masked"], 1)
            pairs(N_A, 2)
            pairs(N_GA, 4, (KD, K2))
            pairs(N_B, 4)
            pairs(N_GB, 4, (KD, K2))
            pairs(N_C, 2)
            pairs(N_GC, 4, (KD, K2))
            pairs(N_WO, 2)

        @block.tensor
        def _(pe):
            def product(dst, k, cg, kc, high, low, kw=0):
                for th in range(2):
                    tok = slice(HALF * th, HALF * th + HALF)
                    for c in range(kc):
                        for p, (w, x) in enumerate(((w_h, high), (w_h, low), (w_l, high))):
                            last = nc.tensor.matmul(dst[:, tok], w[:, k, kw + c, P * cg:P * cg + P], x[:, c, tok],
                                                    start=(c == 0 and p == 0), stop=(c == kc - 1 and p == 2))
                return last

            def product_rows(dst, k, t0):
                for t in range(4):
                    tok = slice((t0 + t) * P, (t0 + t + 1) * P)
                    for c in range(KD):
                        for p, (w, x) in enumerate(((w_h, act_h), (w_h, act_l), (w_l, act_h))):
                            last = nc.tensor.matmul(dst[:, NB * t:NB * t + NB], x[:, c, tok], w[:, k, c, :],
                                                    start=(c == 0 and p == 0), stop=(c == KD - 1 and p == 2))
                return last

            def split_done(n):
                pe.wait_ge(s["w_split"], n + 1)

            def gate_unit(ch, t, cg):
                if cg == 0:
                    split_done(4 * ch + N_GATE + t)
                if t:
                    pe.wait_ge(s["gate_read"], 8 * ch + 2 * t + cg - 1)
                else:
                    pe.wait_ge(s["gate_read"], 8 * ch)
                product(slot(cg), (N_GATE + t) % 2, cg, KD, act_h, act_l).then_inc(s["gemm"], 1)

            def s5_out(ch, t):
                pe.wait_ge(s["x_ready"], 4 * ch + t + 1)
                if t == 0:
                    pe.wait_ge(s["y_read"], ch)
                for th in range(2):
                    tok = slice(HALF * th, HALF * th + HALF)
                    for m in range(2):
                        last = nc.tensor.matmul(slot(3)[:, tok], bct[:, t % 2, 2 + m, :], s5[:, 6 + m, tok],
                                                start=(t == 0 and m == 0), stop=(t == 3 and m == 1),
                                                skip_group_check=True)
                last.then_inc(s["y_done"], 1)

            pe.wait_ge(s["vec_in"], 16 * (len(ROWS_A) + len(ROWS_B)))
            pe.wait_ge(s["const_in"], 16)
            nc.tensor.transpose(slot(0)[:, 0:P], rows[:, 0, :], ident[:])
            nc.tensor.transpose(slot(0)[:, P:P + n_b], rows[0:n_b, 1, :], ident[0:n_b, 0:n_b]).then_inc(s["colt"], 1)
            pe.wait_ge(s["x_in"], 16)
            for c in range(KD):
                if c >= 4:
                    pe.wait_ge(s["h_ready"], c - 3)
                elif c == 0:
                    pe.wait_ge(s["colt_read"], 1)
                for t in range(QB):
                    last = nc.tensor.transpose(slot(c % 4)[:, P * t:P * t + P], x_tok[:, t, P * c:P * c + P], ident[:])
                last.then_inc(s["tr"], 1)

            def sum_squares(k, read, count):
                if k == 0:
                    pe.wait_ge(s["consts_ready"], 2)
                pe.wait_ge(read, count)
                for c in range(KD):
                    pe.wait_ge(s["sq_ready"], KD * k + c + 1)
                    for th in range(2):
                        tok = slice(HALF * th, HALF * th + HALF)
                        last = nc.tensor.matmul(slot(3)[:, tok], ones[:], sq[:, c % 2, tok],
                                                start=(c == 0), stop=(c == KD - 1), skip_group_check=True)
                    last.then_inc(s["sq_used"], 1)

            sum_squares(0, s["h_ready"], KD)

            def ada(dst, k):
                for cg in range(2):
                    for c in range(KD):
                        last = nc.tensor.matmul(dst[:, cg:cg + 1], raw[:, k, c, P * cg:P * cg + P], c_act[:, c:c + 1],
                                                start=(c == 0), stop=(c == KD - 1))
                return last

            pe.wait_ge(s["c_ready"], 1)
            for b in range(N_ADA_EARLY):
                pe.wait_ge(ada_in[b % 2], 16 * (b // 2 + 1))
                ada(slot(2)[:, 2 * b:2 * b + 2], b % 2).then_inc(s["ada_done"], 1)

            pe.wait_ge(s["u_ready"], KD)
            split_done(0)
            for cg in range(2):
                product(slot(cg), 0, cg, KD, act_h, act_l).then_inc(s["gemm"], 1)

            pe.wait_ge(s["us_ready"], 2)
            pe.wait_ge(s["mod_read"], 1)
            with pe.Fori(0, 2) as ch:
                for t in range(4):
                    pe.wait_ge(s["bc_ready"], 4 * ch + t + 1)
                    if t:
                        pe.wait_ge(s["bu_read"], 8 * ch + 2 * t)
                    else:
                        pe.wait_ge(s["bu_read"], 8 * ch)
                    for m in range(4):
                        last = nc.tensor.transpose(slot(2)[:, P * m:P * m + P], bc[:, m, :], ident[:])
                    last.then_inc(s["bct_done"], 1)
                    pe.wait_ge(s["bct_copied"], 4 * ch + t + 1)
                    for m in range(2):
                        if m == 1:
                            gate_unit(ch, t, 0)
                            pe.wait_ge(s["bu_read"], 8 * ch + 2 * t + 1)
                        for th in range(2):
                            tok = HALF * th
                            last = nc.tensor.matmul(slot(2)[:, tok:tok + HALF], bct[:, t % 2, m, :],
                                                    us[:, bass.ds(ch, 1), tok:tok + HALF].rearrange("p a n -> p (a n)"),
                                                    start=True, stop=True)
                        last.then_inc(s["bu_ready"], 1)
                    if t:
                        s5_out(ch, t - 1)
                    gate_unit(ch, t, 1)
                s5_out(ch, 3)

            pe.wait_ge(s["gate_read"], 2 * KD)
            with pe.Fori(0, 2) as i:
                for b in range(2):
                    split_done(2 * i + N_QKV + b)
                    for cg in range(2):
                        if b:
                            pe.wait_ge(s["qkv_read"], 4 * i + cg + 1)
                        else:
                            pe.wait_ge(s["qkv_read"], 4 * i)
                        product(slot(cg), 1 - b, cg, KD, act_h, act_l).then_inc(s["gemm"], 1)
            for b in range(2):
                split_done(N_QKV + 4 + b)
                for h in range(2):
                    pe.wait_ge(s["qkv_read"], 8 + 2 * b + h - 1)
                    product_rows(slot(h), 1 - b, 4 * h).then_inc(s["gemm"], 1)
            pe.wait_ge(s["yg_ready"], 2)
            for o in range(2):
                for th in range(2):
                    tok = slice(HALF * th, HALF * th + HALF)
                    for c in range(2):
                        last = nc.tensor.matmul(slot(2 + o)[:, tok], w_glu[:, c, P * o:P * o + P], yg[:, c, tok],
                                                start=(c == 0), stop=(c == 1))
                last.then_inc(s["glu_done"], 1)

            pe.wait_ge(s["qkv_read"], 12)
            pe.wait_ge(s["y_gated"], 2)

            def scores(p, t):
                e, qb = tiles[t % NT]
                if t % QB == 0:
                    pe.wait_ge(s["staged"], p * (2 * STAGED) + STAGED * (t // QB + 1))
                if t >= 2:
                    pe.wait_ge(s["sm_ready"], NT * p + t - 1)
                n = (qb + 1) * P
                for c0 in range(0, n, HALF):
                    w = min(HALF, max(2 * P, n - c0))
                    for k in (k_hh, k_ll):
                        last = nc.tensor.matmul(slot(t % 2)[:, c0:c0 + w], q2[:, e, P * qb:P * qb + P],
                                                k[:, e, c0:c0 + w], start=(k is k_hh), stop=(k is k_ll))
                last.then_inc(s["s_ready"], 1)

            def transposes(p, t):
                qb = tiles[t % NT][1]
                pe.wait_ge(s["p_ready"], NT * p + t + 1)
                if t:
                    pe.wait_ge(s["ptc0"], NT * p + t)
                for b in range(min(4, qb + 1)):
                    last = nc.tensor.transpose(slot(2)[:, P * b:P * b + P], prob[:, t % 4, P * b:P * b + P], ident[:])
                last.then_inc(s["pt0"], 1)
                if qb >= 4:
                    if t:
                        pe.wait_ge(s["ptc1"], QB * p + t // 2)
                    for b in range(4, qb + 1):
                        last = nc.tensor.transpose(slot(2)[:, P * b:P * b + P], prob[:, t % 4, P * b:P * b + P], ident[:])
                    last.then_inc(s["pt1"], 1)

            def values(p, t):
                e, qb = tiles[t]
                pe.wait_ge(s["ptc0"], NT * p + t + 1)
                if qb >= 4:
                    pe.wait_ge(s["ptc1"], QB * p + t // 2 + 1)
                if t:
                    pe.wait_ge(s["o_ready"], NT * p + t - 1)
                else:
                    pe.wait_ge(s["o_ready"], NT * p)
                dst = slot(3)[:, HALF * (t % 2):HALF * (t % 2) + HALF]
                for b in range(qb + 1):
                    last = nc.tensor.matmul(dst[:, 0:HD], prob_t[:, t % 2, P * b:P * b + P], v_st[:, e, b, :],
                                            start=(b == 0), stop=(b == qb))
                last.then_inc(s["pv"], 1)
                if t % 4 == 3:
                    k = t // 4
                    pe.wait_ge(ada_in[k % 2], 32 * p + 16 * (N_ADA_EARLY // 2 + k // 2 + 1))
                    ada(dst[:, HD:HD + 2], k % 2).then_inc(s["ada_done"], 1)

            def heads(p, last):
                end = NT if last else NT + 3
                for t in range(NT):
                    if t + 3 < end:
                        scores(p, t + 3)
                    if t + 1 < end:
                        transposes(p, t + 1)
                    values(p, t)

            for t in range(3):
                scores(0, t)
            transposes(0, 0)
            with pe.Fori(0, HEADS // 2 - 1) as p:
                heads(p, False)
            heads(HEADS // 2 - 1, True)

            pe.wait_ge(s["o_ready"], HEADS * QB)
            for c in range(KA):
                for t in range(QB):
                    last = nc.tensor.transpose(slot(c)[:, P * t:P * t + P], o_tok[:, t, P * c:P * c + P], ident[:])
                last.then_inc(s["otr"], 1)

            pe.wait_ge(s["ot_ready"], KA)
            pe.wait_ge(s["ys_ready"], 2)
            with pe.Fori(0, 2) as i:
                for b in range(2):
                    split_done(2 * i + N_PROJ + b)
                    for cg in range(2):
                        if b:
                            pe.wait_ge(s["proj_read"], 4 * i + cg + 1)
                        else:
                            pe.wait_ge(s["proj_read"], 4 * i)
                        product(slot(2 * cg), 1 - b, cg, KA, in2_h, in2_l).then_inc(s["gemm"], 1)
                        product(slot(2 * cg + 1), 1 - b, cg, 2, ys_h, ys_l, kw=KA).then_inc(s["gemm"], 1)

            pe.wait_ge(s["merged_ready"], KD)
            with pe.Fori(0, 2) as i:
                pe.wait_ge(s["out_read"], 4 * i)
                for b in range(2):
                    split_done(2 * i + N_OUT + b)
                    for cg in range(2):
                        product(slot(2 * b + cg), 1 - b, cg, KD, act_h, act_l).then_inc(s["gemm"], 1)

            sum_squares(1, s["out_read"], KD)
            pe.wait_ge(s["u_ready"], 2 * KD)
            with pe.Fori(0, 4) as q:
                pe.wait_ge(s["down_read"], 8 * q)
                for p in range(2):
                    for b in range(2):
                        split_done(8 * q + N_FFN + 2 * p + b)
                        for cg in range(2):
                            if p:
                                pe.wait_ge(s["v_read"] if b else s["a_read"], 4 * q + cg + 1)
                            product(slot(2 * b + cg), 1 - b, cg, KD, act_h, act_l).then_inc(s["gemm"], 1)
                pe.wait_ge(s["f_ready"], 4 * q + 4)
                for u in range(8):
                    if u % 2 == 0:
                        split_done(8 * q + N_FFN + 4 + u // 2)
                    if u >= 4:
                        pe.wait_ge(s["down_read"], 8 * q + u - 3)
                    product(slot(u % 4), 1 - (u // 2) % 2, u % 2, 4, in2_h, in2_l).then_inc(s["gemm"], 1)

            sum_squares(2, s["down_read"], 32)
            sum_squares(3, s["std_ready"], 3)
            pe.wait_ge(s["late_in"], 16 * 13)
            for g in range(8):
                last = nc.tensor.transpose(slot(0)[:, P * g:P * g + P], ws_tok[:, P * g:P * g + P], ident[:])
            last.then_inc(s["wst_done"], 1)
            pe.wait_ge(s["u_ready"], 3 * KD)
            for b in range(2):
                split_done(N_V2 + b)
                for h in range(2):
                    if b == 0 and h == 0:
                        pe.wait_ge(s["wst_ready"], 1)
                    product_rows(slot(2 * b + h), 1 - b, 4 * h).then_inc(s["gemm"], 1)
            for p in range(2):
                for b in range(2):
                    split_done(N_A + 2 * p + b)
                    for cg in range(2):
                        if b:
                            pe.wait_ge(s["au_read"], 2 * p + cg + 1)
                        elif p:
                            pe.wait_ge(s["az_read"], cg + 1)
                        else:
                            pe.wait_ge(s["v2_read"], 4)
                        product(slot(cg), 1 - b, cg, KD, act_h, act_l).then_inc(s["gemm"], 1)
                    if b == 0:
                        pe.wait_ge(s["vn_ready"], 1)
                        pe.wait_ge(s["wst_masked"], 1)
                        for cg in range(2):
                            if p:
                                pe.wait_ge(s["sg_read"], cg + 1)
                            for g in range(2):
                                grp = 2 * (2 * p + cg) + g
                                for t in range(QB):
                                    last = nc.tensor.matmul(slot(2 + cg)[HD * g:HD * g + HD, P * t:P * t + P],
                                                            vg[:, t, HD * grp:HD * grp + HD], wst[:, grp, :],
                                                            start=True, stop=True)
                            last.then_inc(s["sg_done"], 1)

            def gate_loop(n0, ready, gate_read, p_read):
                pe.wait_ge(ready, 4)
                with pe.Fori(0, 4) as j:
                    for b in range(2):
                        split_done(2 * j + n0 + b)
                        for cg in range(2):
                            pe.wait_ge(p_read if b else gate_read, 2 * j)
                            if b:
                                product(slot(2 + cg), 0, cg, K2, in2_h, in2_l).then_inc(s["gemm"], 1)
                            else:
                                product(slot(cg), 1, cg, KD, act_h, act_l).then_inc(s["gemm"], 1)

            gate_loop(N_GA, s["a_ready"], s["sa_ready"], s["pa_read"])
            pe.wait_ge(s["pa_read"], KD)
            for p in range(2):
                for b, (before, free) in enumerate(((s["bg_read"], s["xb_read"]), (s["bz_read"], s["bc_read"]))):
                    split_done(N_B + 4 * p + b)
                    for cg in range(2):
                        if p:
                            pe.wait_ge(before, cg + 1)
                        product(slot(2 * b + cg), 1 - b, cg, KD, act_h, act_l).then_inc(s["gemm"], 1)
                for b, free in enumerate((s["xb_read"], s["bc_read"])):
                    split_done(N_B + 4 * p + 2 + b)
                    for cg in range(2):
                        pe.wait_ge(free, 2 * p + cg + 1)
                        product(slot(2 * b + cg), 1 - b, cg, KD, act_h, act_l).then_inc(s["gemm"], 1)
            gate_loop(N_GB, s["b_ready"], s["sb_ready"], s["pb_read"])
            pe.wait_ge(s["pb_read"], KD)
            for p in range(2):
                for b in range(2):
                    split_done(N_C + 2 * p + b)
                    for cg in range(2):
                        if p:
                            pe.wait_ge(s["cz_read"] if b else s["cp_ready"], cg + 1)
                        product(slot(2 * b + cg), 1 - b, cg, KD, act_h, act_l).then_inc(s["gemm"], 1)
                for cg in range(2):
                    c = 2 * p + cg
                    pe.wait_ge(s["pooled"], c + 1)
                    for th in range(2):
                        tok = slice(HALF * th, HALF * th + HALF)
                        last = nc.tensor.matmul(slot(cg)[:, tok], w_pool[:, c, :], pool_in[c % 2][:, tok],
                                                start=True, stop=True)
                    last.then_inc(s["pool_done"], 1)
            gate_loop(N_GC, s["ch_done"], s["sc_ready"], s["pc_read"])

            pe.wait_ge(s["m2_ready"], KD)
            with pe.Fori(0, 2) as i:
                pe.wait_ge(s["y_ready"], 4 * i)
                for b in range(2):
                    split_done(2 * i + N_WO + b)
                    for cg in range(2):
                        product(slot(2 * b + cg), 1 - b, cg, KD, act_h, act_l).then_inc(s["gemm"], 1)
            pe.wait_ge(s["y_ready"], KD)
            for t in range(QB):
                if t >= 4:
                    pe.wait_ge(s["orow"], t - 3)
                for c in range(KD):
                    last = nc.tensor.transpose(slot(t % 4)[:, P * c:P * c + P], y_t[:, c, P * t:P * t + P], ident[:])
                last.then_inc(s["otr2"], 1)

        @block.scalar
        def _(act):
            A = nc.scalar
            step = Steps(act, s["act"])

            act.dma_start(mask_b[:], a["k_mask_b"]).then_inc(s["s5_in"], 16)
            act.dma_start(mask_c[:], a["k_mask_c"]).then_inc(s["s5_in"], 16)
            for m, name in enumerate(("b_re", "b_im")):
                act.dma_start(b_in[:, m], a[name][0].rearrange("(t g) n c -> (g n) t c", g=2)).then_inc(s["s5_in"], 16)
            for m, name in enumerate(("c_re", "c_im")):
                act.dma_start(cc[:, m], a[name][0].rearrange("(h g) c n -> (g c) h n", h=2)).then_inc(s["s5_in"], 16)
            with nc.allow_non_contiguous_dma(reason="sixteen time steps, one value for each state"):
                for g in range(2):
                    act.dma_start(par[NSTATE * g:NSTATE * g + NSTATE, 0, :],
                                  a["log_dt"][0].rearrange("(t g) -> g t", g=2)[g].partition_broadcast(NSTATE))\
                       .then_inc(s["s5_in"], 16)
            act.dma_start(w_glu[:], a["w_glu"][0].rearrange("(k p) n -> p k n", p=P)).then_inc(s["s5_in"], 16)

            act.wait_ge(s["colt_read"], 1)
            A.activation(c_act[:], col_a("c", 0, KD), ACT.Silu).then_inc(s["c_ready"], 1)
            act.wait_ge(s["s5_in"], 16 * 9)
            A.activation(par[:, 1, :], par[:, 0, :], ACT.Exp).then_inc(s["dt_ready"], 1)
            act.wait_ge(s["lrdt_ready"], 1)
            step(A.activation(mag[:], par[:, 2, :], ACT.Exp))
            act.wait_ge(s["angle_ready"], 1)
            step(A.activation(turn[:, 0], prep[:, 3, :, :], ACT.Sin))
            A.activation(turn[:, 1], prep[:, 2, :, :], ACT.Sin).then_inc(s["turn_ready"], 1)

            def squares(k, ready, before):
                for c in range(KD):
                    act.wait_ge(ready, before + c + 1)
                    if c >= 2:
                        act.wait_ge(s["sq_used"], KD * k + c - 1)
                    A.activation(sq[:, c % 2, :], h_t[:, c, :], ACT.Square).then_inc(s["sq_ready"], 1)
                act.wait_ge(s["sq_used"], KD * k + KD)
                if k == 2:
                    act.wait_ge(s["gemm"], units_before(N_V2))
                A.activation(rstd[:], slot(3), ACT.Sqrt, scale=1.0 / D, bias=eps_rms[:]).then_inc(s["std_ready"], 1)

            def norm(nu, scale, shift):
                for c in range(KD):
                    act.wait_ge(s["t_ready"], KD * nu + c + 1)
                    if c == 0 and nu == 2:
                        act.wait_ge(s["gemm"], units_before(N_V2))
                    if c >= 2:
                        act.wait_ge(s["u_ready"], KD * nu + c - 1)
                    b = shift(c) if shift else 0.0
                    step(A.activation(nrm[:, c % 2, :], sq[:, c % 2, :], ACT.Identity, scale=scale(c), bias=b))
                    A.activation(act_h[:, c, :], sq[:, c % 2, :], ACT.Identity, scale=scale(c), bias=b)\
                     .then_inc(s["hi_ready"], 1)

            act.wait_ge(s["consts_ready"], 2)
            act.wait_ge(s["h_ready"], KD)
            act.dma_start(h_d.rearrange("c p t -> p c t"), h_t[:]).then_inc(s["h_out"], 16)
            squares(0, s["h_ready"], 0)
            act.wait_ge(s["mod_ready"], 1)
            norm(0, lambda c: gain[:, 0, c:c + 1], lambda c: mod[:, c:c + 1])

            act.wait_ge(s["us_ready"], 2)

            def gate(ch, j):
                k = j % 2
                act.wait_ge(s["gemm"], 8 * ch + units_before(N_GATE) + j + 1)
                if j >= 2:
                    act.wait_ge(gate_out[k], 64 * ch + 16 * (j // 2))
                else:
                    act.wait_ge(gate_out[k], 64 * ch)
                A.activation(gate_st[:, k, :], slot(k), ACT.Sigmoid,
                             bias=cols_a[:, bass.ds(8 * ch + (at_a["b_gate"] + j), 1)]).then_inc(s["gate_read"], 1)
                act.wait_ge(s["gate_read"], 8 * ch + j + 1)
                act.dma_start(gates_d[bass.ds(8 * ch + j, 1)].rearrange("a p t -> p (a t)"), gate_st[:, k, :])\
                   .then_inc(gate_out[k], 16)

            with act.Fori(0, 2) as ch:
                for t in range(4):
                    act.wait_ge(s["bct_done"], 4 * ch + t + 1)
                    A.activation(bct[:, t % 2].rearrange("p m n -> p (m n)"), slot(2)[:, 0:4 * P], ACT.Copy)\
                     .then_inc(s["bct_copied"], 1)
                    for u in range(2):
                        gate(ch, 2 * t + u)
                act.wait_ge(s["y_read"], ch + 1)
                y = yg[:, bass.ds(ch, 1), :].rearrange("p a n -> p (a n)")
                A.activation(y, y, ACT.Gelu_apprx_tanh).then_inc(s["yg_ready"], 1)
            act.wait_ge(s["yg_ready"], 2)
            with act.Fori(0, 4) as i:
                for b in range(2):
                    act.wait_ge(s["gemm"], 2 * i + units_before(N_QKV) + b + 1)
                    A.activation(qk[:, bass.ds(2 * i + b, 1), :].rearrange("p a n -> p (a n)"), slot(b), ACT.Copy)\
                     .then_inc(s["qkv_read"], 1)
            for b in range(2):
                for h in range(2):
                    act.wait_ge(s["gemm"], units_before(N_QKV + 4 + b) + h + 1)
                    A.activation(v_tok[:, 4 * h:4 * h + 4, NB * b:NB * b + NB],
                                 slot(h).rearrange("p (t n) -> p t n", t=4), ACT.Copy).then_inc(s["qkv_read"], 1)
            for k in range(2):
                act.wait_ge(gate_out[k], 16 * KD)
                act.wait_ge(s["glu_done"], k + 1)
                A.activation(gate_st[:, k, :], slot(2 + k), ACT.Sigmoid, bias=col_a("b_glu", k)).then_inc(s["sig_ready"], 1)

            def softmax(p, t):
                n = (tiles[t % NT][1] + 1) * P
                act.wait_ge(s["sm_ready"], NT * p + t + 1)
                if t >= 3:
                    act.wait_ge(s["o_ready"], NT * p + t - 3)
                elif t == 2:
                    act.wait_ge(s["o_ready"], NT * p)
                A.activation(prob[:, t % 4, 0:n], prob[:, t % 4, 0:n], ACT.Exp, scale=-1.0,
                             bias=neg_max[:, t % 4:t % 4 + 1], accum_out=den[:, t % 4:t % 4 + 1])\
                 .then_inc(s["p_ready"], 1)

            def far_half(p, t):
                n = (tiles[t % NT][1] + 1) * P
                act.wait_ge(s["pt1"], QB * p + t // 2 + 1)
                if t:
                    act.wait_ge(s["pv"], NT * p + t - 1)
                A.activation(prob_t[:, t % 2, HALF:n], slot(2)[:, HALF:n], ACT.Copy).then_inc(s["ptc1"], 1)

            def heads(p, last):
                for t in range(NT):
                    if t + 2 < NT or not last:
                        softmax(p, t + 2)
                    if t % 2 and (t + 1 < NT or not last):
                        far_half(p, t + 1)

            softmax(0, 0)
            softmax(0, 1)
            far_half(0, 0)
            with act.Fori(0, HEADS // 2 - 1) as p:
                heads(p, False)
            heads(HEADS // 2 - 1, True)

            act.wait_ge(s["o_ready"], HEADS * QB)
            for o in range(2):
                act.wait_ge(s["y_gated"], o + 1)
                A.activation(ys_h[:, o, :], yg[:, o, :], ACT.Copy).then_inc(s["ysh"], 1)
            for c in range(KA):
                act.wait_ge(s["otr"], c + 1)
                A.activation(in2_h[:, c, :], slot(c), ACT.Copy).then_inc(s["oh_ready"], 1)
            with act.Fori(0, 2) as i:
                for c in range(4):
                    act.wait_ge(s["mix_ready"], 4 * i + c + 1)
                    A.activation(act_h[:, bass.ds(4 * i + c, 1), :].rearrange("p a n -> p (a n)"), mix[:, 0, :], ACT.Copy)\
                     .then_inc(s["mh_ready"], 1)
            squares(1, s["out_read"], 0)
            norm(1, lambda c: gain[:, 1, c:c + 1], lambda c: mod[:, 3 * KD + c:3 * KD + c + 1])

            base_f = units_before(N_FFN)
            with act.Fori(0, 4) as q:
                for p in range(2):
                    for cg in range(2):
                        c = 2 * p + cg
                        act.wait_ge(s["gemm"], 16 * q + base_f + 4 * p + cg + 1)
                        if p:
                            act.wait_ge(s["f_ready"], 4 * q + cg + 1)
                        else:
                            act.wait_ge(s["f_ready"], 4 * q)
                        A.activation(conv[:, cg, :], slot(cg), ACT.Identity,
                                     scale=cols_b[:, bass.ds(4 * q + (at_b["w_conv"] + c), 1)],
                                     bias=cols_a[:, bass.ds(4 * q + (at_a["b_conv"] + c), 1)]).then_inc(s["acc_ready"], 1)
                    for cg in range(2):
                        c = 2 * p + cg
                        act.wait_ge(s["a_read"], 4 * q + c + 1)
                        A.activation(conv[:, cg, :], conv[:, cg, :], ACT.Silu).then_inc(s["silu_ready"], 1)
                    for cg in range(2):
                        c = 2 * p + cg
                        act.wait_ge(s["v_read"], 4 * q + c + 1)
                        A.activation(in2_h[:, c, :], ffn[:], ACT.Copy).then_inc(s["fh_ready"], 1)

            squares(2, s["down_read"], 24)
            squares(3, s["x2_ready"], 0)
            act.dma_start(x2_d.rearrange("c p t -> p c t"), h_t[:]).then_inc(s["x2_out"], 16)
            norm(2, lambda c: col_b("norm_g_2", c), None)

            act.wait_ge(s["x2_out"], 16)
            for b in range(2):
                for h in range(2):
                    act.wait_ge(s["gemm"], units_before(N_V2 + b) + h + 1)
                    A.activation(vg[:, 4 * h:4 * h + 4, NB * b:NB * b + NB],
                                 slot(2 * b + h).rearrange("p (t n) -> p t n", t=4), ACT.Gelu_apprx_tanh)\
                     .then_inc(s["v2_read"], 1)
            act.wait_ge(s["ln_var"], 1)
            A.activation(ln_rstd[:], ln_rstd[:], ACT.Sqrt).then_inc(s["ln_std"], 1)
            base_a = units_before(N_A)
            for p in range(2):
                for cg in range(2):
                    act.wait_ge(s["gemm"], base_a + 4 * p + cg + 1)
                    if p:
                        act.wait_ge(s["ap_ready"], cg + 1)
                    A.activation(a_u[:, cg, :], slot(cg), ACT.Gelu_apprx_tanh).then_inc(s["au_read"], 1)
                for cg in range(2):
                    act.wait_ge(s["gemm"], base_a + 4 * p + 2 + cg + 1)
                    A.activation(a_z[:, cg, :], slot(cg), ACT.Silu).then_inc(s["az_read"], 1)
                for cg in range(2):
                    c = 2 * p + cg
                    act.wait_ge(s["ap_ready"], c + 1)
                    A.activation(in2_h[:, c, :], a_s[:], ACT.Copy).then_inc(s["ah_ready"], 1)

            def gates2(n0, done, ready):
                with act.Fori(0, 4) as j:
                    for cg in range(2):
                        act.wait_ge(s["gemm"], 4 * j + units_before(n0) + cg + 1)
                        act.wait_ge(done, 2 * j)
                        A.activation(br[:, cg, :], slot(cg), ACT.Sigmoid).then_inc(ready, 1)

            act.wait_ge(s["a_ready"], K2)
            gates2(N_GA, s["pa_read"], s["sa_ready"])
            act.wait_ge(s["pa_read"], KD)
            base_b = units_before(N_B)
            for p in range(2):
                for cg in range(2):
                    act.wait_ge(s["gemm"], base_b + 8 * p + cg + 1)
                    if p:
                        act.wait_ge(s["b_ready"], cg + 1)
                    A.activation(br[:, cg, :], slot(cg), ACT.Copy).then_inc(s["xb_read"], 1)
                for cg in range(2):
                    c = 2 * p + cg
                    act.wait_ge(s["gemm"], base_b + 8 * p + 6 + cg + 1)
                    act.wait_ge(s["bg_read"], c + 1)
                    A.activation(br2[:], slot(2 + cg), ACT.Silu).then_inc(s["bz_read"], 1)
                    act.wait_ge(s["bp_ready"], c + 1)
                    A.activation(in2_h[:, c, :], br[:, cg, :], ACT.Copy).then_inc(s["bh_ready"], 1)
            act.wait_ge(s["b_ready"], K2)
            gates2(N_GB, s["mb_ready"], s["sb_ready"])
            act.wait_ge(s["mb_ready"], KD)
            base_c = units_before(N_C)
            for p in range(2):
                for cg in range(2):
                    c = 2 * p + cg
                    act.wait_ge(s["gemm"], base_c + 4 * p + cg + 1)
                    if cg:
                        act.wait_ge(s["pooled"], c)
                    elif p:
                        act.wait_ge(s["ch_done"], 2)
                    A.activation(br[:, 0, :], slot(cg), ACT.Copy).then_inc(s["xc_read"], 1)
                for cg in range(2):
                    c = 2 * p + cg
                    act.wait_ge(s["gemm"], base_c + 4 * p + 2 + cg + 1)
                    act.wait_ge(s["pooled"], 2 * p + 2)
                    if cg:
                        act.wait_ge(s["pool_done"], 2 * p + 1)
                    A.activation(br[:, cg, :], slot(2 + cg), ACT.Silu).then_inc(s["cz_read"], 1)
                for cg in range(2):
                    c = 2 * p + cg
                    act.wait_ge(s["cp_ready"], c + 1)
                    A.activation(in2_h[:, c, :], br[:, cg, :], ACT.Copy).then_inc(s["ch_ready"], 1)
            act.wait_ge(s["ch_done"], K2)
            gates2(N_GC, s["mc_ready"], s["sc_ready"])
            act.wait_ge(s["mc_ready"], KD)
            for c in range(KD):
                A.activation(act_h[:, c, :], merged[:, c, :], ACT.Copy).then_inc(s["m2_high"], 1)
            for t in range(QB):
                act.wait_ge(s["otr2"], t + 1)
                step(A.activation(o_sq[:], slot(t % 4), ACT.Square, accum_out=o_ssq[:, 0, t:t + 1]))
                A.activation(o_ssq[:, 1, t:t + 1], o_ssq[:, 0, t:t + 1], ACT.Sqrt, scale=1.0 / D, bias=eps_rms[:])\
                 .then_inc(s["ostd"], 1)

        @block.vector
        def _(dve):
            v = nc.vector
            step = Steps(dve, s["dve"])

            dve.wait_ge(s["colt"], 1)
            step(v.tensor_copy(cols_a[:], slot(0)[:, 0:P]))
            v.tensor_copy(cols_b[:, 0:n_b], slot(0)[:, P:P + n_b]).then_inc(s["colt_read"], 1)

            dve.wait_ge(s["s5_in"], 16 * 9)
            ldt, dt, lrdt, ang, abr, abi, nr, den_, rcp, fr, fi, t0, t1 = (par[:, i, :] for i in range(13))
            a_re, a_im = col_a("a_re", 0, 8), col_a("a_im", 0, 8)
            angles, turns, rest, comp = (prep[:, i, :, :] for i in range(4))
            dve.wait_ge(s["dt_ready"], 1)
            v.tensor_tensor(lrdt, a_re, dt, ALU.mult).then_inc(s["lrdt_ready"], 1)
            step(v.tensor_tensor(ang, a_im, dt, ALU.mult))
            for j in range(LOGT):
                step(v.tensor_scalar(angles[:, :, j], ang, float(2**j), None, ALU.mult))
            step(v.tensor_scalar(turns, angles, 1 / (2 * np.pi), ROUND, ALU.mult, ALU.add))
            step(v.tensor_scalar(turns, turns, ROUND, None, ALU.subtract))
            step(v.scalar_tensor_tensor(rest, turns, -TWO_PI_PARTS[0], angles, ALU.mult, ALU.add))
            for part in TWO_PI_PARTS[1:]:
                step(v.scalar_tensor_tensor(rest, turns, -part, rest, ALU.mult, ALU.add))
            step(v.tensor_scalar(rest, rest, 3.1415925, -3.1415925, ALU.min, ALU.max))
            step(v.scalar_tensor_tensor(comp, rest, -1.0, rest, ALU.mult, ALU.min))
            v.tensor_scalar(comp, comp, np.pi / 2, None, ALU.add).then_inc(s["angle_ready"], 1)
            dve.wait_ge(s["turn_ready"], 1)
            cos1, sin1 = turn[:, 0, :, 0], turn[:, 1, :, 0]
            step(v.tensor_tensor(abr, mag[:], cos1, ALU.mult))
            step(v.tensor_tensor(abi, mag[:], sin1, ALU.mult))
            step(v.tensor_scalar(nr, abr, 1.0, None, ALU.subtract))
            step(v.tensor_tensor(den_, a_re, a_re, ALU.mult))
            step(v.tensor_tensor(t0, a_im, a_im, ALU.mult))
            step(v.tensor_tensor(den_, den_, t0, ALU.add))
            step(v.reciprocal(rcp, den_))
            for dst, x, y, op in ((fr, nr, abi, ALU.add), (fi, abi, nr, ALU.subtract)):
                step(v.tensor_tensor(t0, x, a_re, ALU.mult))
                step(v.tensor_tensor(t1, y, a_im, ALU.mult))
                step(v.tensor_tensor(t0, t0, t1, op))
                step(v.tensor_tensor(dst, t0, rcp, ALU.mult))

            def per_state(x):
                return x.unsqueeze(2).to_broadcast([P, STILES, GCH])

            tb = prep2
            for m, (x, y, op) in enumerate(((0, 1, ALU.subtract), (1, 0, ALU.add))):
                step(v.tensor_tensor(bb[:, m], b_in[:, x], per_state(fr), ALU.mult))
                step(v.tensor_tensor(tb[:], b_in[:, y], per_state(fi), ALU.mult))
                step(v.tensor_tensor(bb[:, m], bb[:, m], tb[:], op))

            for c in range(KD):
                dve.wait_ge(s["tr"], c + 1)
                v.tensor_copy(h_t[:, c, :], slot(c % 4)).then_inc(s["h_ready"], 1)

            def modulation(lo, hi, src):
                return v.tensor_tensor(mod[:, lo:hi], src, col_a("b_ada", lo, hi - lo), ALU.add)

            dve.wait_ge(s["ada_done"], N_ADA_EARLY)
            modulation(0, 2 * N_ADA_EARLY, slot(2)[:, 0:2 * N_ADA_EARLY]).then_inc(s["mod_read"], 1)
            dve.wait_ge(s["mod_read"], 1)
            v.scalar_tensor_tensor(gain[:, 0], mod[:, KD:2 * KD], 1.0, col_a("g_mix", 0, KD), ALU.add, ALU.mult)\
             .then_inc(s["mod_ready"], 1)

            def norm(k, nu):
                dve.wait_ge(s["std_ready"], k + 1)
                v.reciprocal(rstd[:], rstd[:]).then_inc(s["rstd_ready"], 1)
                dve.wait_ge(s["rstd_ready"], k + 1)

                def scaled(c):
                    v.tensor_tensor(sq[:, c % 2, :], h_t[:, c, :], rstd[:], ALU.mult).then_inc(s["t_ready"], 1)

                scaled(0)
                scaled(1)
                for c in range(KD):
                    dve.wait_ge(s["hi_ready"], KD * nu + c + 1)
                    v.tensor_tensor(act_l[:, c, :], nrm[:, c % 2, :], act_h[:, c, :].bitcast(F32), ALU.subtract)\
                     .then_inc(s["u_ready"], 1)
                    if c + 2 < KD:
                        scaled(c + 2)

            norm(0, 0)

            dve.wait_ge(s["h_out"], 16)
            dve.wait_ge(s["u_ready"], KD)
            for cg in range(2):
                dve.wait_ge(s["gemm"], cg + 1)
                v.tensor_copy(us[:, cg, :], slot(cg)).then_inc(s["us_ready"], 1)
            dve.wait_ge(s["us_ready"], 2)

            cs, sn, wa, wb, wd, we, xre, xim = (s5[:, i, :] for i in range(8))
            with step.loop(2, 227) as ch:
                for m in range(2):
                    step(v.tensor_copy(cur[:, m], turn[:, m, bass.ds(4 * ch, 4), :]))
                step(v.tensor_copy(cmag[:], mag[:, bass.ds(4 * ch, 4)]))
                for t in range(4):
                    if t:
                        dve.wait_ge(s["bct_done"], 4 * ch + t)
                    else:
                        dve.wait_ge(s["bct_done"], 4 * ch)
                    for m in range(2):
                        rep = bb[:, m, bass.ds(4 * ch + t, 1), :].to_broadcast([P, P // GCH, GCH])
                        step(v.tensor_tensor(bc[:, m, :].rearrange("p (a c) -> p a c", c=GCH),
                                             mask_b[:, t, :].rearrange("p (a c) -> p a c", c=GCH), rep, ALU.mult))
                    rep = cc[:, 0, bass.ds(ch, 1), :].to_broadcast([P, 2, NSTATE])
                    step(v.tensor_tensor(bc[:, 2, :].rearrange("p (a n) -> p a n", a=2),
                                         mask_c[:, t, :].rearrange("p (a n) -> p a n", a=2), rep, ALU.mult))
                    rep = cc[:, 1, bass.ds(ch, 1), :].to_broadcast([P, 2, NSTATE])
                    v.scalar_tensor_tensor(bc[:, 3, :].rearrange("p (a n) -> p a n", a=2), rep, -1.0,
                                           mask_c[:, t, :].rearrange("p (a n) -> p a n", a=2), ALU.mult, ALU.mult)\
                     .then_inc(s["bc_ready"], 1)
                    step(v.memset(cs[:, 0:1], 1.0))
                    step(v.memset(sn[:, 0:1], 0.0))
                    for j in range(LOGT):
                        n = 2**j
                        c1, s1 = cur[:, 0, t, j:j + 1], cur[:, 1, t, j:j + 1]
                        step(v.tensor_scalar(wa[:, 0:n], sn[:, 0:n], s1, None, ALU.mult))
                        step(v.tensor_scalar(wb[:, 0:n], cs[:, 0:n], s1, None, ALU.mult))
                        step(v.scalar_tensor_tensor(cs[:, n:2 * n], cs[:, 0:n], c1, wa[:, 0:n], ALU.mult, ALU.subtract))
                        step(v.scalar_tensor_tensor(sn[:, n:2 * n], sn[:, 0:n], c1, wb[:, 0:n], ALU.mult, ALU.add))
                    dve.wait_ge(s["bu_ready"], 8 * ch + 2 * t + 1)
                    step(v.tensor_tensor(wa, cs, slot(2), ALU.mult))
                    v.tensor_tensor(wb, sn, slot(2), ALU.mult).then_inc(s["bu_read"], 1)
                    dve.wait_ge(s["bu_ready"], 8 * ch + 2 * t + 2)
                    step(v.tensor_tensor(wd, sn, slot(2), ALU.mult))
                    v.tensor_tensor(we, cs, slot(2), ALU.mult).then_inc(s["bu_read"], 1)
                    dve.wait_ge(s["bu_read"], 8 * ch + 2 * t + 2)
                    step(v.tensor_tensor(wa, wa, wd, ALU.add))
                    step(v.tensor_tensor(we, we, wb, ALU.subtract))
                    decay = cmag[:, t:t + 1].to_broadcast([P, T])
                    step(v.tensor_tensor_scan(wd, decay, wa, 0.0, ALU.mult, ALU.add))
                    step(v.tensor_tensor_scan(wb, decay, we, 0.0, ALU.mult, ALU.add))
                    step(v.tensor_tensor(wa, cs, wd, ALU.mult))
                    step(v.tensor_tensor(we, sn, wb, ALU.mult))
                    if t:
                        dve.wait_ge(s["y_done"], 4 * ch + t)
                    else:
                        dve.wait_ge(s["y_done"], 4 * ch)
                    step(v.tensor_tensor(xre, wa, we, ALU.subtract))
                    step(v.tensor_tensor(wa, sn, wd, ALU.mult))
                    step(v.tensor_tensor(we, cs, wb, ALU.mult))
                    v.tensor_tensor(xim, wa, we, ALU.add).then_inc(s["x_ready"], 1)
                    dve.wait_ge(s["x_ready"], 4 * ch + t + 1)
                dve.wait_ge(s["y_done"], 4 * ch + 4)
                one = us[:, bass.ds(ch, 1), :].rearrange("p a n -> p (a n)")
                dst = yg[:, bass.ds(ch, 1), :].rearrange("p a n -> p (a n)")
                v.scalar_tensor_tensor(dst, one, cols_a[:, bass.ds(ch + at_a["d_skip"], 1)], slot(3), ALU.mult, ALU.add)\
                 .then_inc(s["y_read"], 1)
            for o in range(2):
                dve.wait_ge(s["sig_ready"], 2)
                v.tensor_tensor(yg[:, o, :], yg[:, o, :], gate_st[:, o, :], ALU.mult).then_inc(s["y_gated"], 1)

            dve.wait_ge(s["attn_in"], 32)
            dve.wait_ge(s["qkv_read"], 12)

            def head_bias(e):
                step(v.scalar_tensor_tensor(bias[:, e, :], delta[:], -4.0, log8[:], ALU.mult, ALU.add))
                step(v.tensor_scalar(delta[:], delta[:], 0.5, None, ALU.mult))

            def smallest(p, t):
                e, qb = tiles[t % NT]
                n = (qb + 1) * P
                dve.wait_ge(s["s_ready"], NT * p + t + 1)
                if t >= 3:
                    if t % 2:
                        dve.wait_ge(s["pt0"], NT * p + t - 3)
                    else:
                        dve.wait_ge(s["pt1"], QB * p + (t - 4) // 2 + 1)
                dve.sem_inc(s["passed"], 1)
                v.tensor_tensor_reduce(out=prob[:, t % 4, 0:n], in0=slot(t % 2)[:, 0:n],
                                       in1=bias[:, e, T - n:T], scale=-0.125, scalar=3e38,
                                       op0=ALU.add, op1=ALU.min,
                                       accum_out=neg_max[:, t % 4:t % 4 + 1]).then_inc(s["sm_ready"], 1)

            def near_half(p, t):
                n = min(tiles[t % NT][1] + 1, 4) * P
                dve.wait_ge(s["pt0"], NT * p + t + 1)
                if t >= 2:
                    dve.wait_ge(s["pv"], NT * p + t - 1)
                elif t:
                    dve.wait_ge(s["pv"], NT * p)
                v.tensor_copy(prob_t[:, t % 2, 0:n], slot(2)[:, 0:n]).then_inc(s["ptc0"], 1)

            def normalised(p, t):
                e, qb = tiles[t]
                dve.wait_ge(s["pv"], NT * p + t + 1)
                step(v.reciprocal(rden[:, t % 4:t % 4 + 1], den[:, t % 4:t % 4 + 1]))
                src = slot(3)[:, HALF * (t % 2):HALF * (t % 2) + HALF]
                if t % 4 == 3:
                    lo = 2 * N_ADA_EARLY + 2 * (t // 4)
                    dve.wait_ge(s["ada_done"], 4 * p + N_ADA_EARLY + t // 4 + 1)
                    v.tensor_tensor(mod[:, bass.ds(8 * p + lo, 2)], src[:, HD:HD + 2],
                                    cols_a[:, bass.ds(8 * p + lo + at_a["b_ada"], 2)], ALU.add)\
                     .then_inc(s["mod2_ready"], 1)
                v.tensor_scalar(o_tok[:, qb, bass.ds(P * p + HD * e, HD)], src[:, 0:HD],
                                rden[:, t % 4:t % 4 + 1], None, ALU.mult).then_inc(s["o_ready"], 1)

            def heads(p, last):
                for t in range(NT):
                    if t == 1:
                        dve.wait_ge(s["sm_ready"], NT * p)
                        head_bias(1)
                    if t == QB + 1 and not last:
                        dve.wait_ge(s["sm_ready"], NT * p + QB)
                        head_bias(0)
                    if t + 3 < NT or not last:
                        smallest(p, t + 3)
                    if t + 1 < NT or not last:
                        near_half(p, t + 1)
                    normalised(p, t)

            head_bias(0)
            for t in range(3):
                smallest(0, t)
            near_half(0, 0)
            with step.loop(HEADS // 2 - 1, 4 + NT) as p:
                heads(p, False)
            heads(HEADS // 2 - 1, True)
            dve.wait_ge(s["mod2_ready"], 16)
            v.scalar_tensor_tensor(gain[:, 1], mod[:, 4 * KD:5 * KD], 1.0, col_a("g_ffn", 0, KD), ALU.add, ALU.mult)\
             .then_inc(s["mod_ready"], 1)

            for o in range(2):
                dve.wait_ge(s["ysh"], o + 1)
                v.tensor_tensor(ys_l[:, o, :], yg[:, o, :], ys_h[:, o, :].bitcast(F32), ALU.subtract).then_inc(s["ys_ready"], 1)
            for c in range(KA):
                dve.wait_ge(s["oh_ready"], c + 1)
                v.tensor_tensor(in2_l[:, c, :], slot(c), in2_h[:, c, :].bitcast(F32), ALU.subtract).then_inc(s["ot_ready"], 1)

            dve.wait_ge(s["ys_ready"], 2)
            with step.loop(2, 4) as i:
                for b in range(2):
                    for cg in range(2):
                        c = 2 * b + cg
                        dve.wait_ge(gate_back[cg], 64 * i + 32 * (b + 1))
                        dve.wait_ge(s["gemm"], 8 * i + units_before(N_PROJ) + 4 * b + 2 * cg + 2)
                        step(v.tensor_tensor(mix[:, 0, :], slot(2 * cg), gate_in[:, cg, 0, :], ALU.mult))
                        v.tensor_tensor(mix[:, 1, :], slot(2 * cg + 1), gate_in[:, cg, 1, :], ALU.mult)\
                         .then_inc(s["proj_read"], 1)
                        dve.wait_ge(s["proj_read"], 4 * i + c + 1)
                        v.tensor_tensor(mix[:, 0, :], mix[:, 0, :], mix[:, 1, :], ALU.add).then_inc(s["mix_ready"], 1)
                        dve.wait_ge(s["mh_ready"], 4 * i + c + 1)
                        v.tensor_tensor(act_l[:, bass.ds(4 * i + c, 1), :].rearrange("p a n -> p (a n)"), mix[:, 0, :],
                                        act_h[:, bass.ds(4 * i + c, 1), :].rearrange("p a n -> p (a n)").bitcast(F32),
                                        ALU.subtract).then_inc(s["merged_ready"], 1)
                        dve.wait_ge(s["merged_ready"], 4 * i + c + 1)

            for c in range(KD):
                dve.wait_ge(h_back[c], 16)
                dve.wait_ge(s["gemm"], units_before(N_OUT) + c + 1)
                v.scalar_tensor_tensor(h_t[:, c, :], slot(c % 4), mod[:, 2 * KD + c:2 * KD + c + 1], h_t[:, c, :],
                                       ALU.mult, ALU.add).then_inc(s["out_read"], 1)
            dve.wait_ge(s["out_read"], KD)
            norm(1, 1)

            base_f = units_before(N_FFN)
            with step.loop(4, 4) as q:
                for p in range(2):
                    for cg in range(2):
                        c = 2 * p + cg
                        dve.wait_ge(s["acc_ready"], 4 * q + c + 1)
                        for j in range(1, CONV):
                            ins = v.scalar_tensor_tensor(
                                conv[:, cg, j:T], slot(cg)[:, 0:T - j],
                                cols_b[:, bass.ds(4 * q + (at_b["w_conv"] + j * (FF // P) + c), 1)],
                                conv[:, cg, j:T], ALU.mult, ALU.add)
                            if j < CONV - 1:
                                step(ins)
                            else:
                                ins.then_inc(s["a_read"], 1)
                    for cg in range(2):
                        c = 2 * p + cg
                        dve.wait_ge(s["silu_ready"], 4 * q + c + 1)
                        dve.wait_ge(s["gemm"], 16 * q + base_f + 4 * p + 2 + cg + 1)
                        if c:
                            dve.wait_ge(s["f_ready"], 4 * q + c)
                        else:
                            dve.wait_ge(s["f_ready"], 4 * q)
                        v.tensor_tensor(ffn[:], slot(2 + cg), conv[:, cg, :], ALU.mult).then_inc(s["v_read"], 1)
                        dve.wait_ge(s["fh_ready"], 4 * q + c + 1)
                        v.tensor_tensor(in2_l[:, c, :], ffn[:], in2_h[:, c, :].bitcast(F32), ALU.subtract)\
                         .then_inc(s["f_ready"], 1)
                for u in range(KD):
                    dve.wait_ge(s["gemm"], 16 * q + base_f + 8 + u + 1)
                    if u == 0:
                        dve.wait_ge(s["down_read"], 8 * q)
                    v.scalar_tensor_tensor(h_t[:, u, :], slot(u % 4), mod[:, 5 * KD + u:5 * KD + u + 1], h_t[:, u, :],
                                           ALU.mult, ALU.add).then_inc(s["down_read"], 1)

            dve.wait_ge(s["down_read"], 32)
            dve.wait_ge(s["std_ready"], 3)
            v.reciprocal(rstd[:], rstd[:]).then_inc(s["rstd_ready"], 1)
            dve.wait_ge(s["rstd_ready"], 3)
            for c in range(KD):
                v.scalar_tensor_tensor(h_t[:, c, :], h_t[:, c, :], col_b("g_final", c), rstd[:], ALU.mult, ALU.mult)\
                 .then_inc(s["x2_ready"], 1)
            dve.wait_ge(s["x2_ready"], KD)
            dve.wait_ge(s["wst_done"], 1)
            v.tensor_copy(wst[:].rearrange("p g t -> p (g t)"), slot(0)).then_inc(s["wst_ready"], 1)
            norm(3, 2)

            dve.wait_ge(s["v2_read"], 4)
            for t in range(QB):
                step(v.bn_stats(bn[:, t, :], vg[:, t, :]))
                step(v.bn_aggr(bn_mv[:, t, :], bn[:, t, :]))
            v.tensor_scalar(ln_rstd[:], bn_mv[:, :, 1], LN_EPS, None, ALU.add).then_inc(s["ln_var"], 1)
            dve.wait_ge(s["ln_std"], 1)
            step(v.reciprocal(ln_rstd[:], ln_rstd[:]))
            dve.wait_ge(s["late_in"], 16 * 13)
            for t in range(QB):
                step(v.tensor_scalar(vg[:, t, :], vg[:, t, :], bn_mv[:, t, 0:1], ln_rstd[:, t:t + 1],
                                     ALU.subtract, ALU.mult))
                step(v.tensor_tensor(vg[:, t, :], vg[:, t, :], ln_g[:], ALU.mult))
                ins = v.tensor_tensor(vg[:, t, :], vg[:, t, :], ln_b[:], ALU.add)
                if t < QB - 1:
                    step(ins)
                else:
                    ins.then_inc(s["vn_ready"], 1)

            for c in range(K2):
                cg = c % 2
                dve.wait_ge(s["sg_done"], c + 1)
                if c:
                    dve.wait_ge(s["a_ready"], c)
                v.tensor_tensor(a_s[:].rearrange("p (n t) -> p n t", t=P), slot(2 + cg).rearrange("p (n t) -> p n t", t=P),
                                bs_row[:, c:c + 1, :].to_broadcast([P, QB, P]), ALU.add).then_inc(s["sg_read"], 1)
                dve.wait_ge(s["sg_read"], c + 1)
                dve.wait_ge(s["au_read"], c + 1)
                step(v.tensor_tensor(a_s[:], a_s[:], a_u[:, cg, :], ALU.mult))
                dve.wait_ge(s["az_read"], c + 1)
                v.tensor_tensor(a_s[:], a_s[:], a_z[:, cg, :], ALU.mult).then_inc(s["ap_ready"], 1)
                dve.wait_ge(s["ah_ready"], c + 1)
                v.tensor_tensor(in2_l[:, c, :], a_s[:], in2_h[:, c, :].bitcast(F32), ALU.subtract).then_inc(s["a_ready"], 1)

            def gated(n0, sig, p_read, done, add):
                with step.loop(4, 0) as j:
                    for cg in range(2):
                        m = merged[:, bass.ds(2 * j + cg, 1), :].rearrange("p a n -> p (a n)")
                        dve.wait_ge(sig, 2 * j + cg + 1)
                        dve.wait_ge(s["gemm"], 4 * j + units_before(n0 + 1) + cg + 1)
                        if not add:
                            v.tensor_tensor(m, br[:, cg, :], slot(2 + cg), ALU.mult).then_inc(p_read, 1)
                            continue
                        v.tensor_tensor(br[:, cg, :], br[:, cg, :], slot(2 + cg), ALU.mult).then_inc(p_read, 1)
                        dve.wait_ge(p_read, 2 * j + cg + 1)
                        v.tensor_tensor(m, m, br[:, cg, :], ALU.add).then_inc(done, 1)

            dve.wait_ge(s["x2_out"], 16)
            dve.wait_ge(s["a_ready"], K2)
            gated(N_GA, s["sa_ready"], s["pa_read"], None, False)

            base_b = units_before(N_B)
            for p in range(2):
                for cg in range(2):
                    dve.wait_ge(s["xb_read"], 2 * p + cg + 1)
                    dve.wait_ge(s["gemm"], base_b + 8 * p + 2 + cg + 1)
                    v.tensor_tensor(br[:, cg, :], br[:, cg, :], slot(2 + cg), ALU.mult).then_inc(s["bc_read"], 1)
                for cg in range(2):
                    c = 2 * p + cg
                    y, acc = br[:, cg, :], br2

                    def tap(j, c=c):
                        return col_b("conv_w_2", j * K2 + c)

                    dve.wait_ge(s["bc_read"], c + 1)
                    if c:
                        dve.wait_ge(s["b_ready"], c)
                    step(v.tensor_scalar(acc[:], y, tap(2), col_a("conv_b_2", c), ALU.mult, ALU.add))
                    step(v.scalar_tensor_tensor(acc[:, 1:T], y[:, 0:T - 1], tap(1), acc[:, 1:T], ALU.mult, ALU.add))
                    step(v.scalar_tensor_tensor(acc[:, 2:T], y[:, 0:T - 2], tap(0), acc[:, 2:T], ALU.mult, ALU.add))
                    dve.wait_ge(s["gemm"], base_b + 8 * p + 4 + cg + 1)
                    v.tensor_tensor(y, acc[:], slot(cg), ALU.mult).then_inc(s["bg_read"], 1)
                    dve.wait_ge(s["bg_read"], c + 1)
                    dve.wait_ge(s["bz_read"], c + 1)
                    v.tensor_tensor(y, y, acc[:], ALU.mult).then_inc(s["bp_ready"], 1)
                    dve.wait_ge(s["bh_ready"], c + 1)
                    v.tensor_tensor(in2_l[:, c, :], y, in2_h[:, c, :].bitcast(F32), ALU.subtract).then_inc(s["b_ready"], 1)
            dve.wait_ge(s["pa_read"], KD)
            dve.wait_ge(s["b_ready"], K2)
            gated(N_GB, s["sb_ready"], s["pb_read"], s["mb_ready"], True)

            for p in range(2):
                for cg in range(2):
                    c = 2 * p + cg
                    x, other = br[:, 0, :], br2
                    dve.wait_ge(s["xc_read"], c + 1)
                    if c >= 2:
                        dve.wait_ge(s["pool_done"], c)
                    src, dst = x, other[:]
                    for j in range(c + 1):
                        h = 2**j
                        step(v.tensor_copy(dst[:, 0:h], src[:, 0:h]))
                        step(v.tensor_tensor(dst[:, h:T], src[:, h:T], src[:, 0:T - h], ALU.add))
                        src, dst = dst, src
                    res = pool_in[cg]
                    step(v.scalar_tensor_tensor(res[:, 16:T], src[:, 16:T], 1.0 / WINDOWS[c], slot(cg)[:, 16:T],
                                                ALU.mult, ALU.subtract))
                    step(v.tensor_tensor(src[:, 0:16], src[:, 0:16], inv[:, c, :], ALU.mult))
                    v.tensor_tensor(res[:, 0:16], src[:, 0:16], slot(cg)[:, 0:16], ALU.subtract).then_inc(s["pooled"], 1)
                    dve.wait_ge(s["pooled"], c + 1)
                for cg in range(2):
                    c = 2 * p + cg
                    z = br[:, cg, :]
                    dve.wait_ge(s["pool_done"], c + 1)
                    dve.wait_ge(s["cz_read"], c + 1)
                    v.scalar_tensor_tensor(z, slot(cg), col_b("pool_scale_2", c), z, ALU.mult, ALU.mult)\
                     .then_inc(s["cp_ready"], 1)
                    dve.wait_ge(s["ch_ready"], c + 1)
                    v.tensor_tensor(in2_l[:, c, :], z, in2_h[:, c, :].bitcast(F32), ALU.subtract).then_inc(s["ch_done"], 1)
            dve.wait_ge(s["mb_ready"], KD)
            dve.wait_ge(s["ch_done"], K2)
            gated(N_GC, s["sc_ready"], s["pc_read"], s["mc_ready"], True)
            for c in range(KD):
                dve.wait_ge(s["m2_high"], c + 1)
                v.tensor_tensor(act_l[:, c, :], merged[:, c, :], act_h[:, c, :].bitcast(F32), ALU.subtract)\
                 .then_inc(s["m2_ready"], 1)
            for c in range(KD):
                dve.wait_ge(x2_back[c], 16)
                dve.wait_ge(s["gemm"], units_before(N_WO) + c + 1)
                v.tensor_tensor(y_t[:, c, :], y_t[:, c, :], slot(c % 4), ALU.add).then_inc(s["y_ready"], 1)
            dve.wait_ge(s["g_row_in"], 16)
            for t in range(QB):
                dve.wait_ge(s["ostd"], t + 1)
                step(v.reciprocal(o_ssq[:, 2, t:t + 1], o_ssq[:, 1, t:t + 1]))
                if t >= 2:
                    dve.wait_ge(row_out[t % 2], 16 * (t // 2))
                v.scalar_tensor_tensor(o_row[:, t % 2, :], slot(t % 4), o_ssq[:, 2, t:t + 1], g_row[:],
                                       ALU.mult, ALU.mult).then_inc(s["orow"], 1)


def kernel(**inputs):
    import concourse.bacc as bacc
    from concourse.bass_utils import run_bass_kernel_spmd

    nc = bacc.Bacc("TRN2", target_bir_lowering=False, num_devices=1)
    arrays, aps = {}, {}
    for name, value in {**inputs, **constants()}.items():
        value = np.ascontiguousarray(value)
        arrays[f"in_{name}"] = value
        aps[name] = nc.dram_tensor(f"in_{name}", value.shape, mybir.dt.from_np(value.dtype), kind="ExternalInput").ap()
    out = nc.dram_tensor("out", (1, T, D), F32, kind="ExternalOutput").ap()
    build(nc, aps, out)
    return run_bass_kernel_spmd(nc, [arrays], core_ids=[0]).results[0]["out"]
```

```python
from contextlib import ExitStack, contextmanager

import numpy as np

import concourse.bass as bass
from concourse import mybir

ACT = mybir.ActivationFunctionType
ALU = mybir.AluOpType
F32 = mybir.dt.float32
F32R = mybir.dt.float32r

P = 128
T = 1024
D = 1024
KD = D // P
HALF = 512
NB = 256
HEADS, HD = 8, 64
ATT = HEADS * HD
KA = ATT // P
SSM = 256
GROUPS, GCH, NSTATE = 16, 16, 64
STILES = GROUPS * NSTATE // P
LOGT = 10
FF = 2048
CONV = 3
W2 = 512
K2 = W2 // P
QB = T // P
WINDOWS = (2, 4, 8, 16)
RMS_EPS, LN_EPS = 1e-6, 1e-5
TWO_PI_PARTS = (6.28125, 4058 / 2**21, 2 * np.pi - 6.28125 - 4058 / 2**21)
ROUND = 1.5 * 2**23
MASKED = -1e30

N_US, N_GATE, N_QKV, N_PROJ, N_OUT, N_FFN = 0, 1, 9, 15, 19, 23
N_V2, N_A, N_GA, N_B, N_GB, N_C, N_GC, N_WO, N_END = 55, 57, 61, 69, 77, 85, 89, 97, 101
N_ADA_EARLY, N_ADA = 8, 24


def units_before(n):
    return 2 * n if n <= N_PROJ else 30 + 4 * (n - N_PROJ) if n <= N_OUT else 2 * n + 8


ROWS_A = dict(b_ada=48, g_mix=8, b_gate=16, g_ffn=8, b_conv=16, c=8, a_re=8, a_im=8, d_skip=2, b_glu=2,
              conv_b_2=4)
ROWS_B = dict(w_conv=48, g_final=8, norm_g_2=8, conv_w_2=12, pool_scale_2=4)


def places(rows):
    at, out = 0, {}
    for name, n in rows.items():
        out[name] = at
        at += n
    return out, at


class Steps:

    def __init__(self, eng, sem):
        self.eng, self.sem, self.base, self.n = eng, sem, 0, 0

    def __call__(self, ins):
        ins.then_inc(self.sem, 1)
        self.n += 1
        self.eng.wait_ge(self.sem, self.base + self.n)

    @contextmanager
    def loop(self, trips, per):
        start = self.base + self.n
        with self.eng.Fori(0, trips) as i:
            self.base, self.n = i * per + start, 0
            yield i
            assert self.n == per, (self.n, per)
        self.base, self.n = start + trips * per, 0


def constants():
    p, x = np.arange(P)[:, None], np.arange(T)[None, :]
    delta = p + (T - P) - x
    count = ((delta >= 0) & (delta <= 128)).astype(np.float64)
    count += (delta >= 0) & (delta <= 512) & (delta % 4 == 0)
    count += (delta >= 0) & (delta <= 2048) & (delta % 16 == 0)
    log8 = np.where(count > 0, 8 * np.log(np.maximum(count, 1)), MASKED)
    ch, st = np.arange(P)[None, None, :], np.arange(P)[:, None, None]
    k = np.arange(4)[None, :, None]
    mask_b = (ch // GCH == 2 * k + st // NSTATE)
    mask_c = mask_b.transpose(2, 1, 0)
    inv = np.stack([1.0 / np.minimum(np.arange(1, 17), w) for w in WINDOWS])
    return dict(
        k_ident=np.eye(P, dtype=np.float32),
        k_delta=np.ascontiguousarray(delta, np.float32),
        k_log8=np.ascontiguousarray(log8, np.float32),
        k_mask_b=np.ascontiguousarray(mask_b, np.float32),
        k_mask_c=np.ascontiguousarray(mask_c, np.float32),
        k_inv=np.ascontiguousarray(np.broadcast_to(inv[None], (P, 4, 16)), np.float32),
    )


def build(nc, a, out):
    ctx = ExitStack()
    with ctx:
        base = -(-nc.sbuf_base // 32) * 32
        kib = 1024

        def at(name, shape, offset, dt=F32):
            return nc.alloc_sbuf_tensor_at(name, shape, dt, offset=base + offset)

        fence = ctx.enter_context(nc.sbuf_tensor("fence", [P, (nc.sbuf_top - base) // 4], F32))

        act_h = at("act_h", [P, KD, T], 0, F32R)
        act_l = at("act_l", [P, KD, T], 32 * kib, F32R)
        w_h = at("w_h", [P, 2, KD, NB], 64 * kib, F32R)
        w_l = at("w_l", [P, 2, KD, NB], 80 * kib, F32R)
        in2_h = at("in2_h", [P, 4, T], 96 * kib, F32R)
        in2_l = at("in2_l", [P, 4, T], 112 * kib, F32R)
        raw = at("raw", [P, 2, KD, NB], 128 * kib)

        CONST = 144 * kib
        spot = [CONST]

        def keep(name, shape, dt=F32):
            n = int(np.prod(shape[1:])) * 4
            t = at(name, shape, spot[0], dt)
            spot[0] += -(-n // 32) * 32
            return t

        ident = keep("ident", [P, P])
        ones = keep("ones", [P, P])
        cols_a = keep("cols_a", [P, P])
        cols_b = keep("cols_b", [P, P])
        mod = keep("mod", [P, 48])
        eps_rms = keep("eps_rms", [P, 1])
        gain = keep("gain", [P, 2, KD])
        c_act = keep("c_act", [P, KD])
        late = spot[0]
        mask_b = keep("mask_b", [P, 4, P])
        mask_c = keep("mask_c", [P, 4, P])
        bb = keep("bb", [P, 2, STILES, GCH])
        cc = keep("cc", [P, 2, 2, NSTATE])
        mag = keep("mag", [P, STILES])
        turn = keep("turn", [P, 2, STILES, LOGT])
        cur = keep("cur", [P, 2, 4, LOGT])
        cmag = keep("cmag", [P, 4])
        bct = keep("bct", [P, 2, 4, P])
        w_glu = keep("w_glu", [P, 2, SSM])
        assert spot[0] <= 160 * kib, spot[0] / kib
        spot[0] = late
        wst = keep("wst", [P, 8, P])
        ln_g = keep("ln_g", [P, W2])
        ln_b = keep("ln_b", [P, W2])
        bs_row = keep("bs_row", [P, K2, P])
        w_pool = keep("w_pool", [P, 4, P])
        inv = keep("inv", [P, 4, 16])
        bn = keep("bn", [P, QB, 6])
        bn_mv = keep("bn_mv", [P, QB, 2])
        ln_rstd = keep("ln_rstd", [P, QB])
        assert spot[0] <= 160 * kib, spot[0] / kib

        x_tok = at("x_tok", [P, QB, D], 96 * kib)
        rows = at("rows", [P, 2, P], 200 * kib)
        prep = at("prep", [P, 16, STILES, LOGT], 192 * kib)
        b_in = at("b_in", [P, 2, STILES, GCH], 201 * kib)
        prep2 = at("prep2", [P, STILES, GCH], 202 * kib + 512)
        par = at("par", [P, 13, STILES], 202 * kib)
        h_t = at("h_t", [P, KD, T], 160 * kib)
        ada_w = at("ada_w", [P, N_ADA_EARLY, KD, NB], 0)
        sq = at("sq", [P, 2, T], 192 * kib)
        diag = [at(f"diag{i}", [P, QB, P], (192 + 4 * i) * kib) for i in range(2)]
        acc = at("acc", [P, T], 203 * kib)
        acc2 = at("acc2", [P, 2, T], 56 * kib)
        stat = at("stat", [P, 6, QB], 207 * kib)
        gain2 = at("gain2", [P, KD], 207 * kib + 192)
        nrm = at("nrm", [P, 2, T], 104 * kib)
        rstd2 = at("rstd2", [P, 2, T], 112 * kib)
        qk = at("qk", [P, 2 * KA, T], 96 * kib)
        s5 = at("s5", [P, 8, T], 96 * kib)
        yg = at("yg", [P, 2, T], 160 * kib)
        v_tok = at("v_tok", [P, QB, ATT], 168 * kib)
        us = at("us", [P, 2, T], 184 * kib)
        gate_st = at("gate_st", [P, 2, T], 192 * kib)
        bc = at("bc", [P, 4, P], 200 * kib)
        o_tok = at("o_tok", [P, QB, ATT], 184 * kib)
        q2 = at("q2", [P, 2, T], 0, F32R)
        k_hh = at("k_hh", [P, 2, T], 8 * kib, F32R)
        k_ll = at("k_ll", [P, 2, T], 16 * kib, F32R)
        v_st = at("v_st", [P, 2, QB, HD], 24 * kib)
        prob = at("prob", [P, 4, T], 28 * kib)
        prob_t = at("prob_t", [P, 2, T], 44 * kib)
        bias = at("bias", [P, 2, T], 52 * kib)
        delta = at("delta", [P, T], 60 * kib)
        log8 = at("log8", [P, T], 64 * kib)
        neg_max = at("neg_max", [P, 4], 204 * kib)
        ada_part = at("ada_part", [P, 2, NB], 205 * kib)
        den = at("den", [P, 4], 204 * kib + 32)
        rden = at("rden", [P, 4], 204 * kib + 64)
        ys_h = at("ys_h", [P, 2, T], 168 * kib, F32R)
        ys_l = at("ys_l", [P, 2, T], 176 * kib, F32R)
        gate_in = at("gate_in", [P, 2, 2, T], 184 * kib)
        mix = at("mix", [P, 2, T], 160 * kib)
        conv = at("conv", [P, 2, T], 192 * kib)
        ffn = at("ffn", [P, T], 200 * kib)
        ws_tok = at("ws_tok", [P, T], 120 * kib)
        vg = at("vg", [P, QB, W2], 160 * kib)
        a_u = at("a_u", [P, 2, T], 176 * kib)
        a_z = at("a_z", [P, 2, T], 184 * kib)
        a_s = at("a_s", [P, T], 192 * kib)
        merged = at("merged", [P, KD, T], 160 * kib)
        br = at("br", [P, 2, T], 192 * kib)
        br2 = at("br2", [P, T], 200 * kib)
        pool_in = [br[:, 1, :], br2[:]]
        y_t = at("y_t", [P, KD, T], 160 * kib)
        o_row = at("o_row", [P, 2, D], 192 * kib)
        g_row = at("g_row", [P, D], 200 * kib)
        o_sq = at("o_sq", [P, D], 64 * kib)
        o_ssq = at("o_ssq", [P, 3, QB], 68 * kib)

        tiles = [(hh, qb) for hh in range(2) for long in range(QB - 1, QB // 2 - 1, -1) for qb in (long, QB - 1 - long)]
        NT = len(tiles)
        STAGED = 7

        ps = ctx.enter_context(nc.psum_tensor("ps", [P, 4, T], F32))

        gates_d = nc.dram_tensor("gates_scratch", [2 * KD, P, T], F32).ap()
        h_d = nc.dram_tensor("h_scratch", [KD, P, T], F32).ap()
        x2_d = nc.dram_tensor("x2_scratch", [KD, P, T], F32).ap()

        names = """vec_in const_in x_in late_in attn_in g_row_in dve act colt colt_read c_ready consts_ready tr
            h_ready h_out ada_done mod_ready mod_read sq_ready sq_used std_ready rstd_ready t_ready hi_ready
            u_ready w_high w_split gemm us_ready gate_read bc_ready bct_done bct_copied bu_ready bu_read
            x_ready y_done y_read yg_ready qkv_read glu_done sig_ready ys_ready staged s_ready sm_ready
            p_ready pt0 pt1 ptc0 ptc1 pv o_ready otr oh_ready ot_ready ysh proj_read mix_ready mh_ready
            merged_ready out_read acc_ready silu_ready a_read v_read fh_ready f_ready down_read x2_ready
            sums_ready ada_summed gate_half k0_ready ms2_ready diag_ready rstd2_ready wst_done wst_ready wst_masked v2_read vn_ready au_read sg_done sg_read az_read ap_ready
            ah_ready a_ready xb_read bc_read bz_read bg_read bp_ready bh_ready b_ready xc_read pooled
            pool_done cz_read cp_ready ch_ready sa_ready pa_read sb_ready pb_read mb_ready sc_ready pc_read
            mc_ready m2_high m2_ready s5_in dt_ready lrdt_ready angle_ready turn_ready mod2_ready passed
            ln_var ln_std ch_done y_gated y_ready otr2 ostd orow""".split()
        s = {n: ctx.enter_context(nc.semaphore(n)) for n in names}

        def pair(name, n=2):
            return [ctx.enter_context(nc.semaphore(f"{name}{i}")) for i in range(n)]

        ada_in, w_in_, ws_in = pair("ada_in"), pair("w_in"), pair("ws_in")
        gate_out, gate_back = pair("gate_out"), pair("gate_back")
        h_back, x2_back, row_out = pair("h_back"), pair("x2_back"), pair("row_out")
        ada0_in, x2_out = pair("ada0_in", N_ADA_EARLY // 2), pair("x2_out")

        at_a, n_a = places(ROWS_A)
        at_b, n_b = places(ROWS_B)
        assert n_a == P

        def col_a(name, j=0, n=1):
            return cols_a[:, at_a[name] + j:at_a[name] + j + n]

        def col_b(name, j=0, n=1):
            return cols_b[:, at_b[name] + j:at_b[name] + j + n]

        def weights(name, col, n=NB, row=0, k=KD):
            w = a[name][0]
            return w[row:row + k * P, :].rearrange("(k p) n -> p k n", p=P)[:, :, col]

        def slot(i):
            return ps[:, i, :]

        block = ctx.enter_context(nc.Block())

        @block.sync
        def _(sp):
            sp.dma_start(ident[:], a["k_ident"]).then_inc(s["const_in"], 16)
            sp.dma_start(x_tok[:], a["x"][0].rearrange("(t p) d -> p t d", p=P)).then_inc(s["x_in"], 16)
            for t, rr in enumerate((ROWS_A, ROWS_B)):
                for name, r0 in places(rr)[0].items():
                    v = a[name]
                    v = v.flatten() if len(v.shape) > 1 else v
                    sp.dma_start(rows[r0:r0 + rr[name], t, :],
                                 v.rearrange("(r p) -> r p", p=P)).then_inc(s["vec_in"], 16)
            for b in range(0, N_ADA_EARLY, 2):
                for k in range(2):
                    sp.dma_start(ada_w[:, b + k, :, :], weights("w_ada", bass.ds((b + k) * NB, NB)))\
                      .then_inc(ada0_in[b // 2], 16)
            for k in range(2):
                sp.dma_start(raw[:, k, :, :], weights("w_in", bass.ds(3 * ATT + SSM * k, NB))).then_inc(w_in_[k], 16)

            def ada(b, k):
                sp.dma_start(raw[:, k, :, :], weights("w_ada", bass.ds(b * NB, NB))).then_inc(ada_in[k], 16)

            def load(n, k, name, col, row=0, kc=KD):
                sp.wait_ge(s["w_split"], n - 1)
                sp.sem_inc(s["passed"], 1)
                sp.dma_start(raw[:, k, 0:kc, :],
                             weights(name, bass.ds(col, NB), row=row, k=kc)).then_inc(w_in_[k], 16)

            load(2, 0, "w_in", 3 * ATT + SSM + NB)
            with sp.Fori(0, 3) as i:
                for k in range(2):
                    load(2 * i + 3 + k, 1 - k, "w_in", i * (2 * NB) + 3 * ATT + SSM + (2 + k) * NB)
            with sp.Fori(0, 3) as i:
                for k in range(2):
                    load(2 * i + N_QKV + k, 1 - k, "w_in", i * (2 * NB) + k * NB)
            sp.wait_ge(s["w_split"], N_PROJ)
            for b in range(N_ADA_EARLY, N_ADA_EARLY + 2):
                ada(b, b % 2)
            sp.wait_ge(s["gemm"], units_before(N_PROJ))
            sp.dma_start(delta[:], a["k_delta"]).then_inc(s["attn_in"], 16)
            sp.dma_start(log8[:], a["k_log8"]).then_inc(s["attn_in"], 16)
            with sp.Fori(0, (N_ADA - N_ADA_EARLY - 2) // 2) as i:
                for k in range(2):
                    sp.wait_ge(s["ada_summed"], 2 * i + N_ADA_EARLY // 2 + k + 1)
                    sp.sem_inc(s["passed"], 1)
                    ada(2 * i + N_ADA_EARLY + 2 + k, k)

            def proj(j, k):
                sp.dma_start(raw[:, k, 0:KA, :],
                             weights("w_proj_att", bass.ds(j * NB, NB), k=KA)).then_inc(w_in_[k], 16)
                sp.dma_start(raw[:, k, KA:KA + 2, :],
                             weights("w_proj_ssm", bass.ds(j * NB, NB), k=2)).then_inc(ws_in[k], 16)

            def gates(j):
                for cg in range(2):
                    if j:
                        sp.wait_ge(s["proj_read"], 2 * j + cg - 1)
                    for g in range(2):
                        sp.dma_start(gate_in[:, cg, g, :], gates_d[g * KD + 2 * j + cg]).then_inc(gate_back[cg], 16)

            sp.wait_ge(s["ada_done"], N_ADA)
            proj(0, 1)
            proj(1, 0)
            for k in range(2):
                sp.wait_ge(gate_out[k], 16 * KD)
            sp.wait_ge(s["oh_ready"], KA)
            sp.wait_ge(s["ot_ready"], KA)
            gates(0)
            for j in range(2, 4):
                gates(j - 1)
                sp.wait_ge(s["w_split"], N_PROJ + j - 1)
                proj(j, 1 - j % 2)
            gates(3)
            load(N_OUT, 1, "w_out", 0)
            load(N_OUT + 1, 0, "w_out", NB)
            sp.wait_ge(s["h_out"], 16)
            sp.wait_ge(s["gemm"], units_before(N_OUT))
            sp.wait_ge(s["merged_ready"], KD)
            for half in range(2):
                sp.dma_start(h_t[:, 4 * half:4 * half + 4, :], h_d[4 * half:4 * half + 4].rearrange("c p t -> p c t"))\
                  .then_inc(h_back[half], 16)
            for k in range(2):
                load(N_OUT + 2 + k, 1 - k, "w_out", (2 + k) * NB)

            with sp.Fori(0, 4) as q:
                for p in range(2):
                    for k in range(2):
                        load(8 * q + N_FFN + 2 * p + k, 1 - k, "w_up", q * 512 + (k * FF + p * NB))
                for p in range(2):
                    for k in range(2):
                        n = 8 * q + N_FFN + 4 + 2 * p + k
                        sp.wait_ge(s["w_split"], n - 1)
                        sp.sem_inc(s["passed"], 1)
                        wd = a["w_down"][0].rearrange("(q k p) n -> p (q k) n", p=P, k=4)
                        sp.dma_start(raw[:, 1 - k, 0:4, :],
                                     wd[:, bass.ds(q * 4, 4), (2 * p + k) * NB:(2 * p + k + 1) * NB])\
                          .then_inc(w_in_[1 - k], 16)

            sp.dma_start(ln_g[:], a["ln_g_2"].partition_broadcast(P).rearrange("p a n -> p (a n)")).then_inc(s["late_in"], 16)
            sp.dma_start(ln_b[:], a["ln_b_2"].partition_broadcast(P).rearrange("p a n -> p (a n)")).then_inc(s["late_in"], 16)
            for h in range(2):
                for c in range(K2):
                    sp.dma_start(bs_row[64 * h:64 * h + 64, c, :],
                                 a["b_s_2"][0, 2 * c + h].partition_broadcast(64)).then_inc(s["late_in"], 16)
            sp.dma_start(w_pool[:], a["w_pool_2"][0].rearrange("g c d -> c g d")).then_inc(s["late_in"], 16)
            sp.dma_start(inv[:], a["k_inv"]).then_inc(s["late_in"], 16)
            sp.wait_ge(s["gemm"], units_before(N_V2))
            sp.dma_start(ws_tok[:].rearrange("p (g s) -> p g s", g=8),
                         a["w_s_2"][0].rearrange("g t s -> t g s")).then_inc(s["late_in"], 16)
            IN2 = dict(u=0, v=1, za=2, xb=3, bg=4, cg=5, zb=6, xc=7, zc=8)
            GATE2 = 9 * W2

            def pair2(n, k0, k1):
                load(n, 1, "w_in_2", k0)
                load(n + 1, 0, "w_in_2", k1)

            def gate2(n0, g, name):
                with sp.Fori(0, 4) as j:
                    load(2 * j + n0, 1, "w_in_2", j * NB + (GATE2 + g * D))
                    load(2 * j + n0 + 1, 0, name, j * NB, kc=K2)

            pair2(N_V2, IN2["v"] * W2, IN2["v"] * W2 + NB)
            for p in range(2):
                pair2(N_A + 2 * p, IN2["u"] * W2 + p * NB, IN2["za"] * W2 + p * NB)
            gate2(N_GA, 0, "w_pa_2")
            for p in range(2):
                pair2(N_B + 4 * p, IN2["xb"] * W2 + p * NB, IN2["cg"] * W2 + p * NB)
                pair2(N_B + 4 * p + 2, IN2["bg"] * W2 + p * NB, IN2["zb"] * W2 + p * NB)
            gate2(N_GB, 1, "w_pb_2")
            for p in range(2):
                pair2(N_C + 2 * p, IN2["xc"] * W2 + p * NB, IN2["zc"] * W2 + p * NB)
            gate2(N_GC, 2, "w_pc_2")
            pair_wo = [(N_WO, 1), (N_WO + 1, 0)]
            for n, k in pair_wo:
                load(n, k, "w_o_2", (n - N_WO) * NB)
            sp.wait_ge(s["m2_ready"], KD)
            for half in range(2):
                sp.dma_start(y_t[:, 4 * half:4 * half + 4, :], x2_d[4 * half:4 * half + 4].rearrange("c p t -> p c t"))\
                  .then_inc(x2_back[half], 16)
            sp.dma_start(g_row[:], a["final_g_2"].partition_broadcast(P)).then_inc(s["g_row_in"], 16)
            for n, k in pair_wo:
                load(n + 2, k, "w_o_2", (n + 2 - N_WO) * NB)
            for t in range(QB):
                sp.wait_ge(s["orow"], t + 1)
                sp.dma_start(out[0, t * P:(t + 1) * P, :], o_row[:, t % 2, :]).then_inc(row_out[t % 2], 16)
            for k in range(2):
                sp.wait_ge(row_out[k], 16 * QB // 2)

        @block.gpsimd
        def _(pool):
            nc.gpsimd.memset(ones[:], 1.0).then_inc(s["consts_ready"], 1)
            nc.gpsimd.memset(eps_rms[:], RMS_EPS).then_inc(s["consts_ready"], 1)

            def split(n, k, landed, before=None, kc=KD, landed_ssm=None):
                pool.wait_ge(w_in_[k], landed)
                if landed_ssm:
                    pool.wait_ge(ws_in[k], landed_ssm)
                if before is not None:
                    pool.wait_ge(s["gemm"], before)
                pool.sem_inc(s["passed"], 1)
                nc.gpsimd.tensor_scalar(w_h[:, k, 0:kc, :], raw[:, k, 0:kc, :], 1.0, None, ALU.mult)\
                  .then_inc(s["w_high"], 1)
                pool.wait_ge(s["w_high"], n + 1)
                nc.gpsimd.tensor_tensor(w_l[:, k, 0:kc, :], raw[:, k, 0:kc, :],
                                        w_h[:, k, 0:kc, :].bitcast(F32), ALU.subtract).then_inc(s["w_split"], 1)

            def single(n, kc=KD, landed_ssm=None):
                split(n, n % 2, 16 * (n // 2 + 1), units_before(n - 1) if n >= 2 else None, kc, landed_ssm)

            def pairs(n0, trips, kcs=(KD, KD)):
                m = len(kcs)
                with pool.Fori(0, trips) as i:
                    for k, kc in enumerate(kcs):
                        n = n0 + k
                        split(i * m + n, n % 2, i * (8 * m) + 16 * (n // 2 + 1),
                              i * (2 * m) + units_before(n - 1), kc)

            for n in range(3):
                single(n)
            pairs(3, 6)

            stage_step = Steps(pool, s["staged"])

            def stage(p, e, done=None):
                own, other = slice(HD * e, HD * e + HD), slice(HD - HD * e, P - HD * e)
                if done is not None:
                    pool.wait_ge(s["pv"], done)
                q, k = qk[own, p, :], qk[own, p + KA, :]
                stage_step(nc.gpsimd.tensor_scalar(q2[own, e, :], q, 1.0, None, ALU.mult))
                if p or e:
                    stage_step(nc.gpsimd.tensor_scalar(k_hh[own, e, :], k, 1.0, None, ALU.mult))
                    stage_step(nc.gpsimd.tensor_scalar(k_hh[other, e, :], k, 1.0, None, ALU.mult))
                stage_step(nc.gpsimd.tensor_tensor(q2[other, e, :], q, q2[own, e, :].bitcast(F32), ALU.subtract))
                for half in (own, other) if p or e else ():
                    stage_step(nc.gpsimd.tensor_tensor(k_ll[half, e, :], k, k_hh[own, e, :].bitcast(F32), ALU.subtract))
                stage_step(nc.gpsimd.tensor_copy(v_st[:, e], v_tok[:, :, P * p + HD * e:P * p + HD * (e + 1)]))

            pool.wait_ge(s["qkv_read"], 12)
            for head in range(HEADS):
                stage(head // 2, head % 2, QB * (head - 1) if head >= 2 else None)
            for j in range(4):
                single(N_PROJ + j, KA + 2, 16 * (j // 2 + 1))
            single(N_OUT)
            single(N_OUT + 1)
            pairs(N_OUT + 2, 1)
            pairs(N_FFN, 4, (KD,) * 4 + (4,) * 4)
            pairs(N_V2, 1)
            single(N_A)
            single(N_A + 1)
            pool.wait_ge(s["wst_ready"], 1)
            nc.gpsimd.affine_select(out=wst[:], in_=wst[:], compare_op=ALU.is_ge, fill=0.0, base=0,
                                    pattern=[[0, 8], [1, P]], channel_multiplier=-1).then_inc(s["wst_masked"], 1)
            for n in range(N_A + 2, N_GA):
                single(n)
            pairs(N_GA, 4, (KD, K2))
            pairs(N_B, 4)
            pairs(N_GB, 4, (KD, K2))
            pairs(N_C, 2)
            pairs(N_GC, 4, (KD, K2))
            pairs(N_WO, 2)

        @block.tensor
        def _(pe):
            def product_half(dst, k, cg, kc, high, low, th, kw=0):
                tok = slice(HALF * th, HALF * th + HALF)
                for c in range(kc):
                    for p, (w, x) in enumerate(((w_h, high), (w_h, low), (w_l, high))):
                        last = nc.tensor.matmul(dst[:, tok], w[:, k, kw + c, P * cg:P * cg + P], x[:, c, tok],
                                                start=(c == 0 and p == 0), stop=(c == kc - 1 and p == 2))
                return last

            def product(dst, k, cg, kc, high, low, kw=0):
                for th in range(2):
                    last = product_half(dst, k, cg, kc, high, low, th, kw)
                return last

            def product_pair(slots, k, kc, high, low, ready, base=0):
                for c in range(kc):
                    pe.wait_ge(ready, base + (c + 1))
                    for cg in range(2):
                        for th in range(2):
                            tok = slice(HALF * th, HALF * th + HALF)
                            for p, (w, x) in enumerate(((w_h, high), (w_h, low), (w_l, high))):
                                last = nc.tensor.matmul(slot(slots[cg])[:, tok], w[:, k, c, P * cg:P * cg + P], x[:, c, tok],
                                                        start=(c == 0 and p == 0), stop=(c == kc - 1 and p == 2),
                                                        skip_group_check=True)
                        if c == kc - 1:
                            last.then_inc(s["gemm"], 1)

            def rows_chunk(dst, k, t0, t, c):
                tok = slice((t0 + t) * P, (t0 + t + 1) * P)
                for p, (w, x) in enumerate(((w_h, act_h), (w_h, act_l), (w_l, act_h))):
                    last = nc.tensor.matmul(dst[:, NB * t:NB * t + NB], x[:, c, tok], w[:, k, c, :],
                                            start=(c == 0 and p == 0), stop=(c == KD - 1 and p == 2),
                                            skip_group_check=True)
                return last

            def product_rows(dst, k, t0):
                for t in range(4):
                    for c in range(KD):
                        last = rows_chunk(dst, k, t0, t, c)
                return last

            def split_done(n):
                pe.wait_ge(s["w_split"], n + 1)

            def gate_unit(ch, t, cg):
                if cg == 0:
                    split_done(4 * ch + N_GATE + t)
                j = 2 * t + cg
                for th in range(2):
                    if j:
                        pe.wait_ge(s["gate_read"], 16 * ch + 2 * j + th - 1)
                    else:
                        pe.wait_ge(s["gate_read"], 16 * ch)
                    product_half(slot(0), (N_GATE + t) % 2, cg, KD, act_h, act_l, th)\
                        .then_inc(s["gemm"] if th else s["gate_half"], 1)

            def s5_matrices(ch, t):
                pe.wait_ge(s["bc_ready"], 4 * ch + t + 1)
                if t:
                    pe.wait_ge(s["bu_read"], 8 * ch + 2 * t - 1)
                else:
                    pe.wait_ge(s["bu_read"], 8 * ch)
                for m in range(4):
                    last = nc.tensor.transpose(slot(1)[:, P * m:P * m + P], bc[:, m, :], ident[:])
                last.then_inc(s["bct_done"], 1)

            def s5_in(ch, t):
                pe.wait_ge(s["bct_copied"], 4 * ch + t + 1)
                if t:
                    pe.wait_ge(s["bu_read"], 8 * ch + 2 * t)
                for m in range(2):
                    for th in range(2):
                        tok = HALF * th
                        last = nc.tensor.matmul(slot(1 + m)[:, tok:tok + HALF], bct[:, t % 2, m, :],
                                                us[:, bass.ds(ch, 1), tok:tok + HALF].rearrange("p a n -> p (a n)"),
                                                start=True, stop=True)
                    last.then_inc(s["bu_ready"], 1)

            def s5_out(ch, t):
                pe.wait_ge(s["x_ready"], 4 * ch + t + 1)
                if t == 0:
                    pe.wait_ge(s["y_read"], ch)
                for th in range(2):
                    tok = slice(HALF * th, HALF * th + HALF)
                    for m in range(2):
                        last = nc.tensor.matmul(slot(3)[:, tok], bct[:, t % 2, 2 + m, :], s5[:, 6 + m, tok],
                                                start=(t == 0 and m == 0), stop=(t == 3 and m == 1),
                                                skip_group_check=True)
                last.then_inc(s["y_done"], 1)

            pe.wait_ge(s["vec_in"], 16 * (len(ROWS_A) + len(ROWS_B)))
            pe.wait_ge(s["const_in"], 16)
            nc.tensor.transpose(slot(0)[:, 0:P], rows[:, 0, :], ident[:])
            nc.tensor.transpose(slot(0)[:, P:P + n_b], rows[0:n_b, 1, :], ident[0:n_b, 0:n_b]).then_inc(s["colt"], 1)
            pe.wait_ge(s["x_in"], 16)
            for c in range(KD):
                if c >= 4:
                    pe.wait_ge(s["h_ready"], c - 3)
                elif c == 0:
                    pe.wait_ge(s["colt_read"], 1)
                for t in range(QB):
                    last = nc.tensor.transpose(slot(c % 4)[:, P * t:P * t + P], x_tok[:, t, P * c:P * c + P], ident[:])
                last.then_inc(s["tr"], 1)

            def statistics(sums, adds):
                pe.wait_ge(s["sq_used"], adds)
                for i, x in enumerate(sums):
                    for b in range(QB):
                        last = nc.tensor.matmul(slot(3)[:, QB * i + b:QB * i + b + 1], x[:, P * b:P * b + P], ones[:, 0:1],
                                                start=True, stop=True)
                last.then_inc(s["sums_ready"], 1)

            def everywhere(count, dst, i):
                pe.wait_ge(s["diag_ready"], count)
                for th in range(2):
                    last = nc.tensor.matmul(dst[:, HALF * th:HALF * th + HALF], ones[:],
                                            diag[i][:, 4 * th:4 * th + 4, :].rearrange("p b t -> p (b t)"),
                                            start=True, stop=True)
                last.then_inc(s["rstd_ready"], 1)

            def ada(dst, part):
                for cg in range(2):
                    last = nc.tensor.matmul(dst[:, cg:cg + 1], part[:, P * cg:P * cg + P], ones[:, 0:1], start=True, stop=True)
                return last

            pe.wait_ge(s["consts_ready"], 2)
            statistics([acc], KD - 1)
            for b in range(N_ADA_EARLY):
                pe.wait_ge(s["ada_summed"], b // 2 + 1)
                ada(slot(2)[:, 2 * b:2 * b + 2], ada_w[:, b, 0, :]).then_inc(s["ada_done"], 1)
            everywhere(1, slot(3), 0)

            split_done(0)
            product_pair((0, 1), 0, KD, act_h, act_l, s["u_ready"])

            pe.wait_ge(s["us_ready"], 2)
            pe.wait_ge(s["mod_read"], 1)
            with pe.Fori(0, 2) as ch:
                s5_matrices(ch, 0)
                s5_in(ch, 0)
                for t in range(4):
                    gate_unit(ch, t, 0)
                    if t:
                        s5_out(ch, t - 1)
                    if t < 3:
                        s5_matrices(ch, t + 1)
                    gate_unit(ch, t, 1)
                    if t < 3:
                        s5_in(ch, t + 1)
                s5_out(ch, 3)

            pe.wait_ge(s["gate_read"], 4 * KD)
            with pe.Fori(0, 2) as i:
                for b in range(2):
                    split_done(2 * i + N_QKV + b)
                    for cg in range(2):
                        if b:
                            pe.wait_ge(s["qkv_read"], 4 * i + cg + 1)
                        else:
                            pe.wait_ge(s["qkv_read"], 4 * i)
                        product(slot(cg), 1 - b, cg, KD, act_h, act_l).then_inc(s["gemm"], 1)
            for b in range(2):
                split_done(N_QKV + 4 + b)
                for h in range(2):
                    pe.wait_ge(s["qkv_read"], 8 + 2 * b + h - 1)
                    product_rows(slot(h), 1 - b, 4 * h).then_inc(s["gemm"], 1)
            pe.wait_ge(s["yg_ready"], 2)
            for o in range(2):
                for th in range(2):
                    tok = slice(HALF * th, HALF * th + HALF)
                    for c in range(2):
                        last = nc.tensor.matmul(slot(2 + o)[:, tok], w_glu[:, c, P * o:P * o + P], yg[:, c, tok],
                                                start=(c == 0), stop=(c == 1))
                last.then_inc(s["glu_done"], 1)

            pe.wait_ge(s["qkv_read"], 12)
            pe.wait_ge(s["y_gated"], 2)

            def scores(p, t):
                e, qb = tiles[t % NT]
                if t % QB == 0:
                    pe.wait_ge(s["staged"], p * (2 * STAGED) + STAGED * (t // QB + 1) - 4)
                if t >= 2:
                    pe.wait_ge(s["sm_ready"], NT * p + t - 1)
                n = (qb + 1) * P
                for c0 in range(0, n, HALF):
                    w = min(HALF, max(2 * P, n - c0))
                    for k in (k_hh, k_ll):
                        last = nc.tensor.matmul(slot(t % 2)[:, c0:c0 + w], q2[:, e, P * qb:P * qb + P],
                                                k[:, e, c0:c0 + w], start=(k is k_hh), stop=(k is k_ll))
                last.then_inc(s["s_ready"], 1)

            def transposes(p, t):
                qb = tiles[t % NT][1]
                pe.wait_ge(s["p_ready"], NT * p + t + 1)
                if t:
                    pe.wait_ge(s["ptc0"], NT * p + t)
                for b in range(min(4, qb + 1)):
                    last = nc.tensor.transpose(slot(2)[:, P * b:P * b + P], prob[:, t % 4, P * b:P * b + P], ident[:])
                last.then_inc(s["pt0"], 1)
                if qb >= 4:
                    if t:
                        pe.wait_ge(s["ptc1"], QB * p + t // 2)
                    for b in range(4, qb + 1):
                        last = nc.tensor.transpose(slot(2)[:, P * b:P * b + P], prob[:, t % 4, P * b:P * b + P], ident[:])
                    last.then_inc(s["pt1"], 1)

            def values(p, t):
                e, qb = tiles[t]
                pe.wait_ge(s["ptc0"], NT * p + t + 1)
                if qb >= 4:
                    pe.wait_ge(s["ptc1"], QB * p + t // 2 + 1)
                if t:
                    pe.wait_ge(s["o_ready"], NT * p + t - 1)
                else:
                    pe.wait_ge(s["o_ready"], NT * p)
                dst = slot(3)[:, HALF * (t % 2):HALF * (t % 2) + HALF]
                for b in range(qb + 1):
                    last = nc.tensor.matmul(dst[:, 0:HD], prob_t[:, t % 2, P * b:P * b + P], v_st[:, e, b, :],
                                            start=(b == 0), stop=(b == qb))
                last.then_inc(s["pv"], 1)
                if t % 4 == 3:
                    k = t // 4
                    pe.wait_ge(s["ada_summed"], 4 * p + N_ADA_EARLY // 2 + k + 1)
                    ada(dst[:, HD:HD + 2], ada_part[:, k % 2]).then_inc(s["ada_done"], 1)

            def heads(p, last):
                end = NT if last else NT + 3
                for t in range(NT):
                    if t + 3 < end:
                        scores(p, t + 3)
                    if t + 1 < end:
                        transposes(p, t + 1)
                    values(p, t)

            pe.wait_ge(s["k0_ready"], 4)
            for t in range(3):
                scores(0, t)
            transposes(0, 0)
            with pe.Fori(0, HEADS // 2 - 1) as p:
                heads(p, False)
            heads(HEADS // 2 - 1, True)

            pe.wait_ge(s["o_ready"], HEADS * QB)
            for c in range(KA):
                for t in range(QB):
                    last = nc.tensor.transpose(slot(c)[:, P * t:P * t + P], o_tok[:, t, P * c:P * c + P], ident[:])
                last.then_inc(s["otr"], 1)

            pe.wait_ge(s["ys_ready"], 2)
            pe.wait_ge(s["ot_ready"], 2)
            with pe.Fori(0, 2) as i:
                for b in range(2):
                    split_done(2 * i + N_PROJ + b)
                    for cg in range(2):
                        if b:
                            pe.wait_ge(s["proj_read"], 4 * i + cg + 1)
                        else:
                            pe.wait_ge(s["proj_read"], 4 * i)
                        product(slot(2 * cg + 1), 1 - b, cg, 2, ys_h, ys_l, kw=KA).then_inc(s["gemm"], 1)
                        if b == 0 and cg == 0:
                            pe.wait_ge(s["ot_ready"], KA)
                        product(slot(2 * cg), 1 - b, cg, KA, in2_h, in2_l).then_inc(s["gemm"], 1)

            pe.wait_ge(s["proj_read"], KD - 1)
            with pe.Fori(0, 2) as i:
                pe.wait_ge(s["out_read"], 4 * i)
                split_done(2 * i + N_OUT)
                product_pair((0, 1), 1, KD, act_h, act_l, s["merged_ready"])
                split_done(2 * i + N_OUT + 1)
                pe.wait_ge(s["proj_read"], KD)
                for cg in range(2):
                    product(slot(2 + cg), 0, cg, KD, act_h, act_l).then_inc(s["gemm"], 1)

            statistics([acc], 2 * (KD - 1))
            everywhere(2, slot(3), 0)
            with pe.Fori(0, 4) as q:
                pe.wait_ge(s["down_read"], 8 * q)
                split_done(8 * q + N_FFN)
                product_pair((0, 1), 1, KD, act_h, act_l, s["u_ready"], KD)
                for p in range(2):
                    for b in range(2):
                        if p == 0 and b == 0:
                            continue
                        split_done(8 * q + N_FFN + 2 * p + b)
                        for cg in range(2):
                            if p:
                                pe.wait_ge(s["v_read"] if b else s["a_read"], 4 * q + cg + 1)
                            product(slot(2 * b + cg), 1 - b, cg, KD, act_h, act_l).then_inc(s["gemm"], 1)
                pe.wait_ge(s["a_read"], 4 * q + 4)
                split_done(8 * q + N_FFN + 4)
                product_pair((0, 1), 1, 4, in2_h, in2_l, s["f_ready"], 4 * q)
                for u in range(2, 8):
                    if u % 2 == 0:
                        split_done(8 * q + N_FFN + 4 + u // 2)
                    if u >= 4:
                        pe.wait_ge(s["down_read"], 8 * q + u - 3)
                    product(slot(u % 4), 1 - (u // 2) % 2, u % 2, 4, in2_h, in2_l).then_inc(s["gemm"], 1)

            statistics([acc2[:, 0, :], acc2[:, 1, :]], 4 * (KD - 1))
            everywhere(4, slot(3), 0)
            everywhere(4, slot(2), 1)
            pe.wait_ge(s["rstd2_ready"], 2)
            for b in range(2):
                split_done(N_V2 + b)
            for c in range(KD):
                pe.wait_ge(s["u_ready"], 2 * KD + c + 1)
                for b in range(2):
                    for h in range(2):
                        for t in (0, 2):
                            rows_chunk(slot(2 * b + h), 1 - b, 4 * h, t, c)
            for b in range(2):
                for h in range(2):
                    for t in (1, 3):
                        for c in range(KD):
                            last = rows_chunk(slot(2 * b + h), 1 - b, 4 * h, t, c)
                    last.then_inc(s["gemm"], 1)
            pe.wait_ge(s["late_in"], 16 * 13)
            for p in range(2):
                for b in range(2):
                    split_done(N_A + 2 * p + b)
                    for cg in range(2):
                        if b:
                            pe.wait_ge(s["au_read"], 2 * p + cg + 1)
                        elif p:
                            pe.wait_ge(s["az_read"], cg + 1)
                        else:
                            pe.wait_ge(s["v2_read"], cg + 1)
                        product(slot(cg), 1 - b, cg, KD, act_h, act_l).then_inc(s["gemm"], 1)
                        if p == 0 and b == 0 and cg == 0:
                            pe.wait_ge(s["v2_read"], 4)
                            for g in range(8):
                                last = nc.tensor.transpose(slot(2)[:, P * g:P * g + P], ws_tok[:, P * g:P * g + P], ident[:])
                            last.then_inc(s["wst_done"], 1)
                pe.wait_ge(s["vn_ready"], 1)
                pe.wait_ge(s["wst_masked"], 1)
                for cg in range(2):
                    if p:
                        pe.wait_ge(s["sg_read"], cg + 1)
                    for g in range(2):
                        grp = 2 * (2 * p + cg) + g
                        for t in range(QB):
                            last = nc.tensor.matmul(slot(2 + cg)[HD * g:HD * g + HD, P * t:P * t + P],
                                                    vg[:, t, HD * grp:HD * grp + HD], wst[:, grp, :],
                                                    start=True, stop=True)
                    last.then_inc(s["sg_done"], 1)

            def gate_loop(n0, ready, gate_read, p_read, free):
                pe.wait_ge(free, 4)
                with pe.Fori(0, 2) as j:
                    for i in range(4):
                        b = i % 2
                        split_done(4 * j + n0 + i)
                        if b:
                            pe.wait_ge(ready, 4)
                        for cg in range(2):
                            pe.wait_ge(p_read if b else gate_read, 4 * j + 2 * (i // 2))
                            if b:
                                product(slot(2 + cg), 0, cg, K2, in2_h, in2_l).then_inc(s["gemm"], 1)
                            else:
                                product(slot(cg), 1, cg, KD, act_h, act_l).then_inc(s["gemm"], 1)

            gate_loop(N_GA, s["a_ready"], s["sa_ready"], s["pa_read"], s["az_read"])
            pe.wait_ge(s["sa_ready"], KD)
            for p in range(2):
                for b, (before, free) in enumerate(((s["bg_read"], s["xb_read"]), (s["bz_read"], s["bc_read"]))):
                    split_done(N_B + 4 * p + b)
                    if p == 0 and b:
                        pe.wait_ge(s["pa_read"], KD)
                    for cg in range(2):
                        if p:
                            pe.wait_ge(before, cg + 1)
                        product(slot(2 * b + cg), 1 - b, cg, KD, act_h, act_l).then_inc(s["gemm"], 1)
                for b, free in enumerate((s["xb_read"], s["bc_read"])):
                    split_done(N_B + 4 * p + 2 + b)
                    for cg in range(2):
                        pe.wait_ge(free, 2 * p + cg + 1)
                        product(slot(2 * b + cg), 1 - b, cg, KD, act_h, act_l).then_inc(s["gemm"], 1)
            gate_loop(N_GB, s["b_ready"], s["sb_ready"], s["pb_read"], s["bg_read"])
            pe.wait_ge(s["sb_ready"], KD)
            for p in range(2):
                for b in range(2):
                    split_done(N_C + 2 * p + b)
                    if p == 0 and b:
                        pe.wait_ge(s["pb_read"], KD)
                    for cg in range(2):
                        if p:
                            pe.wait_ge(s["cz_read"] if b else s["cp_ready"], cg + 1)
                        product(slot(2 * b + cg), 1 - b, cg, KD, act_h, act_l).then_inc(s["gemm"], 1)
                for cg in range(2):
                    c = 2 * p + cg
                    pe.wait_ge(s["pooled"], c + 1)
                    for th in range(2):
                        tok = slice(HALF * th, HALF * th + HALF)
                        last = nc.tensor.matmul(slot(cg)[:, tok], w_pool[:, c, :], pool_in[c % 2][:, tok],
                                                start=True, stop=True)
                    last.then_inc(s["pool_done"], 1)
            gate_loop(N_GC, s["ch_done"], s["sc_ready"], s["pc_read"], s["cp_ready"])

            pe.wait_ge(s["pc_read"], KD)
            with pe.Fori(0, 2) as i:
                pe.wait_ge(s["y_ready"], 4 * i)
                split_done(2 * i + N_WO)
                product_pair((0, 1), 1, KD, act_h, act_l, s["m2_ready"])
                split_done(2 * i + N_WO + 1)
                for cg in range(2):
                    product(slot(2 + cg), 0, cg, KD, act_h, act_l).then_inc(s["gemm"], 1)
            pe.wait_ge(s["y_ready"], KD)
            for t in range(QB):
                if t >= 4:
                    pe.wait_ge(s["orow"], t - 3)
                for c in range(KD):
                    last = nc.tensor.transpose(slot(t % 4)[:, P * c:P * c + P], y_t[:, c, P * t:P * t + P], ident[:])
                last.then_inc(s["otr2"], 1)

        @block.scalar
        def _(act):
            A = nc.scalar
            step = Steps(act, s["act"])

            act.dma_start(mask_b[:], a["k_mask_b"]).then_inc(s["s5_in"], 16)
            act.dma_start(mask_c[:], a["k_mask_c"]).then_inc(s["s5_in"], 16)
            for m, name in enumerate(("b_re", "b_im")):
                act.dma_start(b_in[:, m], a[name][0].rearrange("(t g) n c -> (g n) t c", g=2)).then_inc(s["s5_in"], 16)
            for m, name in enumerate(("c_re", "c_im")):
                act.dma_start(cc[:, m], a[name][0].rearrange("(h g) c n -> (g c) h n", h=2)).then_inc(s["s5_in"], 16)
            with nc.allow_non_contiguous_dma(reason="sixteen time steps, one value for each state"):
                for g in range(2):
                    act.dma_start(par[NSTATE * g:NSTATE * g + NSTATE, 0, :],
                                  a["log_dt"][0].rearrange("(t g) -> g t", g=2)[g].partition_broadcast(NSTATE))\
                       .then_inc(s["s5_in"], 16)
            act.dma_start(w_glu[:], a["w_glu"][0].rearrange("(k p) n -> p k n", p=P)).then_inc(s["s5_in"], 16)

            act.wait_ge(s["colt_read"], 1)
            A.activation(c_act[:], col_a("c", 0, KD), ACT.Silu).then_inc(s["c_ready"], 1)
            def squares(k, ready):
                for c in range(KD):
                    if k == 0:
                        act.wait_ge(s["tr"], c + 1)
                        A.activation(h_t[:, c, :], slot(c % 4), ACT.Copy).then_inc(s["h_ready"], 1)
                    act.wait_ge(ready, c + 1)
                    if c >= 3:
                        act.wait_ge(s["sq_used"], (KD - 1) * k + c - 2)
                    A.activation(sq[:, c % 2, :] if c else acc[:], h_t[:, c, :], ACT.Square).then_inc(s["sq_ready"], 1)

            def root(count):
                act.wait_ge(s["sums_ready"], count)
                A.activation(stat[:, 0, :], slot(3)[:, 0:QB], ACT.Sqrt, scale=1.0 / D, bias=eps_rms[:])\
                 .then_inc(s["std_ready"], 1)

            def norm(nu, shift):
                for c in range(KD):
                    act.wait_ge(s["t_ready"], KD * nu + c + 1)
                    A.activation(act_h[:, c, :], nrm[:, c % 2, :], ACT.Identity, bias=shift(c) if shift else 0.0)\
                     .then_inc(s["hi_ready"], 1)

            act.wait_ge(s["consts_ready"], 2)
            squares(0, s["h_ready"])
            act.dma_start(h_d.rearrange("c p t -> p c t"), h_t[:]).then_inc(s["h_out"], 16)
            root(1)
            act.wait_ge(s["mod_ready"], 1)
            norm(0, lambda c: mod[:, c:c + 1])

            act.wait_ge(s["s5_in"], 16 * 9)
            A.activation(par[:, 1, :], par[:, 0, :], ACT.Exp).then_inc(s["dt_ready"], 1)
            act.wait_ge(s["lrdt_ready"], 1)
            step(A.activation(mag[:], par[:, 2, :], ACT.Exp))
            act.wait_ge(s["angle_ready"], 1)
            step(A.activation(turn[:, 0], prep[:, 3, :, :], ACT.Sin))
            A.activation(turn[:, 1], prep[:, 2, :, :], ACT.Sin).then_inc(s["turn_ready"], 1)

            act.wait_ge(s["us_ready"], 2)

            def gate(ch, j):
                k = j % 2
                if j >= 2:
                    act.wait_ge(gate_out[k], 64 * ch + 16 * (j // 2))
                else:
                    act.wait_ge(gate_out[k], 64 * ch)
                for th in range(2):
                    tok = slice(HALF * th, HALF * th + HALF)
                    if th:
                        act.wait_ge(s["gemm"], 8 * ch + units_before(N_GATE) + j + 1)
                    else:
                        act.wait_ge(s["gate_half"], 8 * ch + j + 1)
                    act.sem_inc(s["passed"], 1)
                    A.activation(gate_st[:, k, tok], slot(0)[:, tok], ACT.Sigmoid,
                                 bias=cols_a[:, bass.ds(8 * ch + (at_a["b_gate"] + j), 1)]).then_inc(s["gate_read"], 1)
                act.wait_ge(s["gate_read"], 16 * ch + 2 * j + 2)
                act.dma_start(gates_d[bass.ds(8 * ch + j, 1)].rearrange("a p t -> p (a t)"), gate_st[:, k, :])\
                   .then_inc(gate_out[k], 16)

            def matrices(ch, t):
                act.wait_ge(s["bct_done"], 4 * ch + t + 1)
                A.activation(bct[:, t % 2].rearrange("p m n -> p (m n)"), slot(1)[:, 0:4 * P], ACT.Copy)\
                 .then_inc(s["bct_copied"], 1)

            with act.Fori(0, 2) as ch:
                matrices(ch, 0)
                for t in range(4):
                    gate(ch, 2 * t)
                    if t < 3:
                        matrices(ch, t + 1)
                    gate(ch, 2 * t + 1)
                act.wait_ge(s["y_read"], ch + 1)
                y = yg[:, bass.ds(ch, 1), :].rearrange("p a n -> p (a n)")
                A.activation(y, y, ACT.Gelu_apprx_tanh).then_inc(s["yg_ready"], 1)
            act.wait_ge(s["yg_ready"], 2)
            with act.Fori(0, 4) as i:
                for b in range(2):
                    act.wait_ge(s["gemm"], 2 * i + units_before(N_QKV) + b + 1)
                    A.activation(qk[:, bass.ds(2 * i + b, 1), :].rearrange("p a n -> p (a n)"), slot(b), ACT.Copy)\
                     .then_inc(s["qkv_read"], 1)
            for b in range(2):
                for h in range(2):
                    act.wait_ge(s["gemm"], units_before(N_QKV + 4 + b) + h + 1)
                    A.activation(v_tok[:, 4 * h:4 * h + 4, NB * b:NB * b + NB],
                                 slot(h).rearrange("p (t n) -> p t n", t=4), ACT.Copy).then_inc(s["qkv_read"], 1)
            for k in range(2):
                act.wait_ge(gate_out[k], 16 * KD)
                act.wait_ge(s["glu_done"], k + 1)
                A.activation(gate_st[:, k, :], slot(2 + k), ACT.Sigmoid, bias=col_a("b_glu", k)).then_inc(s["sig_ready"], 1)

            def softmax(p, t):
                n = (tiles[t % NT][1] + 1) * P
                act.wait_ge(s["sm_ready"], NT * p + t + 1)
                if t >= 3:
                    act.wait_ge(s["o_ready"], NT * p + t - 3)
                elif t == 2:
                    act.wait_ge(s["o_ready"], NT * p)
                A.activation(prob[:, t % 4, 0:n], prob[:, t % 4, 0:n], ACT.Exp, scale=-1.0,
                             bias=neg_max[:, t % 4:t % 4 + 1], accum_out=den[:, t % 4:t % 4 + 1])\
                 .then_inc(s["p_ready"], 1)

            def far_half(p, t):
                n = (tiles[t % NT][1] + 1) * P
                act.wait_ge(s["pt1"], QB * p + t // 2 + 1)
                if t:
                    act.wait_ge(s["pv"], NT * p + t - 1)
                A.activation(prob_t[:, t % 2, HALF:n], slot(2)[:, HALF:n], ACT.Copy).then_inc(s["ptc1"], 1)

            def heads(p, last):
                for t in range(NT):
                    if t + 2 < NT or not last:
                        softmax(p, t + 2)
                    if t % 2 and (t + 1 < NT or not last):
                        far_half(p, t + 1)

            for half in range(2):
                A.activation(k_hh[HD * half:HD * half + HD, 0, :], qk[0:HD, KA, :], ACT.Copy).then_inc(s["k0_ready"], 1)
            softmax(0, 0)
            softmax(0, 1)
            far_half(0, 0)
            with act.Fori(0, HEADS // 2 - 1) as p:
                heads(p, False)
            heads(HEADS // 2 - 1, True)

            act.wait_ge(s["o_ready"], HEADS * QB)
            for o in range(2):
                act.wait_ge(s["y_gated"], o + 1)
                A.activation(ys_h[:, o, :], yg[:, o, :], ACT.Copy).then_inc(s["ysh"], 1)
            for c in range(KA):
                act.wait_ge(s["otr"], c + 1)
                A.activation(in2_h[:, c, :], slot(c), ACT.Copy).then_inc(s["oh_ready"], 1)
            with act.Fori(0, 2) as i:
                for c in range(4):
                    act.wait_ge(s["mix_ready"], 4 * i + c + 1)
                    A.activation(act_h[:, bass.ds(4 * i + c, 1), :].rearrange("p a n -> p (a n)"), mix[:, 0, :], ACT.Copy)\
                     .then_inc(s["mh_ready"], 1)
            squares(1, s["out_read"])
            root(2)
            norm(1, lambda c: mod[:, 3 * KD + c:3 * KD + c + 1])

            base_f = units_before(N_FFN)
            with act.Fori(0, 4) as q:
                for p in range(2):
                    for cg in range(2):
                        c = 2 * p + cg
                        act.wait_ge(s["gemm"], 16 * q + base_f + 4 * p + cg + 1)
                        if p:
                            act.wait_ge(s["f_ready"], 4 * q + cg + 1)
                        else:
                            act.wait_ge(s["f_ready"], 4 * q)
                        A.activation(conv[:, cg, :], slot(cg), ACT.Identity,
                                     scale=cols_b[:, bass.ds(4 * q + (at_b["w_conv"] + c), 1)],
                                     bias=cols_a[:, bass.ds(4 * q + (at_a["b_conv"] + c), 1)]).then_inc(s["acc_ready"], 1)
                    for cg in range(2):
                        c = 2 * p + cg
                        act.wait_ge(s["a_read"], 4 * q + c + 1)
                        A.activation(conv[:, cg, :], conv[:, cg, :], ACT.Silu).then_inc(s["silu_ready"], 1)
                    for cg in range(2):
                        c = 2 * p + cg
                        act.wait_ge(s["v_read"], 4 * q + c + 1)
                        A.activation(in2_h[:, c, :], ffn[:], ACT.Copy).then_inc(s["fh_ready"], 1)

            for c in range(KD):
                act.wait_ge(s["down_read"], 24 + c + 1)
                for m in range(2):
                    if c >= 2:
                        act.wait_ge(s["sq_used"], 2 * (KD - 1) + 2 * (c - 2) + m + 1)
                    A.activation(sq[:, m, :] if c else acc2[:, m, :], h_t[:, c, :], ACT.Square,
                                 scale=col_b("g_final", c) if m else 1.0).then_inc(s["sq_ready"], 1)
            root(3)
            act.wait_ge(s["ms2_ready"], 1)
            A.activation(stat[:, 3, :], stat[:, 2, :], ACT.Sqrt, scale=1.0 / D, bias=eps_rms[:]).then_inc(s["std_ready"], 1)
            for m in range(2):
                act.wait_ge(s["rstd_ready"], 3 + m)
                A.activation(rstd2[:, m, :], slot(3 - m), ACT.Copy).then_inc(s["rstd2_ready"], 1)
            norm(2, None)
            for half in range(2):
                act.wait_ge(s["x2_ready"], 4 * half + 4)
                act.dma_start(x2_d[4 * half:4 * half + 4].rearrange("c p t -> p c t"), h_t[:, 4 * half:4 * half + 4, :])\
                   .then_inc(x2_out[half], 16)

            act.wait_ge(x2_out[0], 16)
            for b in range(2):
                for h in range(2):
                    act.wait_ge(s["gemm"], units_before(N_V2 + b) + h + 1)
                    A.activation(vg[:, 4 * h:4 * h + 4, NB * b:NB * b + NB],
                                 slot(2 * b + h).rearrange("p (t n) -> p t n", t=4), ACT.Gelu_apprx_tanh)\
                     .then_inc(s["v2_read"], 1)
            act.wait_ge(s["ln_var"], 1)
            A.activation(ln_rstd[:], ln_rstd[:], ACT.Sqrt).then_inc(s["ln_std"], 1)
            act.wait_ge(x2_out[1], 16)
            base_a = units_before(N_A)
            for p in range(2):
                for cg in range(2):
                    act.wait_ge(s["gemm"], base_a + 4 * p + cg + 1)
                    if p:
                        act.wait_ge(s["ap_ready"], cg + 1)
                    A.activation(a_u[:, cg, :], slot(cg), ACT.Gelu_apprx_tanh).then_inc(s["au_read"], 1)
                for cg in range(2):
                    act.wait_ge(s["gemm"], base_a + 4 * p + 2 + cg + 1)
                    A.activation(a_z[:, cg, :], slot(cg), ACT.Silu).then_inc(s["az_read"], 1)
                for cg in range(2):
                    c = 2 * p + cg
                    act.wait_ge(s["ap_ready"], c + 1)
                    A.activation(in2_h[:, c, :], a_s[:], ACT.Copy).then_inc(s["ah_ready"], 1)

            def gates2(n0, done, ready):
                with act.Fori(0, 4) as j:
                    for cg in range(2):
                        act.wait_ge(s["gemm"], 4 * j + units_before(n0) + cg + 1)
                        act.wait_ge(done, 2 * j)
                        A.activation(br[:, cg, :], slot(cg), ACT.Sigmoid).then_inc(ready, 1)

            act.wait_ge(s["a_ready"], K2)
            gates2(N_GA, s["pa_read"], s["sa_ready"])
            act.wait_ge(s["pa_read"], KD)
            base_b = units_before(N_B)
            for p in range(2):
                for cg in range(2):
                    act.wait_ge(s["gemm"], base_b + 8 * p + cg + 1)
                    if p:
                        act.wait_ge(s["b_ready"], cg + 1)
                    A.activation(br[:, cg, :], slot(cg), ACT.Copy).then_inc(s["xb_read"], 1)
                for cg in range(2):
                    c = 2 * p + cg
                    act.wait_ge(s["gemm"], base_b + 8 * p + 6 + cg + 1)
                    act.wait_ge(s["bg_read"], c + 1)
                    A.activation(br2[:], slot(2 + cg), ACT.Silu).then_inc(s["bz_read"], 1)
                    act.wait_ge(s["bp_ready"], c + 1)
                    A.activation(in2_h[:, c, :], br[:, cg, :], ACT.Copy).then_inc(s["bh_ready"], 1)
            act.wait_ge(s["b_ready"], K2)
            gates2(N_GB, s["mb_ready"], s["sb_ready"])
            act.wait_ge(s["mb_ready"], KD)
            base_c = units_before(N_C)
            for p in range(2):
                for cg in range(2):
                    c = 2 * p + cg
                    act.wait_ge(s["gemm"], base_c + 4 * p + cg + 1)
                    if cg:
                        act.wait_ge(s["pooled"], c)
                    elif p:
                        act.wait_ge(s["ch_done"], 2)
                    A.activation(br[:, 0, :], slot(cg), ACT.Copy).then_inc(s["xc_read"], 1)
                for cg in range(2):
                    c = 2 * p + cg
                    act.wait_ge(s["gemm"], base_c + 4 * p + 2 + cg + 1)
                    act.wait_ge(s["pooled"], 2 * p + 2)
                    if cg:
                        act.wait_ge(s["pool_done"], 2 * p + 1)
                    A.activation(br[:, cg, :], slot(2 + cg), ACT.Silu).then_inc(s["cz_read"], 1)
                for cg in range(2):
                    c = 2 * p + cg
                    act.wait_ge(s["cp_ready"], c + 1)
                    A.activation(in2_h[:, c, :], br[:, cg, :], ACT.Copy).then_inc(s["ch_ready"], 1)
            act.wait_ge(s["ch_done"], K2)
            gates2(N_GC, s["mc_ready"], s["sc_ready"])
            for c in range(KD):
                act.wait_ge(s["mc_ready"], c + 1)
                A.activation(act_h[:, c, :], merged[:, c, :], ACT.Copy).then_inc(s["m2_high"], 1)
            for t in range(QB):
                act.wait_ge(s["otr2"], t + 1)
                step(A.activation(o_sq[:], slot(t % 4), ACT.Square, accum_out=o_ssq[:, 0, t:t + 1]))
                A.activation(o_ssq[:, 1, t:t + 1], o_ssq[:, 0, t:t + 1], ACT.Sqrt, scale=1.0 / D, bias=eps_rms[:])\
                 .then_inc(s["ostd"], 1)

        @block.vector
        def _(dve):
            v = nc.vector
            step = Steps(dve, s["dve"])

            dve.wait_ge(s["colt"], 1)
            step(v.tensor_copy(cols_a[:], slot(0)[:, 0:P]))
            v.tensor_copy(cols_b[:, 0:n_b], slot(0)[:, P:P + n_b]).then_inc(s["colt_read"], 1)

            def add_square(k, c):
                dve.wait_ge(s["sq_ready"], KD * k + c + 1)
                if c >= 2:
                    dve.wait_ge(s["sq_used"], (KD - 1) * k + c - 1)
                v.tensor_tensor(acc[:], acc[:], sq[:, c % 2, :], ALU.add).then_inc(s["sq_used"], 1)

            def ada_sums(out, w, chunks=range(KD)):
                for c in chunks:
                    if c == 0:
                        step(v.tensor_scalar(out, w(0), c_act[:, 0:1], None, ALU.mult))
                        continue
                    ins = v.scalar_tensor_tensor(out, w(c), c_act[:, c:c + 1], out, ALU.mult, ALU.add)
                    if c < KD - 1:
                        step(ins)
                    else:
                        ins.then_inc(s["ada_summed"], 1)

            dve.wait_ge(s["c_ready"], 1)
            for i in range(N_ADA_EARLY // 2):
                for c in range(2 * i, 2 * i + 2):
                    if c:
                        add_square(0, c)
                dve.wait_ge(ada0_in[i], 32)
                ada_sums(ada_w[:, 2 * i:2 * i + 2, 0, :], lambda c, i=i: ada_w[:, 2 * i:2 * i + 2, c, :])

            def modulation(lo, hi, src):
                return v.tensor_tensor(mod[:, lo:hi], src, col_a("b_ada", lo, hi - lo), ALU.add)

            dve.wait_ge(s["ada_done"], N_ADA_EARLY)
            modulation(0, 2 * N_ADA_EARLY, slot(2)[:, 0:2 * N_ADA_EARLY]).then_inc(s["mod_read"], 1)
            dve.wait_ge(s["mod_read"], 1)
            v.scalar_tensor_tensor(gain[:, 0], mod[:, KD:2 * KD], 1.0, col_a("g_mix", 0, KD), ALU.add, ALU.mult)\
             .then_inc(s["mod_ready"], 1)

            def on_diagonal(i, x):
                v.tensor_tensor(diag[i][:], ident[:].unsqueeze(1).to_broadcast([P, QB, P]),
                                x.unsqueeze(2).to_broadcast([P, QB, P]), ALU.mult).then_inc(s["diag_ready"], 1)

            def one_over_root(count):
                dve.wait_ge(s["std_ready"], count)
                step(v.reciprocal(stat[:, 1, :], stat[:, 0, :]))

            def norm(nu, g, shift, rstd):
                def scaled(c):
                    v.scalar_tensor_tensor(nrm[:, c % 2, :], h_t[:, c, :], g[:, c:c + 1], rstd, ALU.mult, ALU.mult)\
                     .then_inc(s["t_ready"], 1)

                scaled(0)
                scaled(1)
                for c in range(KD):
                    dve.wait_ge(s["hi_ready"], KD * nu + c + 1)
                    high = act_h[:, c, :].bitcast(F32)
                    if shift is None:
                        ins = v.tensor_tensor(act_l[:, c, :], nrm[:, c % 2, :], high, ALU.subtract)
                    else:
                        ins = v.scalar_tensor_tensor(act_l[:, c, :], nrm[:, c % 2, :], shift(c), high, ALU.add, ALU.subtract)
                    ins.then_inc(s["u_ready"], 1)
                    if c + 2 < KD:
                        dve.wait_ge(s["u_ready"], KD * nu + c + 1)
                        scaled(c + 2)

            one_over_root(1)
            on_diagonal(0, stat[:, 1, :])
            dve.wait_ge(s["rstd_ready"], 1)
            dve.wait_ge(s["mod_ready"], 1)
            norm(0, gain[:, 0], lambda c: mod[:, c:c + 1], slot(3))

            dve.wait_ge(s["s5_in"], 16 * 9)
            ldt, dt, lrdt, ang, abr, abi, nr, den_, rcp, fr, fi, t0, t1 = (par[:, i, :] for i in range(13))
            a_re, a_im = col_a("a_re", 0, 8), col_a("a_im", 0, 8)
            angles, turns, rest, comp = (prep[:, i, :, :] for i in range(4))
            dve.wait_ge(s["dt_ready"], 1)
            v.tensor_tensor(lrdt, a_re, dt, ALU.mult).then_inc(s["lrdt_ready"], 1)
            step(v.tensor_tensor(ang, a_im, dt, ALU.mult))
            for j in range(LOGT):
                step(v.tensor_scalar(angles[:, :, j], ang, float(2**j), None, ALU.mult))
            step(v.tensor_scalar(turns, angles, 1 / (2 * np.pi), ROUND, ALU.mult, ALU.add))
            step(v.tensor_scalar(turns, turns, ROUND, None, ALU.subtract))
            step(v.scalar_tensor_tensor(rest, turns, -TWO_PI_PARTS[0], angles, ALU.mult, ALU.add))
            for part in TWO_PI_PARTS[1:]:
                step(v.scalar_tensor_tensor(rest, turns, -part, rest, ALU.mult, ALU.add))
            step(v.tensor_scalar(rest, rest, 3.1415925, -3.1415925, ALU.min, ALU.max))
            step(v.scalar_tensor_tensor(comp, rest, -1.0, rest, ALU.mult, ALU.min))
            v.tensor_scalar(comp, comp, np.pi / 2, None, ALU.add).then_inc(s["angle_ready"], 1)
            dve.wait_ge(s["turn_ready"], 1)
            cos1, sin1 = turn[:, 0, :, 0], turn[:, 1, :, 0]
            step(v.tensor_tensor(abr, mag[:], cos1, ALU.mult))
            step(v.tensor_tensor(abi, mag[:], sin1, ALU.mult))
            step(v.tensor_scalar(nr, abr, 1.0, None, ALU.subtract))
            step(v.tensor_tensor(den_, a_re, a_re, ALU.mult))
            step(v.tensor_tensor(t0, a_im, a_im, ALU.mult))
            step(v.tensor_tensor(den_, den_, t0, ALU.add))
            step(v.reciprocal(rcp, den_))
            for dst, x, y, op in ((fr, nr, abi, ALU.add), (fi, abi, nr, ALU.subtract)):
                step(v.tensor_tensor(t0, x, a_re, ALU.mult))
                step(v.tensor_tensor(t1, y, a_im, ALU.mult))
                step(v.tensor_tensor(t0, t0, t1, op))
                step(v.tensor_tensor(dst, t0, rcp, ALU.mult))

            def per_state(x):
                return x.unsqueeze(2).to_broadcast([P, STILES, GCH])

            tb = prep2
            for m, (x, y, op) in enumerate(((0, 1, ALU.subtract), (1, 0, ALU.add))):
                step(v.tensor_tensor(bb[:, m], b_in[:, x], per_state(fr), ALU.mult))
                step(v.tensor_tensor(tb[:], b_in[:, y], per_state(fi), ALU.mult))
                step(v.tensor_tensor(bb[:, m], bb[:, m], tb[:], op))

            dve.wait_ge(s["h_out"], 16)
            dve.wait_ge(s["u_ready"], KD)
            for cg in range(2):
                dve.wait_ge(s["gemm"], cg + 1)
                v.tensor_copy(us[:, cg, :], slot(cg)).then_inc(s["us_ready"], 1)
            dve.wait_ge(s["us_ready"], 2)

            cs, sn, wa, wb, wd, we, xre, xim = (s5[:, i, :] for i in range(8))
            def matrices(ch, t):
                if t:
                    dve.wait_ge(s["bct_done"], 4 * ch + t)
                else:
                    dve.wait_ge(s["bct_done"], 4 * ch)
                for m in range(2):
                    rep = bb[:, m, bass.ds(4 * ch + t, 1), :].to_broadcast([P, P // GCH, GCH])
                    step(v.tensor_tensor(bc[:, m, :].rearrange("p (a c) -> p a c", c=GCH),
                                         mask_b[:, t, :].rearrange("p (a c) -> p a c", c=GCH), rep, ALU.mult))
                rep = cc[:, 0, bass.ds(ch, 1), :].to_broadcast([P, 2, NSTATE])
                step(v.tensor_tensor(bc[:, 2, :].rearrange("p (a n) -> p a n", a=2),
                                     mask_c[:, t, :].rearrange("p (a n) -> p a n", a=2), rep, ALU.mult))
                rep = cc[:, 1, bass.ds(ch, 1), :].to_broadcast([P, 2, NSTATE])
                v.scalar_tensor_tensor(bc[:, 3, :].rearrange("p (a n) -> p a n", a=2), rep, -1.0,
                                       mask_c[:, t, :].rearrange("p (a n) -> p a n", a=2), ALU.mult, ALU.mult)\
                 .then_inc(s["bc_ready"], 1)

            with step.loop(2, 227) as ch:
                for m in range(2):
                    step(v.tensor_copy(cur[:, m], turn[:, m, bass.ds(4 * ch, 4), :]))
                step(v.tensor_copy(cmag[:], mag[:, bass.ds(4 * ch, 4)]))
                matrices(ch, 0)
                for t in range(4):
                    step(v.memset(cs[:, 0:1], 1.0))
                    step(v.memset(sn[:, 0:1], 0.0))
                    for j in range(LOGT):
                        n = 2**j
                        c1, s1 = cur[:, 0, t, j:j + 1], cur[:, 1, t, j:j + 1]
                        step(v.tensor_scalar(wa[:, 0:n], sn[:, 0:n], s1, None, ALU.mult))
                        step(v.tensor_scalar(wb[:, 0:n], cs[:, 0:n], s1, None, ALU.mult))
                        step(v.scalar_tensor_tensor(cs[:, n:2 * n], cs[:, 0:n], c1, wa[:, 0:n], ALU.mult, ALU.subtract))
                        step(v.scalar_tensor_tensor(sn[:, n:2 * n], sn[:, 0:n], c1, wb[:, 0:n], ALU.mult, ALU.add))
                    if t < 3:
                        matrices(ch, t + 1)
                    dve.wait_ge(s["bu_ready"], 8 * ch + 2 * t + 1)
                    step(v.tensor_tensor(wa, cs, slot(1), ALU.mult))
                    v.tensor_tensor(wb, sn, slot(1), ALU.mult).then_inc(s["bu_read"], 1)
                    dve.wait_ge(s["bu_ready"], 8 * ch + 2 * t + 2)
                    step(v.tensor_tensor(wd, sn, slot(2), ALU.mult))
                    v.tensor_tensor(we, cs, slot(2), ALU.mult).then_inc(s["bu_read"], 1)
                    dve.wait_ge(s["bu_read"], 8 * ch + 2 * t + 2)
                    step(v.tensor_tensor(wa, wa, wd, ALU.add))
                    step(v.tensor_tensor(we, we, wb, ALU.subtract))
                    decay = cmag[:, t:t + 1].to_broadcast([P, T])
                    step(v.tensor_tensor_scan(wd, decay, wa, 0.0, ALU.mult, ALU.add))
                    step(v.tensor_tensor_scan(wb, decay, we, 0.0, ALU.mult, ALU.add))
                    step(v.tensor_tensor(wa, cs, wd, ALU.mult))
                    step(v.tensor_tensor(we, sn, wb, ALU.mult))
                    if t:
                        dve.wait_ge(s["y_done"], 4 * ch + t)
                    else:
                        dve.wait_ge(s["y_done"], 4 * ch)
                    step(v.tensor_tensor(xre, wa, we, ALU.subtract))
                    step(v.tensor_tensor(wa, sn, wd, ALU.mult))
                    step(v.tensor_tensor(we, cs, wb, ALU.mult))
                    v.tensor_tensor(xim, wa, we, ALU.add).then_inc(s["x_ready"], 1)
                    dve.wait_ge(s["x_ready"], 4 * ch + t + 1)
                dve.wait_ge(s["y_done"], 4 * ch + 4)
                one = us[:, bass.ds(ch, 1), :].rearrange("p a n -> p (a n)")
                dst = yg[:, bass.ds(ch, 1), :].rearrange("p a n -> p (a n)")
                v.scalar_tensor_tensor(dst, one, cols_a[:, bass.ds(ch + at_a["d_skip"], 1)], slot(3), ALU.mult, ALU.add)\
                 .then_inc(s["y_read"], 1)
            for o in range(2):
                dve.wait_ge(s["sig_ready"], 2)
                v.tensor_tensor(yg[:, o, :], yg[:, o, :], gate_st[:, o, :], ALU.mult).then_inc(s["y_gated"], 1)

            dve.wait_ge(s["qkv_read"], 12)

            def head_bias(e):
                step(v.scalar_tensor_tensor(bias[:, e, :], delta[:], -4.0, log8[:], ALU.mult, ALU.add))
                step(v.tensor_scalar(delta[:], delta[:], 0.5, None, ALU.mult))

            def smallest(p, t):
                e, qb = tiles[t % NT]
                n = (qb + 1) * P
                dve.wait_ge(s["s_ready"], NT * p + t + 1)
                if t >= 3:
                    if t % 2:
                        dve.wait_ge(s["pt0"], NT * p + t - 3)
                    else:
                        dve.wait_ge(s["pt1"], QB * p + (t - 4) // 2 + 1)
                dve.sem_inc(s["passed"], 1)
                v.tensor_tensor_reduce(out=prob[:, t % 4, 0:n], in0=slot(t % 2)[:, 0:n],
                                       in1=bias[:, e, T - n:T], scale=-0.125, scalar=3e38,
                                       op0=ALU.add, op1=ALU.min,
                                       accum_out=neg_max[:, t % 4:t % 4 + 1]).then_inc(s["sm_ready"], 1)

            def near_half(p, t):
                n = min(tiles[t % NT][1] + 1, 4) * P
                dve.wait_ge(s["pt0"], NT * p + t + 1)
                if t >= 2:
                    dve.wait_ge(s["pv"], NT * p + t - 1)
                elif t:
                    dve.wait_ge(s["pv"], NT * p)
                v.tensor_copy(prob_t[:, t % 2, 0:n], slot(2)[:, 0:n]).then_inc(s["ptc0"], 1)

            def normalised(p, t):
                e, qb = tiles[t]
                dve.wait_ge(s["pv"], NT * p + t + 1)
                step(v.reciprocal(rden[:, t % 4:t % 4 + 1], den[:, t % 4:t % 4 + 1]))
                src = slot(3)[:, HALF * (t % 2):HALF * (t % 2) + HALF]
                if t % 4 == 3:
                    lo = 2 * N_ADA_EARLY + 2 * (t // 4)
                    dve.wait_ge(s["ada_done"], 4 * p + N_ADA_EARLY + t // 4 + 1)
                    v.tensor_tensor(mod[:, bass.ds(8 * p + lo, 2)], src[:, HD:HD + 2],
                                    cols_a[:, bass.ds(8 * p + lo + at_a["b_ada"], 2)], ALU.add)\
                     .then_inc(s["mod2_ready"], 1)
                v.tensor_scalar(o_tok[:, qb, bass.ds(P * p + HD * e, HD)], src[:, 0:HD],
                                rden[:, t % 4:t % 4 + 1], None, ALU.mult).then_inc(s["o_ready"], 1)

            def heads(p, last):
                for t in range(NT):
                    if t == 1:
                        dve.wait_ge(s["sm_ready"], NT * p)
                        head_bias(1)
                    if t == QB + 1 and not last:
                        dve.wait_ge(s["sm_ready"], NT * p + QB)
                        head_bias(0)
                    if t + 3 < NT or not last:
                        smallest(p, t + 3)
                    if t + 1 < NT or not last:
                        near_half(p, t + 1)
                    k, c = t // 4, 2 * (t % 4)
                    if c == 0:
                        dve.wait_ge(ada_in[k % 2], 32 * p + 16 * (k // 2 + 1))
                        dve.wait_ge(s["ada_done"], 4 * p + N_ADA_EARLY + max(k - 1, 0))
                    ada_sums(ada_part[:, k % 2], lambda c, k=k: raw[:, k % 2, c, :], (c, c + 1))
                    normalised(p, t)

            dve.wait_ge(s["k0_ready"], 2)
            for half in range(2):
                v.tensor_tensor(k_ll[HD * half:HD * half + HD, 0, :], qk[0:HD, KA, :], k_hh[0:HD, 0, :].bitcast(F32),
                                ALU.subtract).then_inc(s["k0_ready"], 1)
            dve.wait_ge(s["attn_in"], 32)
            head_bias(0)
            for t in range(3):
                smallest(0, t)
            near_half(0, 0)
            with step.loop(HEADS // 2 - 1, 4 + NT + 4 * (KD - 1)) as p:
                heads(p, False)
            heads(HEADS // 2 - 1, True)
            dve.wait_ge(s["mod2_ready"], 16)
            v.scalar_tensor_tensor(gain[:, 1], mod[:, 4 * KD:5 * KD], 1.0, col_a("g_ffn", 0, KD), ALU.add, ALU.mult)\
             .then_inc(s["mod_ready"], 1)

            for o in range(2):
                dve.wait_ge(s["ysh"], o + 1)
                v.tensor_tensor(ys_l[:, o, :], yg[:, o, :], ys_h[:, o, :].bitcast(F32), ALU.subtract).then_inc(s["ys_ready"], 1)
            for c in range(KA):
                dve.wait_ge(s["oh_ready"], c + 1)
                v.tensor_tensor(in2_l[:, c, :], slot(c), in2_h[:, c, :].bitcast(F32), ALU.subtract).then_inc(s["ot_ready"], 1)

            dve.wait_ge(s["ys_ready"], 2)
            with step.loop(2, 4) as i:
                for b in range(2):
                    for cg in range(2):
                        c = 2 * b + cg
                        dve.wait_ge(gate_back[cg], 64 * i + 32 * (b + 1))
                        dve.wait_ge(s["gemm"], 8 * i + units_before(N_PROJ) + 4 * b + 2 * cg + 2)
                        step(v.tensor_tensor(mix[:, 0, :], slot(2 * cg), gate_in[:, cg, 0, :], ALU.mult))
                        v.tensor_tensor(mix[:, 1, :], slot(2 * cg + 1), gate_in[:, cg, 1, :], ALU.mult)\
                         .then_inc(s["proj_read"], 1)
                        dve.wait_ge(s["proj_read"], 4 * i + c + 1)
                        v.tensor_tensor(mix[:, 0, :], mix[:, 0, :], mix[:, 1, :], ALU.add).then_inc(s["mix_ready"], 1)
                        dve.wait_ge(s["mh_ready"], 4 * i + c + 1)
                        v.tensor_tensor(act_l[:, bass.ds(4 * i + c, 1), :].rearrange("p a n -> p (a n)"), mix[:, 0, :],
                                        act_h[:, bass.ds(4 * i + c, 1), :].rearrange("p a n -> p (a n)").bitcast(F32),
                                        ALU.subtract).then_inc(s["merged_ready"], 1)
                        dve.wait_ge(s["merged_ready"], 4 * i + c + 1)

            for c in range(KD):
                dve.wait_ge(h_back[c // 4], 16)
                dve.wait_ge(s["gemm"], units_before(N_OUT) + c + 1)
                v.scalar_tensor_tensor(h_t[:, c, :], slot(c % 4), mod[:, 2 * KD + c:2 * KD + c + 1], h_t[:, c, :],
                                       ALU.mult, ALU.add).then_inc(s["out_read"], 1)
                if c >= 2:
                    add_square(1, c - 1)
            add_square(1, KD - 1)
            one_over_root(2)
            on_diagonal(0, stat[:, 1, :])
            dve.wait_ge(s["rstd_ready"], 2)
            dve.wait_ge(s["out_read"], KD)
            norm(1, gain[:, 1], lambda c: mod[:, 3 * KD + c:3 * KD + c + 1], slot(3))

            base_f = units_before(N_FFN)
            def quarter(q, last):
                for p in range(2):
                    for cg in range(2):
                        c = 2 * p + cg
                        dve.wait_ge(s["acc_ready"], 4 * q + c + 1)
                        for j in range(1, CONV):
                            ins = v.scalar_tensor_tensor(
                                conv[:, cg, j:T], slot(cg)[:, 0:T - j],
                                cols_b[:, bass.ds(4 * q + (at_b["w_conv"] + j * (FF // P) + c), 1)],
                                conv[:, cg, j:T], ALU.mult, ALU.add)
                            if j < CONV - 1:
                                step(ins)
                            else:
                                ins.then_inc(s["a_read"], 1)
                    for cg in range(2):
                        c = 2 * p + cg
                        dve.wait_ge(s["silu_ready"], 4 * q + c + 1)
                        dve.wait_ge(s["gemm"], 16 * q + base_f + 4 * p + 2 + cg + 1)
                        if c:
                            dve.wait_ge(s["f_ready"], 4 * q + c)
                        else:
                            dve.wait_ge(s["f_ready"], 4 * q)
                        v.tensor_tensor(ffn[:], slot(2 + cg), conv[:, cg, :], ALU.mult).then_inc(s["v_read"], 1)
                        dve.wait_ge(s["fh_ready"], 4 * q + c + 1)
                        v.tensor_tensor(in2_l[:, c, :], ffn[:], in2_h[:, c, :].bitcast(F32), ALU.subtract)\
                         .then_inc(s["f_ready"], 1)
                for u in range(KD):
                    dve.wait_ge(s["gemm"], 16 * q + base_f + 8 + u + 1)
                    if u == 0:
                        dve.wait_ge(s["down_read"], 8 * q)
                    v.scalar_tensor_tensor(h_t[:, u, :], slot(u % 4), mod[:, 5 * KD + u:5 * KD + u + 1], h_t[:, u, :],
                                           ALU.mult, ALU.add).then_inc(s["down_read"], 1)
                    if last and u >= 2:
                        add_squares(u - 1)

            def add_squares(c):
                for m in range(2):
                    dve.wait_ge(s["sq_ready"], 2 * KD + 2 * c + m + 1)
                    if c >= 2:
                        dve.wait_ge(s["sq_used"], 2 * (KD - 1) + 2 * (c - 2) + m + 1)
                    v.tensor_tensor(acc2[:, m, :], acc2[:, m, :], sq[:, m, :], ALU.add).then_inc(s["sq_used"], 1)

            with step.loop(3, 4) as q:
                quarter(q, False)
            quarter(3, True)
            add_squares(KD - 1)

            step(v.tensor_tensor(gain2[:], col_b("g_final", 0, KD), col_b("norm_g_2", 0, KD), ALU.mult))
            one_over_root(3)
            r1 = stat[:, 1, :]
            step(v.tensor_tensor(stat[:, 2, :], r1, r1, ALU.mult))
            v.tensor_tensor(stat[:, 2, :], stat[:, 2, :], slot(3)[:, QB:2 * QB], ALU.mult).then_inc(s["ms2_ready"], 1)
            dve.wait_ge(s["sq_used"], 4 * (KD - 1))
            on_diagonal(1, r1)
            dve.wait_ge(s["std_ready"], 4)
            step(v.reciprocal(stat[:, 4, :], stat[:, 3, :]))
            step(v.tensor_tensor(stat[:, 5, :], stat[:, 4, :], r1, ALU.mult))
            on_diagonal(0, stat[:, 5, :])
            dve.wait_ge(s["rstd2_ready"], 1)
            dve.wait_ge(s["down_read"], 32)
            norm(2, gain2, None, rstd2[:, 0, :])
            dve.wait_ge(s["rstd2_ready"], 2)
            for c in range(KD):
                v.scalar_tensor_tensor(h_t[:, c, :], h_t[:, c, :], col_b("g_final", c), rstd2[:, 1, :], ALU.mult, ALU.mult)\
                 .then_inc(s["x2_ready"], 1)

            dve.wait_ge(s["v2_read"], 4)
            for t in range(QB):
                step(v.bn_stats(bn[:, t, :], vg[:, t, :]))
                step(v.bn_aggr(bn_mv[:, t, :], bn[:, t, :]))
            v.tensor_scalar(ln_rstd[:], bn_mv[:, :, 1], LN_EPS, None, ALU.add).then_inc(s["ln_var"], 1)
            dve.wait_ge(s["ln_std"], 1)
            step(v.reciprocal(ln_rstd[:], ln_rstd[:]))
            dve.wait_ge(s["late_in"], 16 * 13)
            for t in range(QB):
                step(v.tensor_scalar(vg[:, t, :], vg[:, t, :], bn_mv[:, t, 0:1], ln_rstd[:, t:t + 1],
                                     ALU.subtract, ALU.mult))
                step(v.tensor_tensor(vg[:, t, :], vg[:, t, :], ln_g[:], ALU.mult))
                ins = v.tensor_tensor(vg[:, t, :], vg[:, t, :], ln_b[:], ALU.add)
                if t < QB - 1:
                    step(ins)
                else:
                    ins.then_inc(s["vn_ready"], 1)
            dve.wait_ge(s["wst_done"], 1)
            v.tensor_copy(wst[:].rearrange("p g t -> p (g t)"), slot(2)).then_inc(s["wst_ready"], 1)

            for c in range(K2):
                cg = c % 2
                dve.wait_ge(s["sg_done"], c + 1)
                if c:
                    dve.wait_ge(s["a_ready"], c)
                v.tensor_tensor(a_s[:].rearrange("p (n t) -> p n t", t=P), slot(2 + cg).rearrange("p (n t) -> p n t", t=P),
                                bs_row[:, c:c + 1, :].to_broadcast([P, QB, P]), ALU.add).then_inc(s["sg_read"], 1)
                dve.wait_ge(s["sg_read"], c + 1)
                dve.wait_ge(s["au_read"], c + 1)
                step(v.tensor_tensor(a_s[:], a_s[:], a_u[:, cg, :], ALU.mult))
                dve.wait_ge(s["az_read"], c + 1)
                v.tensor_tensor(a_s[:], a_s[:], a_z[:, cg, :], ALU.mult).then_inc(s["ap_ready"], 1)
                dve.wait_ge(s["ah_ready"], c + 1)
                v.tensor_tensor(in2_l[:, c, :], a_s[:], in2_h[:, c, :].bitcast(F32), ALU.subtract).then_inc(s["a_ready"], 1)

            def gated(n0, sig, p_read, done, add, trips=4):
                with step.loop(trips, 0) as j:
                    for cg in range(2):
                        m = merged[:, bass.ds(2 * j + cg, 1), :].rearrange("p a n -> p (a n)")
                        dve.wait_ge(sig, 2 * j + cg + 1)
                        dve.wait_ge(s["gemm"], 4 * j + units_before(n0 + 1) + cg + 1)
                        if not add:
                            v.tensor_tensor(m, br[:, cg, :], slot(2 + cg), ALU.mult).then_inc(p_read, 1)
                            continue
                        v.tensor_tensor(br[:, cg, :], br[:, cg, :], slot(2 + cg), ALU.mult).then_inc(p_read, 1)
                        dve.wait_ge(p_read, 2 * j + cg + 1)
                        v.tensor_tensor(m, m, br[:, cg, :], ALU.add).then_inc(done, 1)

            for half in range(2):
                dve.wait_ge(x2_out[half], 16)
            dve.wait_ge(s["a_ready"], K2)
            gated(N_GA, s["sa_ready"], s["pa_read"], None, False)

            base_b = units_before(N_B)
            for p in range(2):
                for cg in range(2):
                    dve.wait_ge(s["xb_read"], 2 * p + cg + 1)
                    dve.wait_ge(s["gemm"], base_b + 8 * p + 2 + cg + 1)
                    v.tensor_tensor(br[:, cg, :], br[:, cg, :], slot(2 + cg), ALU.mult).then_inc(s["bc_read"], 1)
                for cg in range(2):
                    c = 2 * p + cg
                    y, taps = br[:, cg, :], br2

                    def tap(j, c=c):
                        return col_b("conv_w_2", j * K2 + c)

                    dve.wait_ge(s["bc_read"], c + 1)
                    if c:
                        dve.wait_ge(s["b_ready"], c)
                    step(v.tensor_scalar(taps[:], y, tap(2), col_a("conv_b_2", c), ALU.mult, ALU.add))
                    step(v.scalar_tensor_tensor(taps[:, 1:T], y[:, 0:T - 1], tap(1), taps[:, 1:T], ALU.mult, ALU.add))
                    step(v.scalar_tensor_tensor(taps[:, 2:T], y[:, 0:T - 2], tap(0), taps[:, 2:T], ALU.mult, ALU.add))
                    dve.wait_ge(s["gemm"], base_b + 8 * p + 4 + cg + 1)
                    v.tensor_tensor(y, taps[:], slot(cg), ALU.mult).then_inc(s["bg_read"], 1)
                    dve.wait_ge(s["bg_read"], c + 1)
                    dve.wait_ge(s["bz_read"], c + 1)
                    v.tensor_tensor(y, y, taps[:], ALU.mult).then_inc(s["bp_ready"], 1)
                    dve.wait_ge(s["bh_ready"], c + 1)
                    v.tensor_tensor(in2_l[:, c, :], y, in2_h[:, c, :].bitcast(F32), ALU.subtract).then_inc(s["b_ready"], 1)
            dve.wait_ge(s["pa_read"], KD)
            dve.wait_ge(s["b_ready"], K2)
            gated(N_GB, s["sb_ready"], s["pb_read"], s["mb_ready"], True)

            for p in range(2):
                for cg in range(2):
                    c = 2 * p + cg
                    x, other = br[:, 0, :], br2
                    dve.wait_ge(s["xc_read"], c + 1)
                    if c >= 2:
                        dve.wait_ge(s["pool_done"], c)
                    src, dst = x, other[:]
                    for j in range(c + 1):
                        h = 2**j
                        step(v.tensor_copy(dst[:, 0:h], src[:, 0:h]))
                        step(v.tensor_tensor(dst[:, h:T], src[:, h:T], src[:, 0:T - h], ALU.add))
                        src, dst = dst, src
                    res = pool_in[cg]
                    step(v.scalar_tensor_tensor(res[:, 16:T], src[:, 16:T], 1.0 / WINDOWS[c], slot(cg)[:, 16:T],
                                                ALU.mult, ALU.subtract))
                    step(v.tensor_tensor(src[:, 0:16], src[:, 0:16], inv[:, c, :], ALU.mult))
                    v.tensor_tensor(res[:, 0:16], src[:, 0:16], slot(cg)[:, 0:16], ALU.subtract).then_inc(s["pooled"], 1)
                    dve.wait_ge(s["pooled"], c + 1)
                for cg in range(2):
                    c = 2 * p + cg
                    z = br[:, cg, :]
                    dve.wait_ge(s["pool_done"], c + 1)
                    dve.wait_ge(s["cz_read"], c + 1)
                    v.scalar_tensor_tensor(z, slot(cg), col_b("pool_scale_2", c), z, ALU.mult, ALU.mult)\
                     .then_inc(s["cp_ready"], 1)
                    dve.wait_ge(s["ch_ready"], c + 1)
                    v.tensor_tensor(in2_l[:, c, :], z, in2_h[:, c, :].bitcast(F32), ALU.subtract).then_inc(s["ch_done"], 1)
            dve.wait_ge(s["mb_ready"], KD)
            dve.wait_ge(s["ch_done"], K2)
            gated(N_GC, s["sc_ready"], s["pc_read"], s["mc_ready"], True, 3)

            def merged_low(c):
                dve.wait_ge(s["m2_high"], c + 1)
                v.tensor_tensor(act_l[:, c, :], merged[:, c, :], act_h[:, c, :].bitcast(F32), ALU.subtract)\
                 .then_inc(s["m2_ready"], 1)

            for c in range(KD - 2):
                merged_low(c)
            for c in (KD - 2, KD - 1):
                cg = c % 2
                dve.wait_ge(s["sc_ready"], c + 1)
                dve.wait_ge(s["gemm"], units_before(N_WO) - 1 + cg)
                v.tensor_tensor(br[:, cg, :], br[:, cg, :], slot(2 + cg), ALU.mult).then_inc(s["pc_read"], 1)
                dve.wait_ge(s["pc_read"], c + 1)
                v.tensor_tensor(merged[:, c, :], merged[:, c, :], br[:, cg, :], ALU.add).then_inc(s["mc_ready"], 1)
            for c in (KD - 2, KD - 1):
                merged_low(c)
            for c in range(KD):
                dve.wait_ge(x2_back[c // 4], 16)
                dve.wait_ge(s["gemm"], units_before(N_WO) + c + 1)
                v.tensor_tensor(y_t[:, c, :], y_t[:, c, :], slot(c % 4), ALU.add).then_inc(s["y_ready"], 1)
            dve.wait_ge(s["g_row_in"], 16)
            for t in range(QB):
                dve.wait_ge(s["ostd"], t + 1)
                step(v.reciprocal(o_ssq[:, 2, t:t + 1], o_ssq[:, 1, t:t + 1]))
                if t >= 2:
                    dve.wait_ge(row_out[t % 2], 16 * (t // 2))
                v.scalar_tensor_tensor(o_row[:, t % 2, :], slot(t % 4), o_ssq[:, 2, t:t + 1], g_row[:],
                                       ALU.mult, ALU.mult).then_inc(s["orow"], 1)


def kernel(**inputs):
    import concourse.bacc as bacc
    from concourse.bass_utils import run_bass_kernel_spmd

    nc = bacc.Bacc("TRN2", target_bir_lowering=False, num_devices=1)
    arrays, aps = {}, {}
    for name, value in {**inputs, **constants()}.items():
        value = np.ascontiguousarray(value)
        arrays[f"in_{name}"] = value
        aps[name] = nc.dram_tensor(f"in_{name}", value.shape, mybir.dt.from_np(value.dtype), kind="ExternalInput").ap()
    out = nc.dram_tensor("out", (1, T, D), F32, kind="ExternalOutput").ap()
    build(nc, aps, out)
    return run_bass_kernel_spmd(nc, [arrays], core_ids=[0]).results[0]["out"]
```

```python
from contextlib import ExitStack, contextmanager

import numpy as np

import concourse.bass as bass
from concourse import mybir

ACT = mybir.ActivationFunctionType
ALU = mybir.AluOpType
F32 = mybir.dt.float32
F32R = mybir.dt.float32r

P = 128
T = 1024
D = 1024
KD = D // P
HALF = 512
NB = 256
HEADS, HD = 8, 64
ATT = HEADS * HD
KA = ATT // P
SSM = 256
GROUPS, GCH, NSTATE = 16, 16, 64
STILES = GROUPS * NSTATE // P
LOGT = 10
LOGS = 6
SHORT = 2**LOGS
FF = 2048
CONV = 3
W2 = 512
K2 = W2 // P
QB = T // P
WINDOWS = (2, 4, 8, 16)
RMS_EPS, LN_EPS = 1e-6, 1e-5
TWO_PI_PARTS = (6.28125, 4058 / 2**21, 2 * np.pi - 6.28125 - 4058 / 2**21)
ROUND = 1.5 * 2**23
MASKED = -1e30

N_US, N_GATE, N_QKV, N_PROJ, N_OUT, N_FFN = 0, 1, 9, 15, 19, 23
N_V2, N_A, N_GA, N_B, N_GB, N_C, N_GC, N_WO, N_END = 55, 57, 61, 69, 77, 85, 89, 97, 101
N_ADA_EARLY, N_ADA = 8, 24
SUMMED = 2


def units_before(n):
    return 2 * n if n <= N_PROJ else 30 + 4 * (n - N_PROJ) if n <= N_OUT else 2 * n + 8


ROWS_A = dict(b_ada=48, g_mix=8, b_gate=16, g_ffn=8, b_conv=16, c=8, a_re=8, a_im=8, d_skip=2, b_glu=2,
              conv_b_2=4)
ROWS_B = dict(w_conv=48, g_final=8, norm_g_2=8, conv_w_2=12, pool_scale_2=4)


def places(rows):
    at, out = 0, {}
    for name, n in rows.items():
        out[name] = at
        at += n
    return out, at


AHEAD = 1
RAISED = """gate_read bu_read qkv_read o_ready proj_read out_read down_read y_ready pv f_ready pa_read
    pb_read pc_read mb_ready mc_ready bct_done y_done sa_ready sb_ready sc_ready pt0 sm_ready""".split()


class Steps:

    def __init__(self, eng, sem):
        self.eng, self.sem, self.base, self.n = eng, sem, 0, 0

    def __call__(self, ins):
        ins.then_inc(self.sem, 1)
        self.n += 1
        self.eng.wait_ge(self.sem, self.base + self.n)

    @contextmanager
    def loop(self, trips, per):
        start = self.base + self.n
        with self.eng.Fori(0, trips) as i:
            self.base, self.n = i * per + start, 0
            yield i
            assert self.n == per, (self.n, per)
        self.base, self.n = start + trips * per, 0


def constants():
    p, x = np.arange(P)[:, None], np.arange(T)[None, :]
    delta = p + (T - P) - x
    count = ((delta >= 0) & (delta <= 128)).astype(np.float64)
    count += (delta >= 0) & (delta <= 512) & (delta % 4 == 0)
    count += (delta >= 0) & (delta <= 2048) & (delta % 16 == 0)
    log8 = np.where(count > 0, 8 * np.log(np.maximum(count, 1)), MASKED)
    ch, st = np.arange(P)[None, None, :], np.arange(P)[:, None, None]
    k = np.arange(4)[None, :, None]
    mask_b = (ch // GCH == 2 * k + st // NSTATE)
    mask_c = mask_b.transpose(2, 1, 0)
    inv = np.stack([1.0 / np.minimum(np.arange(1, 17), w) for w in WINDOWS])
    return dict(
        k_ident=np.eye(P, dtype=np.float32),
        k_delta=np.ascontiguousarray(delta, np.float32),
        k_log8=np.ascontiguousarray(log8, np.float32),
        k_mask_b=np.ascontiguousarray(mask_b, np.float32),
        k_mask_c=np.ascontiguousarray(mask_c, np.float32),
        k_inv=np.ascontiguousarray(np.broadcast_to(inv[None], (P, 4, 16)), np.float32),
    )


def build(nc, a, out):
    ctx = ExitStack()
    with ctx:
        base = -(-nc.sbuf_base // 32) * 32
        kib = 1024

        def at(name, shape, offset, dt=F32):
            return nc.alloc_sbuf_tensor_at(name, shape, dt, offset=base + offset)

        fence = ctx.enter_context(nc.sbuf_tensor("fence", [P, (nc.sbuf_top - base) // 4], F32))

        act_h = at("act_h", [P, KD, T], 0, F32R)
        act_l = at("act_l", [P, KD, T], 32 * kib, F32R)
        w_h = at("w_h", [P, 2, KD, NB], 64 * kib, F32R)
        w_l = at("w_l", [P, 2, KD, NB], 80 * kib, F32R)
        in2_h = at("in2_h", [P, 4, T], 96 * kib, F32R)
        in2_l = at("in2_l", [P, 4, T], 112 * kib, F32R)
        raw = at("raw", [P, 2, KD, NB], 128 * kib)

        CONST = 144 * kib
        spot = [CONST]

        def keep(name, shape, dt=F32):
            n = int(np.prod(shape[1:])) * 4
            t = at(name, shape, spot[0], dt)
            spot[0] += -(-n // 32) * 32
            return t

        ident = keep("ident", [P, P])
        ones = keep("ones", [P, P])
        cols_a = keep("cols_a", [P, P])
        cols_b = keep("cols_b", [P, P])
        mod = keep("mod", [P, 48])
        eps_rms = keep("eps_rms", [P, 1])
        gain = keep("gain", [P, 2, KD])
        c_act = keep("c_act", [P, KD])
        late = spot[0]
        mask_b = keep("mask_b", [P, 4, P])
        mask_c = keep("mask_c", [P, 4, P])
        bb = keep("bb", [P, 2, STILES, GCH])
        cc = keep("cc", [P, 2, 2, NSTATE])
        mag = keep("mag", [P, STILES])
        turn = keep("turn", [P, 2, STILES, LOGT])
        cur = keep("cur", [P, 2, 4, LOGT])
        cmag = keep("cmag", [P, 4])
        bct_place = spot[0]
        bct = keep("bct", [P, 2, 4, P])
        w_glu = keep("w_glu", [P, 2, SSM])
        assert spot[0] <= 160 * kib, spot[0] / kib
        spot[0] = late
        wst = keep("wst", [P, 8, P])
        ln_g = keep("ln_g", [P, W2])
        ln_b = keep("ln_b", [P, W2])
        bs_row = keep("bs_row", [P, K2, P])
        w_pool = keep("w_pool", [P, 4, P])
        inv = keep("inv", [P, 4, 16])
        bn = keep("bn", [P, QB, 6])
        bn_mv = keep("bn_mv", [P, QB, 2])
        ln_rstd = keep("ln_rstd", [P, QB])
        assert spot[0] <= 160 * kib, spot[0] / kib

        x_tok = at("x_tok", [P, QB, D], 96 * kib)
        rows = at("rows", [P, 2, P], 200 * kib)
        prep = at("prep", [P, 4, STILES, LOGT], bct_place)
        b_in = at("b_in", [P, 2, STILES, GCH], 201 * kib)
        prep2 = at("prep2", [P, STILES, GCH], 202 * kib + 512)
        par = at("par", [P, 13, STILES], 202 * kib)
        h_t = at("h_t", [P, KD, T], 160 * kib)
        ada_w = at("ada_w", [P, N_ADA_EARLY, KD, NB], 0)
        sq = at("sq", [P, 2, T], 192 * kib)
        diag = [at(f"diag{i}", [P, QB, P], (192 + 4 * i) * kib) for i in range(2)]
        acc = at("acc", [P, T], 203 * kib)
        acc2 = at("acc2", [P, 2, T], 56 * kib)
        stat = at("stat", [P, 6, QB], 207 * kib)
        gain2 = at("gain2", [P, KD], 207 * kib + 192)
        slopes = at("slopes", [P, HEADS], 207 * kib + 224)
        nrm = at("nrm", [P, 2, T], 104 * kib)
        rstd2 = at("rstd2", [P, 2, T], 112 * kib)
        qk = at("qk", [P, 2 * KA, T], 96 * kib)
        s5 = at("s5", [P, 8, T], 96 * kib)
        turns0 = at("turns0", [P, 2, STILES, SHORT], 203 * kib)
        part0 = at("part0", [P, 2, 2, STILES, SHORT // 2], 96 * kib)
        yg = at("yg", [P, 2, T], 160 * kib)
        v_tok = at("v_tok", [P, QB, ATT], 168 * kib)
        us = at("us", [P, 2, T], 184 * kib)
        gate_st = at("gate_st", [P, 2, T], 192 * kib)
        bc = at("bc", [P, 4, P], 200 * kib)
        o_tok = at("o_tok", [P, QB, ATT], 184 * kib)
        q2 = at("q2", [P, 2, T], 0, F32R)
        k_hh = at("k_hh", [P, 2, T], 8 * kib, F32R)
        k_ll = at("k_ll", [P, 2, T], 16 * kib, F32R)
        v_st = at("v_st", [P, 2, QB, HD], 24 * kib)
        prob = at("prob", [P, 4, T], 28 * kib)
        prob_t = at("prob_t", [P, 2, T], 44 * kib)
        bias = at("bias", [P, 2, T], 52 * kib)
        delta = at("delta", [P, T], 60 * kib)
        log8 = at("log8", [P, T], 64 * kib)
        neg_max = at("neg_max", [P, 4], 204 * kib)
        ada_part = at("ada_part", [P, 2, NB], 205 * kib)
        den = at("den", [P, 4], 204 * kib + 32)
        rden = at("rden", [P, 4], 204 * kib + 64)
        proj_raw = at("proj_raw", [P, KA + 2, NB], 96 * kib)
        ys_h = at("ys_h", [P, 2, T], 168 * kib, F32R)
        ys_l = at("ys_l", [P, 2, T], 176 * kib, F32R)
        gate_in = at("gate_in", [P, 2, 2, T], 184 * kib)
        mix = at("mix", [P, 2, T], 160 * kib)
        conv = at("conv", [P, 2, T], 192 * kib)
        ffn = at("ffn", [P, T], 200 * kib)
        ws_tok = at("ws_tok", [P, T], 120 * kib)
        vg = at("vg", [P, QB, W2], 160 * kib)
        a_u = at("a_u", [P, 2, T], 176 * kib)
        a_z = at("a_z", [P, 2, T], 184 * kib)
        a_s = at("a_s", [P, T], 192 * kib)
        merged = at("merged", [P, KD, T], 160 * kib)
        br = at("br", [P, 2, T], 192 * kib)
        br2 = at("br2", [P, T], 200 * kib)
        pool_in = [br[:, 1, :], br2[:]]
        y_t = at("y_t", [P, KD, T], 160 * kib)
        o_row = at("o_row", [P, 2, D], 192 * kib)
        g_row = at("g_row", [P, D], 200 * kib)
        o_sq = at("o_sq", [P, D], 64 * kib)
        o_ssq = at("o_ssq", [P, 3, QB], 68 * kib)

        tiles = [(hh, qb) for hh in range(2) for long in range(QB - 1, QB // 2 - 1, -1) for qb in (long, QB - 1 - long)]
        NT = len(tiles)
        STAGED = 7

        ps = ctx.enter_context(nc.psum_tensor("ps", [P, 4, T], F32))

        gates_d = nc.dram_tensor("gates_scratch", [2 * KD, P, T], F32).ap()
        h_d = nc.dram_tensor("h_scratch", [KD, P, T], F32).ap()
        x2_d = nc.dram_tensor("x2_scratch", [KD, P, T], F32).ap()

        names = """vec_in const_in x_in late_in attn_in g_row_in dve act colt colt_read c_ready consts_ready tr
            h_ready h_out ada_done mod_ready mod_read sq_ready sq_used std_ready rstd_ready t_ready hi_ready
            u_ready w_high w_half w_split gemm us_ready gate_read bc_ready bct_done bct_copied bu_ready bu_read
            x_ready y_done y_read yg_ready qkv_read glu_done sig_ready ys_ready staged s_ready sm_ready
            p_ready pt0 pt1 ptc0 ptc1 pv o_ready otr oh_ready ot_ready ysh proj_read mix_ready mh_ready
            merged_ready out_read acc_ready silu_ready a_read v_read fh_ready f_ready down_read x2_ready
            sums_ready ada_summed gate_half ada_row row_copied ptshort k0_ready ms2_ready diag_ready rstd2_ready wst_done wst_ready wst_masked v2_read vn_ready au_read sg_done sg_read az_read ap_ready
            ah_ready a_ready xb_read bc_read bz_read bg_read bp_ready bh_ready b_ready xc_read pooled
            pool_done cz_read cp_ready ch_ready sa_ready pa_read sb_ready pb_read mb_ready sc_ready pc_read
            mc_ready m2_high m2_ready s5_in dt_ready lrdt_ready angle_ready turn_ready mod2_ready passed
            ln_var ln_std ch_done y_gated y_ready otr2 ostd orow""".split()
        s = {n: ctx.enter_context(nc.semaphore(n)) for n in names}

        def pair(name, n=2):
            return [ctx.enter_context(nc.semaphore(f"{name}{i}")) for i in range(n)]

        ada_in, w_in_, ws_in = pair("ada_in"), pair("w_in"), pair("ws_in")
        gate_out, gate_back = pair("gate_out"), pair("gate_back")
        h_back, x2_back, row_out = pair("h_back"), pair("x2_back"), pair("row_out")
        ada0_in, x2_out = pair("ada0_in", N_ADA_EARLY // 2), pair("x2_out")

        at_a, n_a = places(ROWS_A)
        at_b, n_b = places(ROWS_B)
        assert n_a == P

        def col_a(name, j=0, n=1):
            return cols_a[:, at_a[name] + j:at_a[name] + j + n]

        def col_b(name, j=0, n=1):
            return cols_b[:, at_b[name] + j:at_b[name] + j + n]

        def weights(name, col, n=NB, row=0, k=KD):
            w = a[name][0]
            return w[row:row + k * P, :].rearrange("(k p) n -> p k n", p=P)[:, :, col]

        def slot(i):
            return ps[:, i, :]

        block = ctx.enter_context(nc.Block())

        @block.sync
        def _(sp):
            sp.dma_start(ident[:], a["k_ident"]).then_inc(s["const_in"], 16)
            sp.dma_start(x_tok[:], a["x"][0].rearrange("(t p) d -> p t d", p=P)).then_inc(s["x_in"], 16)
            for t, rr in enumerate((ROWS_A, ROWS_B)):
                for name, r0 in places(rr)[0].items():
                    v = a[name]
                    v = v.flatten() if len(v.shape) > 1 else v
                    sp.dma_start(rows[r0:r0 + rr[name], t, :],
                                 v.rearrange("(r p) -> r p", p=P)).then_inc(s["vec_in"], 16)
            for b in range(0, N_ADA_EARLY, 2):
                for k in range(2):
                    sp.dma_start(ada_w[:, b + k, :, :], weights("w_ada", bass.ds((b + k) * NB, NB)))\
                      .then_inc(ada0_in[b // 2], 16)
            for k in range(2):
                sp.dma_start(raw[:, k, :, :], weights("w_in", bass.ds(3 * ATT + SSM * k, NB))).then_inc(w_in_[k], 16)

            for sem in [s[n] for n in RAISED] + gate_out:
                sp.sem_inc(sem, AHEAD)

            def ada(b, k):
                sp.dma_start(raw[:, k, :, :], weights("w_ada", bass.ds(b * NB, NB))).then_inc(ada_in[k], 16)

            def load(n, k, name, col, row=0, kc=KD):
                sp.wait_ge(s["w_split"], n - 1)
                sp.sem_inc(s["passed"], 1)
                sp.dma_start(raw[:, k, 0:kc, :],
                             weights(name, bass.ds(col, NB), row=row, k=kc)).then_inc(w_in_[k], 16)

            load(2, 0, "w_in", 3 * ATT + SSM + NB)
            with sp.Fori(0, 3) as i:
                for k in range(2):
                    load(2 * i + 3 + k, 1 - k, "w_in", i * (2 * NB) + 3 * ATT + SSM + (2 + k) * NB)
            with sp.Fori(0, 3) as i:
                for k in range(2):
                    load(2 * i + N_QKV + k, 1 - k, "w_in", i * (2 * NB) + k * NB)
            sp.wait_ge(s["w_split"], N_PROJ)
            for b in range(N_ADA_EARLY, N_ADA_EARLY + 2):
                ada(b, b % 2)
            sp.wait_ge(s["gemm"], units_before(N_PROJ))
            sp.dma_start(delta[:], a["k_delta"]).then_inc(s["attn_in"], 16)
            sp.dma_start(log8[:], a["k_log8"]).then_inc(s["attn_in"], 16)
            with sp.Fori(0, (N_ADA - N_ADA_EARLY - 2) // 2) as i:
                for k in range(2):
                    sp.wait_ge(s["ada_summed"], 2 * i + SUMMED + k + 1)
                    sp.sem_inc(s["passed"], 1)
                    ada(2 * i + N_ADA_EARLY + 2 + k, k)

            def proj(j, k):
                sp.dma_start(raw[:, k, 0:KA, :],
                             weights("w_proj_att", bass.ds(j * NB, NB), k=KA)).then_inc(w_in_[k], 16)
                sp.dma_start(raw[:, k, KA:KA + 2, :],
                             weights("w_proj_ssm", bass.ds(j * NB, NB), k=2)).then_inc(ws_in[k], 16)

            def gates(j):
                for cg in range(2):
                    if j:
                        sp.wait_ge(s["proj_read"], AHEAD + 2 * j + cg - 1)
                    for g in range(2):
                        sp.dma_start(gate_in[:, cg, g, :], gates_d[g * KD + 2 * j + cg]).then_inc(gate_back[cg], 16)

            sp.wait_ge(s["ada_summed"], SUMMED + N_ADA - N_ADA_EARLY)
            proj(1, 0)
            for k in range(2):
                sp.wait_ge(gate_out[k], AHEAD + 16 * KD)
            sp.wait_ge(s["oh_ready"], KA)
            sp.wait_ge(s["ot_ready"], KA)
            gates(0)
            for j in range(2, 4):
                gates(j - 1)
                sp.wait_ge(s["w_split"], N_PROJ + j - 1)
                proj(j, 1 - j % 2)
            load(N_OUT, 1, "w_out", 0)
            gates(3)
            load(N_OUT + 1, 0, "w_out", NB)
            sp.wait_ge(s["h_out"], 16)
            sp.wait_ge(s["gemm"], units_before(N_OUT))
            sp.wait_ge(s["merged_ready"], KD)
            for half in range(2):
                sp.dma_start(h_t[:, 4 * half:4 * half + 4, :], h_d[4 * half:4 * half + 4].rearrange("c p t -> p c t"))\
                  .then_inc(h_back[half], 16)
            for k in range(2):
                load(N_OUT + 2 + k, 1 - k, "w_out", (2 + k) * NB)

            with sp.Fori(0, 4) as q:
                for p in range(2):
                    for k in range(2):
                        load(8 * q + N_FFN + 2 * p + k, 1 - k, "w_up", q * 512 + (k * FF + p * NB))
                for p in range(2):
                    for k in range(2):
                        n = 8 * q + N_FFN + 4 + 2 * p + k
                        sp.wait_ge(s["w_split"], n - 1)
                        sp.sem_inc(s["passed"], 1)
                        wd = a["w_down"][0].rearrange("(q k p) n -> p (q k) n", p=P, k=4)
                        sp.dma_start(raw[:, 1 - k, 0:4, :],
                                     wd[:, bass.ds(q * 4, 4), (2 * p + k) * NB:(2 * p + k + 1) * NB])\
                          .then_inc(w_in_[1 - k], 16)

            sp.dma_start(ln_g[:], a["ln_g_2"].partition_broadcast(P).rearrange("p a n -> p (a n)")).then_inc(s["late_in"], 16)
            sp.dma_start(ln_b[:], a["ln_b_2"].partition_broadcast(P).rearrange("p a n -> p (a n)")).then_inc(s["late_in"], 16)
            for h in range(2):
                for c in range(K2):
                    sp.dma_start(bs_row[64 * h:64 * h + 64, c, :],
                                 a["b_s_2"][0, 2 * c + h].partition_broadcast(64)).then_inc(s["late_in"], 16)
            sp.dma_start(w_pool[:], a["w_pool_2"][0].rearrange("g c d -> c g d")).then_inc(s["late_in"], 16)
            sp.dma_start(inv[:], a["k_inv"]).then_inc(s["late_in"], 16)
            IN2 = dict(u=0, v=1, za=2, xb=3, bg=4, cg=5, zb=6, xc=7, zc=8)
            GATE2 = 9 * W2

            def pair2(n, k0, k1):
                load(n, 1, "w_in_2", k0)
                load(n + 1, 0, "w_in_2", k1)

            def gate2(n0, g, name):
                with sp.Fori(0, 4) as j:
                    load(2 * j + n0, 1, "w_in_2", j * NB + (GATE2 + g * D))
                    load(2 * j + n0 + 1, 0, name, j * NB, kc=K2)

            pair2(N_V2, IN2["v"] * W2, IN2["v"] * W2 + NB)
            sp.wait_ge(s["gemm"], units_before(N_V2))
            sp.dma_start(ws_tok[:].rearrange("p (g s) -> p g s", g=8),
                         a["w_s_2"][0].rearrange("g t s -> t g s")).then_inc(s["late_in"], 16)
            for p in range(2):
                pair2(N_A + 2 * p, IN2["u"] * W2 + p * NB, IN2["za"] * W2 + p * NB)
            gate2(N_GA, 0, "w_pa_2")
            for p in range(2):
                pair2(N_B + 4 * p, IN2["xb"] * W2 + p * NB, IN2["cg"] * W2 + p * NB)
                pair2(N_B + 4 * p + 2, IN2["bg"] * W2 + p * NB, IN2["zb"] * W2 + p * NB)
            gate2(N_GB, 1, "w_pb_2")
            for p in range(2):
                pair2(N_C + 2 * p, IN2["xc"] * W2 + p * NB, IN2["zc"] * W2 + p * NB)
            gate2(N_GC, 2, "w_pc_2")
            pair_wo = [(N_WO, 1), (N_WO + 1, 0)]
            for n, k in pair_wo:
                load(n, k, "w_o_2", (n - N_WO) * NB)
            sp.wait_ge(s["m2_ready"], KD)
            for half in range(2):
                sp.dma_start(y_t[:, 4 * half:4 * half + 4, :], x2_d[4 * half:4 * half + 4].rearrange("c p t -> p c t"))\
                  .then_inc(x2_back[half], 16)
            sp.dma_start(g_row[:], a["final_g_2"].partition_broadcast(P)).then_inc(s["g_row_in"], 16)
            for n, k in pair_wo:
                load(n + 2, k, "w_o_2", (n + 2 - N_WO) * NB)
            for t in range(QB):
                sp.wait_ge(s["orow"], t + 1)
                sp.dma_start(out[0, t * P:(t + 1) * P, :], o_row[:, t % 2, :]).then_inc(row_out[t % 2], 16)
            for k in range(2):
                sp.wait_ge(row_out[k], 16 * QB // 2)

        @block.gpsimd
        def _(pool):
            nc.gpsimd.memset(ones[:], 1.0).then_inc(s["consts_ready"], 1)
            nc.gpsimd.memset(eps_rms[:], RMS_EPS).then_inc(s["consts_ready"], 1)
            for head in range(HEADS):
                nc.gpsimd.memset(slopes[:, head:head + 1], -8.0 * 2.0**-(head + 1)).then_inc(s["consts_ready"], 1)
            for c in range(1, KD):
                pool.wait_ge(s["sq_ready"], c + 1)
                if c >= 2:
                    pool.wait_ge(s["sq_used"], c - 1)
                nc.gpsimd.tensor_tensor(acc[:], acc[:], sq[:, c % 2, :], ALU.add).then_inc(s["sq_used"], 1)

            def split(n, k, landed, before=None, kc=KD, landed_ssm=None, place=None):
                src = raw[:, k] if place is None else place
                pool.wait_ge(w_in_[k], landed)
                if landed_ssm:
                    pool.wait_ge(ws_in[k], landed_ssm)
                if before is not None:
                    pool.wait_ge(s["gemm"], before)
                pool.sem_inc(s["passed"], 1)
                for half, done in enumerate((s["w_half"], s["w_split"])):
                    c = slice(half * kc // 2, (half + 1) * kc // 2)
                    nc.gpsimd.tensor_scalar(w_h[:, k, c, :], src[:, c, :], 1.0, None, ALU.mult).then_inc(s["w_high"], 1)
                    pool.wait_ge(s["w_high"], 2 * n + half + 1)
                    nc.gpsimd.tensor_tensor(w_l[:, k, c, :], src[:, c, :],
                                            w_h[:, k, c, :].bitcast(F32), ALU.subtract).then_inc(done, 1)

            def single(n, kc=KD, landed_ssm=None, place=None):
                split(n, n % 2, 16 * (n // 2 + 1), units_before(n - 1) if n >= 2 else None, kc, landed_ssm, place)

            def pairs(n0, trips, kcs=(KD, KD)):
                m = len(kcs)
                with pool.Fori(0, trips) as i:
                    for k, kc in enumerate(kcs):
                        n = n0 + k
                        split(i * m + n, n % 2, i * (8 * m) + 16 * (n // 2 + 1),
                              i * (2 * m) + units_before(n - 1), kc)

            for n in range(3):
                single(n)
            pairs(3, 6)

            stage_step = Steps(pool, s["staged"])

            def stage(p, e, done=None):
                own, other = slice(HD * e, HD * e + HD), slice(HD - HD * e, P - HD * e)
                if done is not None:
                    pool.wait_ge(s["s_ready"], done)
                q, k = qk[own, p, :], qk[own, p + KA, :]
                stage_step(nc.gpsimd.tensor_scalar(q2[own, e, :], q, 1.0, None, ALU.mult))
                if p or e:
                    stage_step(nc.gpsimd.tensor_scalar(k_hh[own, e, :], k, 1.0, None, ALU.mult))
                    stage_step(nc.gpsimd.tensor_scalar(k_hh[other, e, :], k, 1.0, None, ALU.mult))
                stage_step(nc.gpsimd.tensor_tensor(q2[other, e, :], q, q2[own, e, :].bitcast(F32), ALU.subtract))
                for half in (own, other) if p or e else ():
                    stage_step(nc.gpsimd.tensor_tensor(k_ll[half, e, :], k, k_hh[own, e, :].bitcast(F32), ALU.subtract))
                if done is not None:
                    pool.wait_ge(s["pv"], AHEAD + done)
                stage_step(nc.gpsimd.tensor_copy(v_st[:, e], v_tok[:, :, P * p + HD * e:P * p + HD * (e + 1)]))

            pool.wait_ge(s["qkv_read"], AHEAD + 12)
            for head in range(HEADS):
                stage(head // 2, head % 2, QB * (head - 1) if head >= 2 else None)
            for j in range(4):
                single(N_PROJ + j, KA + 2, 16 * (j // 2 + 1), None if j else proj_raw)
            single(N_OUT)
            single(N_OUT + 1)
            pairs(N_OUT + 2, 1)
            pairs(N_FFN, 4, (KD,) * 4 + (4,) * 4)
            pairs(N_V2, 1)
            single(N_A)
            single(N_A + 1)
            pool.wait_ge(s["wst_ready"], 1)
            nc.gpsimd.affine_select(out=wst[:], in_=wst[:], compare_op=ALU.is_ge, fill=0.0, base=0,
                                    pattern=[[0, 8], [1, P]], channel_multiplier=-1).then_inc(s["wst_masked"], 1)
            for n in range(N_A + 2, N_GA):
                single(n)
            pairs(N_GA, 4, (KD, K2))
            pairs(N_B, 4)
            pairs(N_GB, 4, (KD, K2))
            pairs(N_C, 2)
            pairs(N_GC, 4, (KD, K2))
            pairs(N_WO, 2)

        @block.tensor
        def _(pe):
            def product_half(dst, k, cg, kc, high, low, th, kw=0, rest=None):
                tok = slice(HALF * th, HALF * th + HALF)
                for c in range(kc):
                    if rest is not None and c == kc // 2:
                        split_done(rest)
                    for p, (w, x) in enumerate(((w_h, high), (w_h, low), (w_l, high))):
                        last = nc.tensor.matmul(dst[:, tok], w[:, k, kw + c, P * cg:P * cg + P], x[:, c, tok],
                                                start=(c == 0 and p == 0), stop=(c == kc - 1 and p == 2))
                return last

            def product(dst, k, cg, kc, high, low, kw=0, rest=None):
                for th in range(2):
                    last = product_half(dst, k, cg, kc, high, low, th, kw, None if th else rest)
                return last

            def product_pair(slots, k, kc, high, low, ready, base=0):
                for c in range(kc):
                    pe.wait_ge(ready, base + (c + 1))
                    for cg in range(2):
                        for th in range(2):
                            tok = slice(HALF * th, HALF * th + HALF)
                            for p, (w, x) in enumerate(((w_h, high), (w_h, low), (w_l, high))):
                                last = nc.tensor.matmul(slot(slots[cg])[:, tok], w[:, k, c, P * cg:P * cg + P], x[:, c, tok],
                                                        start=(c == 0 and p == 0), stop=(c == kc - 1 and p == 2),
                                                        skip_group_check=True)
                        if c == kc - 1:
                            last.then_inc(s["gemm"], 1)

            def rows_chunk(dst, k, t0, t, c):
                tok = slice((t0 + t) * P, (t0 + t + 1) * P)
                for p, (w, x) in enumerate(((w_h, act_h), (w_h, act_l), (w_l, act_h))):
                    last = nc.tensor.matmul(dst[:, NB * t:NB * t + NB], x[:, c, tok], w[:, k, c, :],
                                            start=(c == 0 and p == 0), stop=(c == KD - 1 and p == 2),
                                            skip_group_check=True)
                return last

            def product_rows(dst, k, t0):
                for t in range(4):
                    for c in range(KD):
                        last = rows_chunk(dst, k, t0, t, c)
                return last

            def split_done(n):
                pe.wait_ge(s["w_split"], n + 1)

            def gate_unit(ch, t, cg):
                if cg == 0:
                    split_done(4 * ch + N_GATE + t)
                j = 2 * t + cg
                for th in range(2):
                    if j:
                        pe.wait_ge(s["gate_read"], AHEAD + 16 * ch + 2 * j + th - 1)
                    else:
                        pe.wait_ge(s["gate_read"], AHEAD + 16 * ch)
                    product_half(slot(0), (N_GATE + t) % 2, cg, KD, act_h, act_l, th)\
                        .then_inc(s["gemm"] if th else s["gate_half"], 1)

            def s5_matrices(ch, t):
                pe.wait_ge(s["bc_ready"], 4 * ch + t + 1)
                if t:
                    pe.wait_ge(s["bu_read"], AHEAD + 8 * ch + 2 * t - 1)
                else:
                    pe.wait_ge(s["bu_read"], AHEAD + 8 * ch)
                for m in range(4):
                    last = nc.tensor.transpose(slot(1)[:, P * m:P * m + P], bc[:, m, :], ident[:])
                last.then_inc(s["bct_done"], 1)

            def s5_in(ch, t):
                pe.wait_ge(s["bct_copied"], 4 * ch + t + 1)
                if t:
                    pe.wait_ge(s["bu_read"], AHEAD + 8 * ch + 2 * t)
                for m in range(2):
                    for th in range(2):
                        tok = HALF * th
                        last = nc.tensor.matmul(slot(1 + m)[:, tok:tok + HALF], bct[:, t % 2, m, :],
                                                us[:, bass.ds(ch, 1), tok:tok + HALF].rearrange("p a n -> p (a n)"),
                                                start=True, stop=True)
                    last.then_inc(s["bu_ready"], 1)

            def s5_out(ch, t):
                pe.wait_ge(s["x_ready"], 4 * ch + t + 1)
                if t == 0:
                    pe.wait_ge(s["y_read"], ch)
                for th in range(2):
                    tok = slice(HALF * th, HALF * th + HALF)
                    for m in range(2):
                        last = nc.tensor.matmul(slot(3)[:, tok], bct[:, t % 2, 2 + m, :], s5[:, 6 + m, tok],
                                                start=(t == 0 and m == 0), stop=(t == 3 and m == 1),
                                                skip_group_check=True)
                last.then_inc(s["y_done"], 1)

            pe.wait_ge(s["vec_in"], 16 * (len(ROWS_A) + len(ROWS_B)))
            pe.wait_ge(s["const_in"], 16)
            nc.tensor.transpose(slot(0)[:, 0:P], rows[:, 0, :], ident[:])
            nc.tensor.transpose(slot(0)[:, P:P + n_b], rows[0:n_b, 1, :], ident[0:n_b, 0:n_b]).then_inc(s["colt"], 1)
            pe.wait_ge(s["x_in"], 16)
            for c in range(KD):
                if c >= 4:
                    pe.wait_ge(s["h_ready"], c - 3)
                elif c == 0:
                    pe.wait_ge(s["colt_read"], 1)
                for t in range(QB):
                    last = nc.tensor.transpose(slot(c % 4)[:, P * t:P * t + P], x_tok[:, t, P * c:P * c + P], ident[:])
                last.then_inc(s["tr"], 1)

            def statistics(x, adds, dst):
                pe.wait_ge(s["sq_used"], adds)
                for b in range(QB):
                    last = nc.tensor.matmul(dst[:, b:b + 1], x[:, P * b:P * b + P], ones[:, 0:1], start=True, stop=True)
                last.then_inc(s["sums_ready"], 1)

            def everywhere(count, dst, i):
                pe.wait_ge(s["diag_ready"], count)
                for th in range(2):
                    last = nc.tensor.matmul(dst[:, HALF * th:HALF * th + HALF], ones[:],
                                            diag[i][:, 4 * th:4 * th + 4, :].rearrange("p b t -> p (b t)"),
                                            start=True, stop=True)
                last.then_inc(s["rstd_ready"], 1)

            def ada(dst, part):
                for cg in range(2):
                    last = nc.tensor.matmul(dst[:, cg:cg + 1], part[:, P * cg:P * cg + P], ones[:, 0:1], start=True, stop=True)
                return last

            pe.wait_ge(s["consts_ready"], 2 + HEADS)
            pe.wait_ge(s["h_ready"], KD - 1)
            def ada_row(i):
                pe.wait_ge(ada0_in[i], 32)
                dst = slot(i - SUMMED)[0:1, 0:2 * NB].rearrange("p (b n) -> p b n", b=2)
                for c in range(KD):
                    last = nc.tensor.matmul(dst, c_act[:, c:c + 1], ada_w[:, 2 * i:2 * i + 2, c, :],
                                            start=(c == 0), stop=(c == KD - 1))
                last.then_inc(s["ada_row"], 1)

            def ada_columns(i):
                if i < SUMMED:
                    pe.wait_ge(s["ada_summed"], i + 1)
                else:
                    pe.wait_ge(s["row_copied"], i - SUMMED + 1)
                for b in (2 * i, 2 * i + 1):
                    dst = slot(2)[:, 2 * b:2 * b + 2]
                    if i < SUMMED:
                        last = ada(dst, ada_w[:, b, 0, :])
                    else:
                        for cg in range(2):
                            last = nc.tensor.matmul(dst[:, cg:cg + 1], ada_w[0:1, b, 0, P * cg:P * cg + P], ones[0:1, 0:1],
                                                    start=True, stop=True)
                    last.then_inc(s["ada_done"], 1)

            ada_row(2)
            statistics(acc, KD - 1, slot(3))
            ada_row(3)
            for i in range(SUMMED):
                ada_columns(i)
            everywhere(1, slot(3), 0)
            for i in range(SUMMED, N_ADA_EARLY // 2):
                ada_columns(i)

            split_done(0)
            product_pair((0, 1), 0, KD, act_h, act_l, s["u_ready"])

            pe.wait_ge(s["us_ready"], 2)
            pe.wait_ge(s["mod_read"], 1)
            with pe.Fori(0, 2) as ch:
                s5_matrices(ch, 0)
                s5_in(ch, 0)
                for t in range(4):
                    gate_unit(ch, t, 0)
                    if t:
                        s5_out(ch, t - 1)
                    if t < 3:
                        s5_matrices(ch, t + 1)
                    gate_unit(ch, t, 1)
                    if t < 3:
                        s5_in(ch, t + 1)
                s5_out(ch, 3)

            pe.wait_ge(s["gate_read"], AHEAD + 4 * KD)
            with pe.Fori(0, 2) as i:
                for b in range(2):
                    split_done(2 * i + N_QKV + b)
                    for cg in range(2):
                        if b:
                            pe.wait_ge(s["qkv_read"], AHEAD + 4 * i + cg + 1)
                        else:
                            pe.wait_ge(s["qkv_read"], AHEAD + 4 * i)
                        product(slot(cg), 1 - b, cg, KD, act_h, act_l).then_inc(s["gemm"], 1)
            for b in range(2):
                split_done(N_QKV + 4 + b)
                for h in range(2):
                    pe.wait_ge(s["qkv_read"], AHEAD + 8 + 2 * b + h - 1)
                    product_rows(slot(h), 1 - b, 4 * h).then_inc(s["gemm"], 1)
            pe.wait_ge(s["yg_ready"], 2)
            for o in range(2):
                for th in range(2):
                    tok = slice(HALF * th, HALF * th + HALF)
                    for c in range(2):
                        last = nc.tensor.matmul(slot(2 + o)[:, tok], w_glu[:, c, P * o:P * o + P], yg[:, c, tok],
                                                start=(c == 0), stop=(c == 1))
                last.then_inc(s["glu_done"], 1)

            pe.wait_ge(s["qkv_read"], AHEAD + 12)

            def scores(p, t):
                e, qb = tiles[t % NT]
                if t % QB == 0:
                    pe.wait_ge(s["staged"], p * (2 * STAGED) + STAGED * (t // QB + 1) - 4)
                if t >= 2:
                    pe.wait_ge(s["sm_ready"], AHEAD + NT * p + t - 1)
                n = (qb + 1) * P
                for c0 in range(0, n, HALF):
                    w = min(HALF, max(2 * P, n - c0))
                    for k in (k_hh, k_ll):
                        last = nc.tensor.matmul(slot(t % 2)[:, c0:c0 + w], q2[:, e, P * qb:P * qb + P],
                                                k[:, e, c0:c0 + w], start=(k is k_hh), stop=(k is k_ll))
                last.then_inc(s["s_ready"], 1)

            def transposes(p, t):
                qb = tiles[t % NT][1]
                pe.wait_ge(s["p_ready"], NT * p + t + 1)
                if t % 2:
                    pe.wait_ge(s["ptc0"], QB * p + t // 2 + 1)
                elif t:
                    pe.wait_ge(s["ptshort"], QB * p + t // 2)
                for b in range(min(4, qb + 1)):
                    last = nc.tensor.transpose(slot(2)[:, P * b:P * b + P], prob[:, t % 4, P * b:P * b + P], ident[:])
                last.then_inc(s["pt0"], 1)
                if qb >= 4:
                    if t:
                        pe.wait_ge(s["ptc1"], QB * p + t // 2)
                    for b in range(4, qb + 1):
                        last = nc.tensor.transpose(slot(2)[:, P * b:P * b + P], prob[:, t % 4, P * b:P * b + P], ident[:])
                    last.then_inc(s["pt1"], 1)

            def values(p, t):
                e, qb = tiles[t]
                if qb >= 4:
                    pe.wait_ge(s["ptc0"], QB * p + t // 2 + 1)
                    pe.wait_ge(s["ptc1"], QB * p + t // 2 + 1)
                else:
                    pe.wait_ge(s["ptshort"], QB * p + t // 2 + 1)
                if t:
                    pe.wait_ge(s["o_ready"], AHEAD + NT * p + t - 1)
                else:
                    pe.wait_ge(s["o_ready"], AHEAD + NT * p)
                dst = slot(3)[:, HALF * (t % 2):HALF * (t % 2) + HALF]
                for b in range(qb + 1):
                    last = nc.tensor.matmul(dst[:, 0:HD], prob_t[:, t % 2, P * b:P * b + P], v_st[:, e, b, :],
                                            start=(b == 0), stop=(b == qb))
                last.then_inc(s["pv"], 1)
                if t % 4 == 3:
                    k = t // 4
                    pe.wait_ge(s["ada_summed"], 4 * p + SUMMED + k + 1)
                    ada(dst[:, HD:HD + 2], ada_part[:, k % 2]).then_inc(s["ada_done"], 1)

            def heads(p, last):
                end = NT if last else NT + 3
                for t in range(NT):
                    if t + 3 < end:
                        scores(p, t + 3)
                    if t + 1 < end:
                        transposes(p, t + 1)
                    values(p, t)

            pe.wait_ge(s["k0_ready"], 4)
            for t in range(3):
                scores(0, t)
            pe.wait_ge(s["y_gated"], 2)
            transposes(0, 0)
            with pe.Fori(0, HEADS // 2 - 1) as p:
                heads(p, False)
            heads(HEADS // 2 - 1, True)

            pe.wait_ge(s["o_ready"], AHEAD + HEADS * QB)
            for c in range(KA):
                for t in range(QB):
                    last = nc.tensor.transpose(slot(c)[:, P * t:P * t + P], o_tok[:, t, P * c:P * c + P], ident[:])
                last.then_inc(s["otr"], 1)

            pe.wait_ge(s["ys_ready"], 2)
            pe.wait_ge(s["ot_ready"], 2)
            with pe.Fori(0, 2) as i:
                for b in range(2):
                    split_done(2 * i + N_PROJ + b)
                    for cg in range(2):
                        if b:
                            pe.wait_ge(s["proj_read"], AHEAD + 4 * i + cg + 1)
                        else:
                            pe.wait_ge(s["proj_read"], AHEAD + 4 * i)
                        product(slot(2 * cg + 1), 1 - b, cg, 2, ys_h, ys_l, kw=KA).then_inc(s["gemm"], 1)
                        if b == 0 and cg == 0:
                            pe.wait_ge(s["ot_ready"], KA)
                        product(slot(2 * cg), 1 - b, cg, KA, in2_h, in2_l).then_inc(s["gemm"], 1)

            pe.wait_ge(s["proj_read"], AHEAD + KD - 1)
            with pe.Fori(0, 2) as i:
                pe.wait_ge(s["out_read"], AHEAD + 4 * i)
                split_done(2 * i + N_OUT)
                product_pair((0, 1), 1, KD, act_h, act_l, s["merged_ready"])
                split_done(2 * i + N_OUT + 1)
                pe.wait_ge(s["proj_read"], AHEAD + KD)
                for cg in range(2):
                    product(slot(2 + cg), 0, cg, KD, act_h, act_l).then_inc(s["gemm"], 1)

            statistics(acc, 2 * (KD - 1), slot(3))
            everywhere(2, slot(3), 0)
            with pe.Fori(0, 4) as q:
                pe.wait_ge(s["down_read"], AHEAD + 8 * q)
                split_done(8 * q + N_FFN)
                product_pair((0, 1), 1, KD, act_h, act_l, s["u_ready"], KD)
                for p in range(2):
                    for b in range(2):
                        if p == 0 and b == 0:
                            continue
                        split_done(8 * q + N_FFN + 2 * p + b)
                        for cg in range(2):
                            if p:
                                pe.wait_ge(s["v_read"] if b else s["a_read"], 4 * q + cg + 1)
                            product(slot(2 * b + cg), 1 - b, cg, KD, act_h, act_l).then_inc(s["gemm"], 1)
                pe.wait_ge(s["a_read"], 4 * q + 4)
                split_done(8 * q + N_FFN + 4)
                product_pair((0, 1), 1, 4, in2_h, in2_l, s["f_ready"], AHEAD + 4 * q)
                for u in range(2, 8):
                    if u % 2 == 0:
                        split_done(8 * q + N_FFN + 4 + u // 2)
                    if u >= 4:
                        pe.wait_ge(s["down_read"], AHEAD + 8 * q + u - 3)
                    product(slot(u % 4), 1 - (u // 2) % 2, u % 2, 4, in2_h, in2_l).then_inc(s["gemm"], 1)

            for m in range(2):
                statistics(acc2[:, m, :], 4 * (KD - 1) - 1 + m, slot(3 - m))
            everywhere(4, slot(3), 0)
            everywhere(4, slot(2), 1)
            pe.wait_ge(s["rstd2_ready"], 2)
            for b in range(2):
                split_done(N_V2 + b)
            for c in range(KD):
                pe.wait_ge(s["u_ready"], 2 * KD + c + 1)
                for b in range(2):
                    for h in range(2):
                        for t in (0, 2):
                            rows_chunk(slot(2 * b + h), 1 - b, 4 * h, t, c)
            for b in range(2):
                for h in range(2):
                    for t in (1, 3):
                        for c in range(KD):
                            last = rows_chunk(slot(2 * b + h), 1 - b, 4 * h, t, c)
                    last.then_inc(s["gemm"], 1)
            pe.wait_ge(s["late_in"], 16 * 13)
            for p in range(2):
                for b in range(2):
                    split_done(N_A + 2 * p + b)
                    for cg in range(2):
                        if b:
                            pe.wait_ge(s["au_read"], 2 * p + cg + 1)
                        elif p:
                            pe.wait_ge(s["az_read"], cg + 1)
                        else:
                            pe.wait_ge(s["v2_read"], cg + 1)
                        product(slot(cg), 1 - b, cg, KD, act_h, act_l).then_inc(s["gemm"], 1)
                        if p == 0 and b == 0 and cg == 0:
                            pe.wait_ge(s["v2_read"], 4)
                            for g in range(8):
                                last = nc.tensor.transpose(slot(2)[:, P * g:P * g + P], ws_tok[:, P * g:P * g + P], ident[:])
                            last.then_inc(s["wst_done"], 1)
                pe.wait_ge(s["vn_ready"], 1)
                pe.wait_ge(s["wst_masked"], 1)
                for cg in range(2):
                    if p:
                        pe.wait_ge(s["sg_read"], cg + 1)
                    for g in range(2):
                        grp = 2 * (2 * p + cg) + g
                        for t in range(QB):
                            last = nc.tensor.matmul(slot(2 + cg)[HD * g:HD * g + HD, P * t:P * t + P],
                                                    vg[:, t, HD * grp:HD * grp + HD], wst[:, grp, :],
                                                    start=True, stop=True)
                    last.then_inc(s["sg_done"], 1)

            def gate_loop(n0, ready, gate_read, p_read, free):
                pe.wait_ge(free, 4)
                with pe.Fori(0, 2) as j:
                    for i in range(4):
                        b = i % 2
                        n = 4 * j + n0 + i
                        pe.wait_ge(s["w_half"], n + 1)
                        if b:
                            pe.wait_ge(ready, 4)
                        for cg in range(2):
                            pe.wait_ge(p_read if b else gate_read, AHEAD + 4 * j + 2 * (i // 2))
                            if b:
                                product(slot(2 + cg), 0, cg, K2, in2_h, in2_l, rest=None if cg else n).then_inc(s["gemm"], 1)
                            else:
                                product(slot(cg), 1, cg, KD, act_h, act_l, rest=None if cg else n).then_inc(s["gemm"], 1)

            gate_loop(N_GA, s["a_ready"], s["sa_ready"], s["pa_read"], s["az_read"])
            pe.wait_ge(s["sa_ready"], AHEAD + KD)
            for p in range(2):
                for b, before in enumerate((s["bg_read"], s["bz_read"])):
                    split_done(N_B + 4 * p + b)
                    if p == 0 and b:
                        pe.wait_ge(s["pa_read"], AHEAD + KD)
                    for cg in range(2):
                        if p:
                            pe.wait_ge(before, cg + 1)
                        product(slot(2 * b + cg), 1 - b, cg, KD, act_h, act_l).then_inc(s["gemm"], 1)
                for b, free in enumerate((s["xb_read"], s["bc_read"])):
                    split_done(N_B + 4 * p + 2 + b)
                    for cg in range(2):
                        pe.wait_ge(free, 2 * p + cg + 1)
                        product(slot(2 * b + cg), 1 - b, cg, KD, act_h, act_l).then_inc(s["gemm"], 1)
            gate_loop(N_GB, s["b_ready"], s["sb_ready"], s["pb_read"], s["bg_read"])
            pe.wait_ge(s["sb_ready"], AHEAD + KD)
            for p in range(2):
                for b in range(2):
                    split_done(N_C + 2 * p + b)
                    if p == 0 and b:
                        pe.wait_ge(s["pb_read"], AHEAD + KD)
                    for cg in range(2):
                        if p:
                            pe.wait_ge(s["cz_read"] if b else s["cp_ready"], cg + 1)
                        product(slot(2 * b + cg), 1 - b, cg, KD, act_h, act_l).then_inc(s["gemm"], 1)
                for cg in range(2):
                    c = 2 * p + cg
                    pe.wait_ge(s["pooled"], c + 1)
                    for th in range(2):
                        tok = slice(HALF * th, HALF * th + HALF)
                        last = nc.tensor.matmul(slot(cg)[:, tok], w_pool[:, c, :], pool_in[c % 2][:, tok],
                                                start=True, stop=True)
                    last.then_inc(s["pool_done"], 1)
            gate_loop(N_GC, s["ch_done"], s["sc_ready"], s["pc_read"], s["cp_ready"])

            pe.wait_ge(s["pc_read"], AHEAD + KD)
            with pe.Fori(0, 2) as i:
                pe.wait_ge(s["y_ready"], AHEAD + 4 * i)
                split_done(2 * i + N_WO)
                product_pair((0, 1), 1, KD, act_h, act_l, s["m2_ready"])
                split_done(2 * i + N_WO + 1)
                for cg in range(2):
                    product(slot(2 + cg), 0, cg, KD, act_h, act_l).then_inc(s["gemm"], 1)
            pe.wait_ge(s["y_ready"], AHEAD + KD)
            for t in range(QB):
                if t >= 4:
                    pe.wait_ge(s["orow"], t - 3)
                for c in range(KD):
                    last = nc.tensor.transpose(slot(t % 4)[:, P * c:P * c + P], y_t[:, c, P * t:P * t + P], ident[:])
                last.then_inc(s["otr2"], 1)

        @block.scalar
        def _(act):
            A = nc.scalar
            step = Steps(act, s["act"])

            act.dma_start(mask_b[:], a["k_mask_b"]).then_inc(s["s5_in"], 16)
            act.dma_start(mask_c[:], a["k_mask_c"]).then_inc(s["s5_in"], 16)
            for m, name in enumerate(("b_re", "b_im")):
                act.dma_start(b_in[:, m], a[name][0].rearrange("(t g) n c -> (g n) t c", g=2)).then_inc(s["s5_in"], 16)
            for m, name in enumerate(("c_re", "c_im")):
                act.dma_start(cc[:, m], a[name][0].rearrange("(h g) c n -> (g c) h n", h=2)).then_inc(s["s5_in"], 16)
            with nc.allow_non_contiguous_dma(reason="sixteen time steps, one value for each state"):
                for g in range(2):
                    act.dma_start(par[NSTATE * g:NSTATE * g + NSTATE, 0, :],
                                  a["log_dt"][0].rearrange("(t g) -> g t", g=2)[g].partition_broadcast(NSTATE))\
                       .then_inc(s["s5_in"], 16)
            act.dma_start(w_glu[:], a["w_glu"][0].rearrange("(k p) n -> p k n", p=P)).then_inc(s["s5_in"], 16)

            act.wait_ge(s["colt_read"], 1)
            A.activation(c_act[:], col_a("c", 0, KD), ACT.Silu).then_inc(s["c_ready"], 1)
            act.wait_ge(s["s5_in"], 16 * 9)
            A.activation(par[:, 1, :], par[:, 0, :], ACT.Exp).then_inc(s["dt_ready"], 1)
            act.wait_ge(s["lrdt_ready"], 1)
            step(A.activation(mag[:], par[:, 2, :], ACT.Exp))
            act.wait_ge(s["angle_ready"], 1)
            step(A.activation(turn[:, 0], prep[:, 3, :, :], ACT.Sin))
            A.activation(turn[:, 1], prep[:, 2, :, :], ACT.Sin).then_inc(s["turn_ready"], 1)

            def squares(k, ready, ahead=0):
                for c in range(KD):
                    if k == 0:
                        act.wait_ge(s["tr"], c + 1)
                        A.activation(h_t[:, c, :], slot(c % 4), ACT.Copy).then_inc(s["h_ready"], 1)
                    act.wait_ge(ready, ahead + c + 1)
                    if c >= 3:
                        act.wait_ge(s["sq_used"], (KD - 1) * k + c - 2)
                    A.activation(sq[:, c % 2, :] if c else acc[:], h_t[:, c, :], ACT.Square).then_inc(s["sq_ready"], 1)

            def root(count):
                act.wait_ge(s["sums_ready"], count)
                A.activation(stat[:, 0, :], slot(3)[:, 0:QB], ACT.Sqrt, scale=1.0 / D, bias=eps_rms[:])\
                 .then_inc(s["std_ready"], 1)

            def norm(nu, shift):
                for c in range(KD):
                    act.wait_ge(s["t_ready"], KD * nu + c + 1)
                    A.activation(act_h[:, c, :], nrm[:, c % 2, :], ACT.Identity, bias=shift(c) if shift else 0.0)\
                     .then_inc(s["hi_ready"], 1)

            act.wait_ge(s["consts_ready"], 2 + HEADS)
            squares(0, s["h_ready"])
            act.dma_start(h_d.rearrange("c p t -> p c t"), h_t[:]).then_inc(s["h_out"], 16)
            def row(i):
                act.wait_ge(s["ada_row"], i - SUMMED + 1)
                A.activation(ada_w[0:1, 2 * i:2 * i + 2, 0, :],
                             slot(i - SUMMED)[0:1, 0:2 * NB].rearrange("p (b n) -> p b n", b=2), ACT.Copy)\
                 .then_inc(s["row_copied"], 1)

            row(2)
            root(1)
            row(3)
            act.wait_ge(s["mod_ready"], 1)
            norm(0, lambda c: mod[:, c:c + 1])

            act.wait_ge(s["h_out"], 16)
            act.wait_ge(s["u_ready"], KD)
            for cg in range(2):
                act.wait_ge(s["gemm"], cg + 1)
                A.activation(us[:, cg, :], slot(cg), ACT.Copy).then_inc(s["us_ready"], 1)

            def gate(ch, j):
                k = j % 2
                if j >= 2:
                    act.wait_ge(gate_out[k], AHEAD + 64 * ch + 16 * (j // 2))
                else:
                    act.wait_ge(gate_out[k], AHEAD + 64 * ch)
                for th in range(2):
                    tok = slice(HALF * th, HALF * th + HALF)
                    if th:
                        act.wait_ge(s["gemm"], 8 * ch + units_before(N_GATE) + j + 1)
                    else:
                        act.wait_ge(s["gate_half"], 8 * ch + j + 1)
                    act.sem_inc(s["passed"], 1)
                    A.activation(gate_st[:, k, tok], slot(0)[:, tok], ACT.Sigmoid,
                                 bias=cols_a[:, bass.ds(8 * ch + (at_a["b_gate"] + j), 1)]).then_inc(s["gate_read"], 1)
                act.wait_ge(s["gate_read"], AHEAD + 16 * ch + 2 * j + 2)
                act.dma_start(gates_d[bass.ds(8 * ch + j, 1)].rearrange("a p t -> p (a t)"), gate_st[:, k, :])\
                   .then_inc(gate_out[k], 16)

            def matrices(ch, t):
                act.wait_ge(s["bct_done"], AHEAD + 4 * ch + t + 1)
                A.activation(bct[:, t % 2].rearrange("p m n -> p (m n)"), slot(1)[:, 0:4 * P], ACT.Copy)\
                 .then_inc(s["bct_copied"], 1)

            with act.Fori(0, 2) as ch:
                matrices(ch, 0)
                for t in range(4):
                    gate(ch, 2 * t)
                    if t < 3:
                        matrices(ch, t + 1)
                    gate(ch, 2 * t + 1)
                act.wait_ge(s["y_read"], ch + 1)
                y = yg[:, bass.ds(ch, 1), :].rearrange("p a n -> p (a n)")
                A.activation(y, y, ACT.Gelu_apprx_tanh).then_inc(s["yg_ready"], 1)
            act.wait_ge(s["yg_ready"], 2)
            with act.Fori(0, 4) as i:
                for b in range(2):
                    act.wait_ge(s["gemm"], 2 * i + units_before(N_QKV) + b + 1)
                    A.activation(qk[:, bass.ds(2 * i + b, 1), :].rearrange("p a n -> p (a n)"), slot(b), ACT.Copy)\
                     .then_inc(s["qkv_read"], 1)
            for b in range(2):
                for h in range(2):
                    act.wait_ge(s["gemm"], units_before(N_QKV + 4 + b) + h + 1)
                    A.activation(v_tok[:, 4 * h:4 * h + 4, NB * b:NB * b + NB],
                                 slot(h).rearrange("p (t n) -> p t n", t=4), ACT.Copy).then_inc(s["qkv_read"], 1)
            act.wait_ge(s["qkv_read"], AHEAD + 12)
            for half in range(2):
                A.activation(k_hh[HD * half:HD * half + HD, 0, :], qk[0:HD, KA, :], ACT.Copy).then_inc(s["k0_ready"], 1)
            for k in range(2):
                act.wait_ge(gate_out[k], AHEAD + 16 * KD)
                act.wait_ge(s["glu_done"], k + 1)
                A.activation(gate_st[:, k, :], slot(2 + k), ACT.Sigmoid, bias=col_a("b_glu", k)).then_inc(s["sig_ready"], 1)

            def softmax(p, t):
                n = (tiles[t % NT][1] + 1) * P
                act.wait_ge(s["sm_ready"], AHEAD + NT * p + t + 1)
                if t >= 3:
                    act.wait_ge(s["o_ready"], AHEAD + NT * p + t - 3)
                elif t == 2:
                    act.wait_ge(s["o_ready"], AHEAD + NT * p)
                A.activation(prob[:, t % 4, 0:n], prob[:, t % 4, 0:n], ACT.Exp, scale=-1.0,
                             bias=neg_max[:, t % 4:t % 4 + 1], accum_out=den[:, t % 4:t % 4 + 1])\
                 .then_inc(s["p_ready"], 1)

            def transposed(p, t):
                qb = tiles[t % NT][1]
                if qb >= 4:
                    act.wait_ge(s["pt1"], QB * p + t // 2 + 1)
                else:
                    act.wait_ge(s["pt0"], AHEAD + NT * p + t + 1)
                if t >= 2:
                    act.wait_ge(s["pv"], AHEAD + NT * p + t - 1)
                elif t:
                    act.wait_ge(s["pv"], AHEAD + NT * p)
                keys = slice(HALF if qb >= 4 else 0, (qb + 1) * P)
                A.activation(prob_t[:, t % 2, keys], slot(2)[:, keys], ACT.Copy)\
                 .then_inc(s["ptc1"] if qb >= 4 else s["ptshort"], 1)

            def heads(p, last):
                for t in range(NT):
                    if t + 1 < NT or not last:
                        transposed(p, t + 1)
                    if t + 2 < NT or not last:
                        softmax(p, t + 2)

            softmax(0, 0)
            softmax(0, 1)
            transposed(0, 0)
            with act.Fori(0, HEADS // 2 - 1) as p:
                heads(p, False)
            act.wait_ge(s["staged"], 4 * STAGED - 4)
            act.dma_start(proj_raw[:, 0:KA, :], weights("w_proj_att", slice(0, NB), k=KA)).then_inc(w_in_[1], 16)
            act.dma_start(proj_raw[:, KA:KA + 2, :], weights("w_proj_ssm", slice(0, NB), k=2)).then_inc(ws_in[1], 16)
            heads(HEADS // 2 - 1, True)

            act.wait_ge(s["staged"], HEADS * STAGED - 4)
            for o in range(2):
                act.wait_ge(s["y_gated"], o + 1)
                A.activation(ys_h[:, o, :], yg[:, o, :], ACT.Copy).then_inc(s["ysh"], 1)
            act.wait_ge(s["w_split"], N_PROJ + 1)
            for c in range(KA):
                act.wait_ge(s["otr"], c + 1)
                A.activation(in2_h[:, c, :], slot(c), ACT.Copy).then_inc(s["oh_ready"], 1)
            with act.Fori(0, 2) as i:
                for c in range(4):
                    act.wait_ge(s["mix_ready"], 4 * i + c + 1)
                    A.activation(act_h[:, bass.ds(4 * i + c, 1), :].rearrange("p a n -> p (a n)"), mix[:, 0, :], ACT.Copy)\
                     .then_inc(s["mh_ready"], 1)
            squares(1, s["out_read"], AHEAD)
            root(2)
            norm(1, lambda c: mod[:, 3 * KD + c:3 * KD + c + 1])

            base_f = units_before(N_FFN)
            with act.Fori(0, 4) as q:
                for p in range(2):
                    for cg in range(2):
                        c = 2 * p + cg
                        act.wait_ge(s["gemm"], 16 * q + base_f + 4 * p + cg + 1)
                        if p:
                            act.wait_ge(s["f_ready"], AHEAD + 4 * q + cg + 1)
                        else:
                            act.wait_ge(s["f_ready"], AHEAD + 4 * q)
                        A.activation(conv[:, cg, :], slot(cg), ACT.Identity,
                                     scale=cols_b[:, bass.ds(4 * q + (at_b["w_conv"] + c), 1)],
                                     bias=cols_a[:, bass.ds(4 * q + (at_a["b_conv"] + c), 1)]).then_inc(s["acc_ready"], 1)
                    for cg in range(2):
                        c = 2 * p + cg
                        act.wait_ge(s["a_read"], 4 * q + c + 1)
                        A.activation(conv[:, cg, :], conv[:, cg, :], ACT.Silu).then_inc(s["silu_ready"], 1)
                    for cg in range(2):
                        c = 2 * p + cg
                        act.wait_ge(s["v_read"], 4 * q + c + 1)
                        A.activation(in2_h[:, c, :], ffn[:], ACT.Copy).then_inc(s["fh_ready"], 1)

            for c in range(KD):
                act.wait_ge(s["down_read"], AHEAD + 24 + c + 1)
                for m in range(2):
                    if c >= 2:
                        act.wait_ge(s["sq_used"], 2 * (KD - 1) + 2 * (c - 2) + m + 1)
                    A.activation(sq[:, m, :] if c else acc2[:, m, :], h_t[:, c, :], ACT.Square,
                                 scale=col_b("g_final", c) if m else 1.0).then_inc(s["sq_ready"], 1)
            root(3)
            act.wait_ge(s["ms2_ready"], 1)
            A.activation(stat[:, 3, :], stat[:, 2, :], ACT.Sqrt, scale=1.0 / D, bias=eps_rms[:]).then_inc(s["std_ready"], 1)
            for m in range(2):
                act.wait_ge(s["rstd_ready"], 3 + m)
                A.activation(rstd2[:, m, :], slot(3 - m), ACT.Copy).then_inc(s["rstd2_ready"], 1)
            norm(2, None)
            for half in range(2):
                act.wait_ge(s["x2_ready"], 4 * half + 4)
                act.dma_start(x2_d[4 * half:4 * half + 4].rearrange("c p t -> p c t"), h_t[:, 4 * half:4 * half + 4, :])\
                   .then_inc(x2_out[half], 16)

            act.wait_ge(x2_out[0], 16)
            for b in range(2):
                for h in range(2):
                    act.wait_ge(s["gemm"], units_before(N_V2 + b) + h + 1)
                    A.activation(vg[:, 4 * h:4 * h + 4, NB * b:NB * b + NB],
                                 slot(2 * b + h).rearrange("p (t n) -> p t n", t=4), ACT.Gelu_apprx_tanh)\
                     .then_inc(s["v2_read"], 1)
            act.wait_ge(s["ln_var"], 1)
            A.activation(ln_rstd[:], ln_rstd[:], ACT.Sqrt).then_inc(s["ln_std"], 1)
            act.wait_ge(x2_out[1], 16)
            base_a = units_before(N_A)
            for p in range(2):
                for cg in range(2):
                    act.wait_ge(s["gemm"], base_a + 4 * p + cg + 1)
                    if p:
                        act.wait_ge(s["ap_ready"], cg + 1)
                    A.activation(a_u[:, cg, :], slot(cg), ACT.Gelu_apprx_tanh).then_inc(s["au_read"], 1)
                for cg in range(2):
                    act.wait_ge(s["gemm"], base_a + 4 * p + 2 + cg + 1)
                    A.activation(a_z[:, cg, :], slot(cg), ACT.Silu).then_inc(s["az_read"], 1)
                for cg in range(2):
                    c = 2 * p + cg
                    act.wait_ge(s["ap_ready"], c + 1)
                    A.activation(in2_h[:, c, :], a_s[:], ACT.Copy).then_inc(s["ah_ready"], 1)

            def gates2(n0, done, ready):
                with act.Fori(0, 4) as j:
                    for cg in range(2):
                        act.wait_ge(s["gemm"], 4 * j + units_before(n0) + cg + 1)
                        act.wait_ge(done, AHEAD + 2 * j)
                        A.activation(br[:, cg, :], slot(cg), ACT.Sigmoid).then_inc(ready, 1)

            act.wait_ge(s["a_ready"], K2)
            gates2(N_GA, s["pa_read"], s["sa_ready"])
            act.wait_ge(s["pa_read"], AHEAD + KD)
            base_b = units_before(N_B)
            for p in range(2):
                for cg in range(2):
                    act.wait_ge(s["gemm"], base_b + 8 * p + cg + 1)
                    if p:
                        act.wait_ge(s["b_ready"], cg + 1)
                    A.activation(br[:, cg, :], slot(cg), ACT.Copy).then_inc(s["xb_read"], 1)
                for cg in range(2):
                    c = 2 * p + cg
                    act.wait_ge(s["gemm"], base_b + 8 * p + 6 + cg + 1)
                    act.wait_ge(s["bg_read"], c + 1)
                    A.activation(br2[:], slot(2 + cg), ACT.Silu).then_inc(s["bz_read"], 1)
                    act.wait_ge(s["bp_ready"], c + 1)
                    A.activation(in2_h[:, c, :], br[:, cg, :], ACT.Copy).then_inc(s["bh_ready"], 1)
            act.wait_ge(s["b_ready"], K2)
            gates2(N_GB, s["mb_ready"], s["sb_ready"])
            act.wait_ge(s["mb_ready"], AHEAD + KD)
            base_c = units_before(N_C)
            for p in range(2):
                for cg in range(2):
                    c = 2 * p + cg
                    act.wait_ge(s["gemm"], base_c + 4 * p + cg + 1)
                    if cg:
                        act.wait_ge(s["pooled"], c)
                    elif p:
                        act.wait_ge(s["ch_done"], 2)
                    A.activation(br[:, 0, :], slot(cg), ACT.Copy).then_inc(s["xc_read"], 1)
                for cg in range(2):
                    c = 2 * p + cg
                    act.wait_ge(s["gemm"], base_c + 4 * p + 2 + cg + 1)
                    act.wait_ge(s["pooled"], 2 * p + 2)
                    if cg:
                        act.wait_ge(s["pool_done"], 2 * p + 1)
                    A.activation(br[:, cg, :], slot(2 + cg), ACT.Silu).then_inc(s["cz_read"], 1)
                for cg in range(2):
                    c = 2 * p + cg
                    act.wait_ge(s["cp_ready"], c + 1)
                    A.activation(in2_h[:, c, :], br[:, cg, :], ACT.Copy).then_inc(s["ch_ready"], 1)
            act.wait_ge(s["ch_done"], K2)
            gates2(N_GC, s["mc_ready"], s["sc_ready"])
            for c in range(KD):
                act.wait_ge(s["mc_ready"], AHEAD + c + 1)
                A.activation(act_h[:, c, :], merged[:, c, :], ACT.Copy).then_inc(s["m2_high"], 1)
            for t in range(QB):
                act.wait_ge(s["otr2"], t + 1)
                step(A.activation(o_sq[:], slot(t % 4), ACT.Square, accum_out=o_ssq[:, 0, t:t + 1]))
                A.activation(o_ssq[:, 1, t:t + 1], o_ssq[:, 0, t:t + 1], ACT.Sqrt, scale=1.0 / D, bias=eps_rms[:])\
                 .then_inc(s["ostd"], 1)

        @block.vector
        def _(dve):
            v = nc.vector
            step = Steps(dve, s["dve"])

            dve.wait_ge(s["colt"], 1)
            step(v.tensor_copy(cols_a[:], slot(0)[:, 0:P]))
            v.tensor_copy(cols_b[:, 0:n_b], slot(0)[:, P:P + n_b]).then_inc(s["colt_read"], 1)

            dve.wait_ge(s["s5_in"], 16 * 9)
            ldt, dt, lrdt, ang, abr, abi, nr, den_, rcp, fr, fi, t0, t1 = (par[:, i, :] for i in range(13))
            a_re, a_im = col_a("a_re", 0, 8), col_a("a_im", 0, 8)
            angles, turns, rest, comp = (prep[:, i, :, :] for i in range(4))
            dve.wait_ge(s["dt_ready"], 1)
            v.tensor_tensor(lrdt, a_re, dt, ALU.mult).then_inc(s["lrdt_ready"], 1)
            step(v.tensor_tensor(ang, a_im, dt, ALU.mult))
            for j in range(LOGT):
                step(v.tensor_scalar(angles[:, :, j], ang, float(2**j), None, ALU.mult))
            step(v.tensor_scalar(turns, angles, 1 / (2 * np.pi), ROUND, ALU.mult, ALU.add))
            step(v.tensor_scalar(turns, turns, ROUND, None, ALU.subtract))
            step(v.scalar_tensor_tensor(rest, turns, -TWO_PI_PARTS[0], angles, ALU.mult, ALU.add))
            for part in TWO_PI_PARTS[1:]:
                step(v.scalar_tensor_tensor(rest, turns, -part, rest, ALU.mult, ALU.add))
            step(v.tensor_scalar(rest, rest, 3.1415925, -3.1415925, ALU.min, ALU.max))
            step(v.scalar_tensor_tensor(comp, rest, -1.0, rest, ALU.mult, ALU.min))
            v.tensor_scalar(comp, comp, np.pi / 2, None, ALU.add).then_inc(s["angle_ready"], 1)
            dve.wait_ge(s["turn_ready"], 1)
            cos1, sin1 = turn[:, 0, :, 0], turn[:, 1, :, 0]
            step(v.tensor_tensor(abr, mag[:], cos1, ALU.mult))
            step(v.tensor_tensor(abi, mag[:], sin1, ALU.mult))
            step(v.tensor_scalar(nr, abr, 1.0, None, ALU.subtract))
            step(v.tensor_tensor(den_, a_re, a_re, ALU.mult))
            step(v.tensor_tensor(t0, a_im, a_im, ALU.mult))
            step(v.tensor_tensor(den_, den_, t0, ALU.add))
            step(v.reciprocal(rcp, den_))
            for dst, x, y, op in ((fr, nr, abi, ALU.add), (fi, abi, nr, ALU.subtract)):
                step(v.tensor_tensor(t0, x, a_re, ALU.mult))
                step(v.tensor_tensor(t1, y, a_im, ALU.mult))
                step(v.tensor_tensor(t0, t0, t1, op))
                step(v.tensor_tensor(dst, t0, rcp, ALU.mult))

            def per_state(x):
                return x.unsqueeze(2).to_broadcast([P, STILES, GCH])

            tb = prep2
            for m, (x, y, op) in enumerate(((0, 1, ALU.subtract), (1, 0, ALU.add))):
                step(v.tensor_tensor(bb[:, m], b_in[:, x], per_state(fr), ALU.mult))
                step(v.tensor_tensor(tb[:], b_in[:, y], per_state(fi), ALU.mult))
                step(v.tensor_tensor(bb[:, m], bb[:, m], tb[:], op))

            def add_square(k, c):
                dve.wait_ge(s["sq_ready"], KD * k + c + 1)
                if c >= 2:
                    dve.wait_ge(s["sq_used"], (KD - 1) * k + c - 1)
                v.tensor_tensor(acc[:], acc[:], sq[:, c % 2, :], ALU.add).then_inc(s["sq_used"], 1)

            def ada_sums(out, w, chunks=range(KD)):
                for c in chunks:
                    if c == 0:
                        step(v.tensor_scalar(out, w(0), c_act[:, 0:1], None, ALU.mult))
                        continue
                    ins = v.scalar_tensor_tensor(out, w(c), c_act[:, c:c + 1], out, ALU.mult, ALU.add)
                    if c < KD - 1:
                        step(ins)
                    else:
                        ins.then_inc(s["ada_summed"], 1)

            def ada_early(i):
                dve.wait_ge(ada0_in[i], 32)
                ada_sums(ada_w[:, 2 * i:2 * i + 2, 0, :], lambda c: ada_w[:, 2 * i:2 * i + 2, c, :])

            dve.wait_ge(s["c_ready"], 1)
            for i in range(SUMMED):
                ada_early(i)

            def modulation(lo, hi, src):
                return v.tensor_tensor(mod[:, lo:hi], src, col_a("b_ada", lo, hi - lo), ALU.add)

            def on_diagonal(i, x):
                v.tensor_tensor(diag[i][:], ident[:].unsqueeze(1).to_broadcast([P, QB, P]),
                                x.unsqueeze(2).to_broadcast([P, QB, P]), ALU.mult).then_inc(s["diag_ready"], 1)

            def one_over_root(count):
                dve.wait_ge(s["std_ready"], count)
                step(v.reciprocal(stat[:, 1, :], stat[:, 0, :]))

            def norm(nu, g, shift, rstd):
                def scaled(c):
                    v.scalar_tensor_tensor(nrm[:, c % 2, :], h_t[:, c, :], g[:, c:c + 1], rstd, ALU.mult, ALU.mult)\
                     .then_inc(s["t_ready"], 1)

                scaled(0)
                scaled(1)
                for c in range(KD):
                    dve.wait_ge(s["hi_ready"], KD * nu + c + 1)
                    high = act_h[:, c, :].bitcast(F32)
                    if shift is None:
                        ins = v.tensor_tensor(act_l[:, c, :], nrm[:, c % 2, :], high, ALU.subtract)
                    else:
                        ins = v.scalar_tensor_tensor(act_l[:, c, :], nrm[:, c % 2, :], shift(c), high, ALU.add, ALU.subtract)
                    ins.then_inc(s["u_ready"], 1)
                    if c + 2 < KD:
                        dve.wait_ge(s["u_ready"], KD * nu + c + 1)
                        scaled(c + 2)

            one_over_root(1)
            on_diagonal(0, stat[:, 1, :])
            dve.wait_ge(s["ada_done"], N_ADA_EARLY)
            modulation(0, 2 * N_ADA_EARLY, slot(2)[:, 0:2 * N_ADA_EARLY]).then_inc(s["mod_read"], 1)
            dve.wait_ge(s["mod_read"], 1)
            v.scalar_tensor_tensor(gain[:, 0], mod[:, KD:2 * KD], 1.0, col_a("g_mix", 0, KD), ALU.add, ALU.mult)\
             .then_inc(s["mod_ready"], 1)
            dve.wait_ge(s["rstd_ready"], 1)
            dve.wait_ge(s["mod_ready"], 1)
            norm(0, gain[:, 0], lambda c: mod[:, c:c + 1], slot(3))

            dve.wait_ge(s["h_out"], 16)
            dve.wait_ge(s["u_ready"], KD)
            step(v.memset(turns0[:, 0, :, 0:1], 1.0))
            step(v.memset(turns0[:, 1, :, 0:1], 0.0))
            for j in range(LOGS):
                n = 2**j
                for m in range(2):
                    by = turn[:, m, :, j].unsqueeze(1).unsqueeze(3).to_broadcast([P, 2, STILES, n])
                    step(v.tensor_tensor(part0[:, m, :, :, 0:n], turns0[:, :, :, 0:n], by, ALU.mult))
                for m, op in enumerate((ALU.subtract, ALU.add)):
                    step(v.tensor_tensor(turns0[:, m, :, n:2 * n], part0[:, 0, m, :, 0:n], part0[:, 1, 1 - m, :, 0:n], op))

            cs, sn, wa, wb, wd, we, xre, xim = (s5[:, i, :] for i in range(8))
            def matrices(ch, t):
                if t:
                    dve.wait_ge(s["bct_done"], AHEAD + 4 * ch + t)
                else:
                    dve.wait_ge(s["bct_done"], AHEAD + 4 * ch)
                for m in range(2):
                    rep = bb[:, m, bass.ds(4 * ch + t, 1), :].to_broadcast([P, P // GCH, GCH])
                    step(v.tensor_tensor(bc[:, m, :].rearrange("p (a c) -> p a c", c=GCH),
                                         mask_b[:, t, :].rearrange("p (a c) -> p a c", c=GCH), rep, ALU.mult))
                rep = cc[:, 0, bass.ds(ch, 1), :].to_broadcast([P, 2, NSTATE])
                step(v.tensor_tensor(bc[:, 2, :].rearrange("p (a n) -> p a n", a=2),
                                     mask_c[:, t, :].rearrange("p (a n) -> p a n", a=2), rep, ALU.mult))
                rep = cc[:, 1, bass.ds(ch, 1), :].to_broadcast([P, 2, NSTATE])
                v.scalar_tensor_tensor(bc[:, 3, :].rearrange("p (a n) -> p a n", a=2), rep, -1.0,
                                       mask_c[:, t, :].rearrange("p (a n) -> p a n", a=2), ALU.mult, ALU.mult)\
                 .then_inc(s["bc_ready"], 1)

            with step.loop(2, 227 - 16 * LOGS) as ch:
                for m in range(2):
                    step(v.tensor_copy(cur[:, m], turn[:, m, bass.ds(4 * ch, 4), :]))
                step(v.tensor_copy(cmag[:], mag[:, bass.ds(4 * ch, 4)]))
                matrices(ch, 0)
                for t in range(4):
                    for m, table in enumerate((cs, sn)):
                        step(v.tensor_copy(table[:, 0:SHORT],
                                           turns0[:, m, bass.ds(4 * ch + t, 1), :].rearrange("p a n -> p (a n)")))
                    for j in range(LOGS, LOGT):
                        n = 2**j
                        c1, s1 = cur[:, 0, t, j:j + 1], cur[:, 1, t, j:j + 1]
                        step(v.tensor_scalar(wa[:, 0:n], sn[:, 0:n], s1, None, ALU.mult))
                        step(v.tensor_scalar(wb[:, 0:n], cs[:, 0:n], s1, None, ALU.mult))
                        step(v.scalar_tensor_tensor(cs[:, n:2 * n], cs[:, 0:n], c1, wa[:, 0:n], ALU.mult, ALU.subtract))
                        step(v.scalar_tensor_tensor(sn[:, n:2 * n], sn[:, 0:n], c1, wb[:, 0:n], ALU.mult, ALU.add))
                    if t < 3:
                        matrices(ch, t + 1)
                    dve.wait_ge(s["bu_ready"], 8 * ch + 2 * t + 1)
                    step(v.tensor_tensor(wa, cs, slot(1), ALU.mult))
                    v.tensor_tensor(wb, sn, slot(1), ALU.mult).then_inc(s["bu_read"], 1)
                    dve.wait_ge(s["bu_ready"], 8 * ch + 2 * t + 2)
                    step(v.tensor_tensor(wd, sn, slot(2), ALU.mult))
                    v.tensor_tensor(we, cs, slot(2), ALU.mult).then_inc(s["bu_read"], 1)
                    dve.wait_ge(s["bu_read"], AHEAD + 8 * ch + 2 * t + 2)
                    step(v.tensor_tensor(wa, wa, wd, ALU.add))
                    step(v.tensor_tensor(we, we, wb, ALU.subtract))
                    decay = cmag[:, t:t + 1].to_broadcast([P, T])
                    step(v.tensor_tensor_scan(wd, decay, wa, 0.0, ALU.mult, ALU.add))
                    step(v.tensor_tensor_scan(wb, decay, we, 0.0, ALU.mult, ALU.add))
                    step(v.tensor_tensor(wa, cs, wd, ALU.mult))
                    step(v.tensor_tensor(we, sn, wb, ALU.mult))
                    if t:
                        dve.wait_ge(s["y_done"], AHEAD + 4 * ch + t)
                    else:
                        dve.wait_ge(s["y_done"], AHEAD + 4 * ch)
                    step(v.tensor_tensor(xre, wa, we, ALU.subtract))
                    step(v.tensor_tensor(wa, sn, wd, ALU.mult))
                    step(v.tensor_tensor(we, cs, wb, ALU.mult))
                    v.tensor_tensor(xim, wa, we, ALU.add).then_inc(s["x_ready"], 1)
                    dve.wait_ge(s["x_ready"], 4 * ch + t + 1)
                dve.wait_ge(s["y_done"], AHEAD + 4 * ch + 4)
                one = us[:, bass.ds(ch, 1), :].rearrange("p a n -> p (a n)")
                dst = yg[:, bass.ds(ch, 1), :].rearrange("p a n -> p (a n)")
                v.scalar_tensor_tensor(dst, one, cols_a[:, bass.ds(ch + at_a["d_skip"], 1)], slot(3), ALU.mult, ALU.add)\
                 .then_inc(s["y_read"], 1)

            dve.wait_ge(s["qkv_read"], AHEAD + 12)

            def head_bias(p, e, keys=slice(0, T)):
                step(v.scalar_tensor_tensor(bias[:, e % 2, keys], delta[:, keys], slopes[:, bass.ds(2 * p + e, 1)],
                                            log8[:, keys], ALU.mult, ALU.add))

            def smallest(p, t):
                e, qb = tiles[t % NT]
                n = (qb + 1) * P
                dve.wait_ge(s["s_ready"], NT * p + t + 1)
                if t >= 3:
                    if t % 2:
                        dve.wait_ge(s["pt0"], AHEAD + NT * p + t - 3)
                    else:
                        dve.wait_ge(s["pt1"], QB * p + (t - 4) // 2 + 1)
                dve.sem_inc(s["passed"], 1)
                v.tensor_tensor_reduce(out=prob[:, t % 4, 0:n], in0=slot(t % 2)[:, 0:n],
                                       in1=bias[:, e, T - n:T], scale=-0.125, scalar=3e38,
                                       op0=ALU.add, op1=ALU.min,
                                       accum_out=neg_max[:, t % 4:t % 4 + 1]).then_inc(s["sm_ready"], 1)

            def near_half(p, t):
                dve.wait_ge(s["pt0"], AHEAD + NT * p + t + 1)
                if t:
                    dve.wait_ge(s["pv"], AHEAD + NT * p + t - 1)
                v.tensor_copy(prob_t[:, t % 2, 0:HALF], slot(2)[:, 0:HALF]).then_inc(s["ptc0"], 1)

            def normalised(p, t):
                e, qb = tiles[t]
                dve.wait_ge(s["pv"], AHEAD + NT * p + t + 1)
                step(v.reciprocal(rden[:, t % 4:t % 4 + 1], den[:, t % 4:t % 4 + 1]))
                src = slot(3)[:, HALF * (t % 2):HALF * (t % 2) + HALF]
                if t % 4 == 3:
                    lo = 2 * N_ADA_EARLY + 2 * (t // 4)
                    dve.wait_ge(s["ada_done"], 4 * p + N_ADA_EARLY + t // 4 + 1)
                    v.tensor_tensor(mod[:, bass.ds(8 * p + lo, 2)], src[:, HD:HD + 2],
                                    cols_a[:, bass.ds(8 * p + lo + at_a["b_ada"], 2)], ALU.add)\
                     .then_inc(s["mod2_ready"], 1)
                v.tensor_scalar(o_tok[:, qb, bass.ds(P * p + HD * e, HD)], src[:, 0:HD],
                                rden[:, t % 4:t % 4 + 1], None, ALU.mult).then_inc(s["o_ready"], 1)

            def heads(p, last):
                for t in range(NT):
                    if t % 2 and (t + 1 < NT or not last):
                        near_half(p, t + 1)
                    if t + 3 < NT or not last:
                        smallest(p, t + 3)
                    k = t // 4
                    if t % 4 == 0:
                        dve.wait_ge(ada_in[k % 2], 32 * p + 16 * (k // 2 + 1))
                        dve.wait_ge(s["ada_done"], 4 * p + N_ADA_EARLY + max(k - 1, 0))
                    ada_sums(ada_part[:, k % 2], lambda c, k=k: raw[:, k % 2, c, :], ((0, 1, 2), (3, 4, 5), (6, 7), ())[t % 4])
                    normalised(p, t)
                    half = slice(HALF * (t % 2), HALF * (t % 2) + HALF)
                    if t < 2:
                        dve.wait_ge(s["sm_ready"], AHEAD + NT * p + 3)
                        head_bias(p, 1, half)
                    if t in (QB, QB + 1) and not last:
                        dve.wait_ge(s["sm_ready"], AHEAD + NT * p + QB)
                        head_bias(p, 2, half)

            dve.wait_ge(s["k0_ready"], 2)
            for half in range(2):
                v.tensor_tensor(k_ll[HD * half:HD * half + HD, 0, :], qk[0:HD, KA, :], k_hh[0:HD, 0, :].bitcast(F32),
                                ALU.subtract).then_inc(s["k0_ready"], 1)
            dve.wait_ge(s["attn_in"], 32)
            dve.wait_ge(s["consts_ready"], 2 + HEADS)
            head_bias(0, 0)
            for o in range(2):
                dve.wait_ge(s["sig_ready"], 2)
                v.tensor_tensor(yg[:, o, :], yg[:, o, :], gate_st[:, o, :], ALU.mult).then_inc(s["y_gated"], 1)
            for t in range(3):
                smallest(0, t)
            near_half(0, 0)
            with step.loop(HEADS // 2 - 1, 4 + NT + 4 * (KD - 1)) as p:
                heads(p, False)
            heads(HEADS // 2 - 1, True)
            dve.wait_ge(s["mod2_ready"], 16)
            v.scalar_tensor_tensor(gain[:, 1], mod[:, 4 * KD:5 * KD], 1.0, col_a("g_ffn", 0, KD), ALU.add, ALU.mult)\
             .then_inc(s["mod_ready"], 1)

            for o in range(2):
                dve.wait_ge(s["ysh"], o + 1)
                v.tensor_tensor(ys_l[:, o, :], yg[:, o, :], ys_h[:, o, :].bitcast(F32), ALU.subtract).then_inc(s["ys_ready"], 1)
            for c in range(KA):
                dve.wait_ge(s["oh_ready"], c + 1)
                v.tensor_tensor(in2_l[:, c, :], slot(c), in2_h[:, c, :].bitcast(F32), ALU.subtract).then_inc(s["ot_ready"], 1)

            dve.wait_ge(s["ys_ready"], 2)
            with step.loop(2, 4) as i:
                for b in range(2):
                    for cg in range(2):
                        c = 2 * b + cg
                        dve.wait_ge(gate_back[cg], 64 * i + 32 * (b + 1))
                        dve.wait_ge(s["gemm"], 8 * i + units_before(N_PROJ) + 4 * b + 2 * cg + 2)
                        step(v.tensor_tensor(mix[:, 0, :], slot(2 * cg), gate_in[:, cg, 0, :], ALU.mult))
                        v.tensor_tensor(mix[:, 1, :], slot(2 * cg + 1), gate_in[:, cg, 1, :], ALU.mult)\
                         .then_inc(s["proj_read"], 1)
                        dve.wait_ge(s["proj_read"], AHEAD + 4 * i + c + 1)
                        v.tensor_tensor(mix[:, 0, :], mix[:, 0, :], mix[:, 1, :], ALU.add).then_inc(s["mix_ready"], 1)
                        dve.wait_ge(s["mh_ready"], 4 * i + c + 1)
                        v.tensor_tensor(act_l[:, bass.ds(4 * i + c, 1), :].rearrange("p a n -> p (a n)"), mix[:, 0, :],
                                        act_h[:, bass.ds(4 * i + c, 1), :].rearrange("p a n -> p (a n)").bitcast(F32),
                                        ALU.subtract).then_inc(s["merged_ready"], 1)
                        dve.wait_ge(s["merged_ready"], 4 * i + c + 1)

            for c in range(KD):
                dve.wait_ge(h_back[c // 4], 16)
                dve.wait_ge(s["gemm"], units_before(N_OUT) + c + 1)
                v.scalar_tensor_tensor(h_t[:, c, :], slot(c % 4), mod[:, 2 * KD + c:2 * KD + c + 1], h_t[:, c, :],
                                       ALU.mult, ALU.add).then_inc(s["out_read"], 1)
                if c >= 2:
                    add_square(1, c - 1)
            add_square(1, KD - 1)
            one_over_root(2)
            on_diagonal(0, stat[:, 1, :])
            dve.wait_ge(s["rstd_ready"], 2)
            dve.wait_ge(s["out_read"], AHEAD + KD)
            norm(1, gain[:, 1], lambda c: mod[:, 3 * KD + c:3 * KD + c + 1], slot(3))

            base_f = units_before(N_FFN)
            def quarter(q, last):
                for p in range(2):
                    for cg in range(2):
                        c = 2 * p + cg
                        dve.wait_ge(s["acc_ready"], 4 * q + c + 1)
                        for j in range(1, CONV):
                            ins = v.scalar_tensor_tensor(
                                conv[:, cg, j:T], slot(cg)[:, 0:T - j],
                                cols_b[:, bass.ds(4 * q + (at_b["w_conv"] + j * (FF // P) + c), 1)],
                                conv[:, cg, j:T], ALU.mult, ALU.add)
                            if j < CONV - 1:
                                step(ins)
                            else:
                                ins.then_inc(s["a_read"], 1)
                    for cg in range(2):
                        c = 2 * p + cg
                        dve.wait_ge(s["silu_ready"], 4 * q + c + 1)
                        dve.wait_ge(s["gemm"], 16 * q + base_f + 4 * p + 2 + cg + 1)
                        if c:
                            dve.wait_ge(s["f_ready"], AHEAD + 4 * q + c)
                        else:
                            dve.wait_ge(s["f_ready"], AHEAD + 4 * q)
                        v.tensor_tensor(ffn[:], slot(2 + cg), conv[:, cg, :], ALU.mult).then_inc(s["v_read"], 1)
                        dve.wait_ge(s["fh_ready"], 4 * q + c + 1)
                        v.tensor_tensor(in2_l[:, c, :], ffn[:], in2_h[:, c, :].bitcast(F32), ALU.subtract)\
                         .then_inc(s["f_ready"], 1)
                for u in range(KD):
                    dve.wait_ge(s["gemm"], 16 * q + base_f + 8 + u + 1)
                    if u == 0:
                        dve.wait_ge(s["down_read"], AHEAD + 8 * q)
                    v.scalar_tensor_tensor(h_t[:, u, :], slot(u % 4), mod[:, 5 * KD + u:5 * KD + u + 1], h_t[:, u, :],
                                           ALU.mult, ALU.add).then_inc(s["down_read"], 1)
                    if last and u >= 2:
                        add_squares(u - 1)

            def add_squares(c):
                for m in range(2):
                    dve.wait_ge(s["sq_ready"], 2 * KD + 2 * c + m + 1)
                    if c >= 2:
                        dve.wait_ge(s["sq_used"], 2 * (KD - 1) + 2 * (c - 2) + m + 1)
                    v.tensor_tensor(acc2[:, m, :], acc2[:, m, :], sq[:, m, :], ALU.add).then_inc(s["sq_used"], 1)

            with step.loop(3, 4) as q:
                quarter(q, False)
            quarter(3, True)
            add_squares(KD - 1)

            step(v.tensor_tensor(gain2[:], col_b("g_final", 0, KD), col_b("norm_g_2", 0, KD), ALU.mult))
            one_over_root(3)
            r1 = stat[:, 1, :]
            step(v.tensor_tensor(stat[:, 2, :], r1, r1, ALU.mult))
            dve.wait_ge(s["sums_ready"], 4)
            v.tensor_tensor(stat[:, 2, :], stat[:, 2, :], slot(2)[:, 0:QB], ALU.mult).then_inc(s["ms2_ready"], 1)
            dve.wait_ge(s["sq_used"], 4 * (KD - 1))
            on_diagonal(1, r1)
            dve.wait_ge(s["std_ready"], 4)
            step(v.reciprocal(stat[:, 4, :], stat[:, 3, :]))
            step(v.tensor_tensor(stat[:, 5, :], stat[:, 4, :], r1, ALU.mult))
            on_diagonal(0, stat[:, 5, :])
            dve.wait_ge(s["rstd2_ready"], 1)
            dve.wait_ge(s["down_read"], AHEAD + 32)
            norm(2, gain2, None, rstd2[:, 0, :])
            dve.wait_ge(s["rstd2_ready"], 2)
            for c in range(KD):
                v.scalar_tensor_tensor(h_t[:, c, :], h_t[:, c, :], col_b("g_final", c), rstd2[:, 1, :], ALU.mult, ALU.mult)\
                 .then_inc(s["x2_ready"], 1)

            dve.wait_ge(s["v2_read"], 4)
            for t in range(QB):
                step(v.bn_stats(bn[:, t, :], vg[:, t, :]))
                step(v.bn_aggr(bn_mv[:, t, :], bn[:, t, :]))
            v.tensor_scalar(ln_rstd[:], bn_mv[:, :, 1], LN_EPS, None, ALU.add).then_inc(s["ln_var"], 1)
            dve.wait_ge(s["ln_std"], 1)
            step(v.reciprocal(ln_rstd[:], ln_rstd[:]))
            dve.wait_ge(s["late_in"], 16 * 13)
            for t in range(QB):
                step(v.tensor_scalar(vg[:, t, :], vg[:, t, :], bn_mv[:, t, 0:1], ln_rstd[:, t:t + 1],
                                     ALU.subtract, ALU.mult))
                step(v.tensor_tensor(vg[:, t, :], vg[:, t, :], ln_g[:], ALU.mult))
                ins = v.tensor_tensor(vg[:, t, :], vg[:, t, :], ln_b[:], ALU.add)
                if t < QB - 1:
                    step(ins)
                else:
                    ins.then_inc(s["vn_ready"], 1)
            dve.wait_ge(s["wst_done"], 1)
            v.tensor_copy(wst[:].rearrange("p g t -> p (g t)"), slot(2)).then_inc(s["wst_ready"], 1)

            for c in range(K2):
                cg = c % 2
                dve.wait_ge(s["sg_done"], c + 1)
                if c:
                    dve.wait_ge(s["a_ready"], c)
                v.tensor_tensor(a_s[:].rearrange("p (n t) -> p n t", t=P), slot(2 + cg).rearrange("p (n t) -> p n t", t=P),
                                bs_row[:, c:c + 1, :].to_broadcast([P, QB, P]), ALU.add).then_inc(s["sg_read"], 1)
                dve.wait_ge(s["sg_read"], c + 1)
                dve.wait_ge(s["au_read"], c + 1)
                step(v.tensor_tensor(a_s[:], a_s[:], a_u[:, cg, :], ALU.mult))
                dve.wait_ge(s["az_read"], c + 1)
                v.tensor_tensor(a_s[:], a_s[:], a_z[:, cg, :], ALU.mult).then_inc(s["ap_ready"], 1)
                dve.wait_ge(s["ah_ready"], c + 1)
                v.tensor_tensor(in2_l[:, c, :], a_s[:], in2_h[:, c, :].bitcast(F32), ALU.subtract).then_inc(s["a_ready"], 1)

            def gated(n0, sig, p_read, done, add, trips=4):
                with step.loop(trips, 0) as j:
                    for cg in range(2):
                        m = merged[:, bass.ds(2 * j + cg, 1), :].rearrange("p a n -> p (a n)")
                        dve.wait_ge(sig, AHEAD + 2 * j + cg + 1)
                        dve.wait_ge(s["gemm"], 4 * j + units_before(n0 + 1) + cg + 1)
                        if not add:
                            v.tensor_tensor(m, br[:, cg, :], slot(2 + cg), ALU.mult).then_inc(p_read, 1)
                            continue
                        v.tensor_tensor(br[:, cg, :], br[:, cg, :], slot(2 + cg), ALU.mult).then_inc(p_read, 1)
                        dve.wait_ge(p_read, AHEAD + 2 * j + cg + 1)
                        v.tensor_tensor(m, m, br[:, cg, :], ALU.add).then_inc(done, 1)

            for half in range(2):
                dve.wait_ge(x2_out[half], 16)
            dve.wait_ge(s["a_ready"], K2)
            gated(N_GA, s["sa_ready"], s["pa_read"], None, False)

            base_b = units_before(N_B)
            for p in range(2):
                for cg in range(2):
                    dve.wait_ge(s["xb_read"], 2 * p + cg + 1)
                    dve.wait_ge(s["gemm"], base_b + 8 * p + 2 + cg + 1)
                    v.tensor_tensor(br[:, cg, :], br[:, cg, :], slot(2 + cg), ALU.mult).then_inc(s["bc_read"], 1)
                for cg in range(2):
                    c = 2 * p + cg
                    y, taps = br[:, cg, :], br2

                    def tap(j, c=c):
                        return col_b("conv_w_2", j * K2 + c)

                    dve.wait_ge(s["bc_read"], c + 1)
                    if c:
                        dve.wait_ge(s["b_ready"], c)
                    step(v.tensor_scalar(taps[:], y, tap(2), col_a("conv_b_2", c), ALU.mult, ALU.add))
                    step(v.scalar_tensor_tensor(taps[:, 1:T], y[:, 0:T - 1], tap(1), taps[:, 1:T], ALU.mult, ALU.add))
                    step(v.scalar_tensor_tensor(taps[:, 2:T], y[:, 0:T - 2], tap(0), taps[:, 2:T], ALU.mult, ALU.add))
                    dve.wait_ge(s["gemm"], base_b + 8 * p + 4 + cg + 1)
                    v.tensor_tensor(y, taps[:], slot(cg), ALU.mult).then_inc(s["bg_read"], 1)
                    dve.wait_ge(s["bg_read"], c + 1)
                    dve.wait_ge(s["bz_read"], c + 1)
                    v.tensor_tensor(y, y, taps[:], ALU.mult).then_inc(s["bp_ready"], 1)
                    dve.wait_ge(s["bh_ready"], c + 1)
                    v.tensor_tensor(in2_l[:, c, :], y, in2_h[:, c, :].bitcast(F32), ALU.subtract).then_inc(s["b_ready"], 1)
            dve.wait_ge(s["pa_read"], AHEAD + KD)
            dve.wait_ge(s["b_ready"], K2)
            gated(N_GB, s["sb_ready"], s["pb_read"], s["mb_ready"], True)

            for p in range(2):
                for cg in range(2):
                    c = 2 * p + cg
                    x, other = br[:, 0, :], br2
                    dve.wait_ge(s["xc_read"], c + 1)
                    if c >= 2:
                        dve.wait_ge(s["pool_done"], 2)
                    src, dst = x, other[:]
                    for j in range(c + 1):
                        h = 2**j
                        step(v.tensor_copy(dst[:, 0:h], src[:, 0:h]))
                        step(v.tensor_tensor(dst[:, h:T], src[:, h:T], src[:, 0:T - h], ALU.add))
                        src, dst = dst, src
                    res = pool_in[cg]
                    step(v.scalar_tensor_tensor(res[:, 16:T], src[:, 16:T], 1.0 / WINDOWS[c], slot(cg)[:, 16:T],
                                                ALU.mult, ALU.subtract))
                    step(v.tensor_tensor(src[:, 0:16], src[:, 0:16], inv[:, c, :], ALU.mult))
                    v.tensor_tensor(res[:, 0:16], src[:, 0:16], slot(cg)[:, 0:16], ALU.subtract).then_inc(s["pooled"], 1)
                    dve.wait_ge(s["pooled"], c + 1)
                for cg in range(2):
                    c = 2 * p + cg
                    z = br[:, cg, :]
                    dve.wait_ge(s["pool_done"], c + 1)
                    dve.wait_ge(s["cz_read"], c + 1)
                    v.scalar_tensor_tensor(z, slot(cg), col_b("pool_scale_2", c), z, ALU.mult, ALU.mult)\
                     .then_inc(s["cp_ready"], 1)
                    dve.wait_ge(s["ch_ready"], c + 1)
                    v.tensor_tensor(in2_l[:, c, :], z, in2_h[:, c, :].bitcast(F32), ALU.subtract).then_inc(s["ch_done"], 1)
            dve.wait_ge(s["mb_ready"], AHEAD + KD)
            dve.wait_ge(s["ch_done"], K2)
            gated(N_GC, s["sc_ready"], s["pc_read"], s["mc_ready"], True, 3)

            def merged_low(c):
                dve.wait_ge(s["m2_high"], c + 1)
                v.tensor_tensor(act_l[:, c, :], merged[:, c, :], act_h[:, c, :].bitcast(F32), ALU.subtract)\
                 .then_inc(s["m2_ready"], 1)

            for c in range(KD - 2):
                merged_low(c)
            for c in (KD - 2, KD - 1):
                cg = c % 2
                dve.wait_ge(s["sc_ready"], AHEAD + c + 1)
                dve.wait_ge(s["gemm"], units_before(N_WO) - 1 + cg)
                v.tensor_tensor(br[:, cg, :], br[:, cg, :], slot(2 + cg), ALU.mult).then_inc(s["pc_read"], 1)
                dve.wait_ge(s["pc_read"], AHEAD + c + 1)
                v.tensor_tensor(merged[:, c, :], merged[:, c, :], br[:, cg, :], ALU.add).then_inc(s["mc_ready"], 1)
            for c in (KD - 2, KD - 1):
                merged_low(c)
            for c in range(KD):
                dve.wait_ge(x2_back[c // 4], 16)
                dve.wait_ge(s["gemm"], units_before(N_WO) + c + 1)
                v.tensor_tensor(y_t[:, c, :], y_t[:, c, :], slot(c % 4), ALU.add).then_inc(s["y_ready"], 1)
            dve.wait_ge(s["g_row_in"], 16)
            for t in range(QB):
                dve.wait_ge(s["ostd"], t + 1)
                step(v.reciprocal(o_ssq[:, 2, t:t + 1], o_ssq[:, 1, t:t + 1]))
                if t >= 2:
                    dve.wait_ge(row_out[t % 2], 16 * (t // 2))
                v.scalar_tensor_tensor(o_row[:, t % 2, :], slot(t % 4), o_ssq[:, 2, t:t + 1], g_row[:],
                                       ALU.mult, ALU.mult).then_inc(s["orow"], 1)


def kernel(**inputs):
    import concourse.bacc as bacc
    from concourse.bass_utils import run_bass_kernel_spmd

    nc = bacc.Bacc("TRN2", target_bir_lowering=False, num_devices=1)
    arrays, aps = {}, {}
    for name, value in {**inputs, **constants()}.items():
        value = np.ascontiguousarray(value)
        arrays[f"in_{name}"] = value
        aps[name] = nc.dram_tensor(f"in_{name}", value.shape, mybir.dt.from_np(value.dtype), kind="ExternalInput").ap()
    out = nc.dram_tensor("out", (1, T, D), F32, kind="ExternalOutput").ap()
    build(nc, aps, out)
    return run_bass_kernel_spmd(nc, [arrays], core_ids=[0]).results[0]["out"]
```
